# Optimizing a Trainium2 kernel written in Bass

```python
import math
import jax, jax.numpy as jnp
from jax import lax
import numpy as np

D_MODEL = 1024
BATCH = 1
SEQ = 2048
DEPTH = 1

CHUNK = 64

SSD_EXPAND = 2
SSD_INNER = SSD_EXPAND * D_MODEL
SSD_HEADDIM = 64
SSD_HEADS = SSD_INNER // SSD_HEADDIM
SSD_GROUPS = 4
SSD_STATE = 128
SSD_CONV = 4
SSD_CONV_DIM = SSD_INNER + 2 * SSD_GROUPS * SSD_STATE
DT_MIN = 0.001
DT_MAX = 0.1

SC_WIDTH = D_MODEL
SC_CONV = 3

N_BRANCHES = 2

_S0 = SSD_INNER
_S1 = _S0 + SSD_CONV_DIM
_S2 = _S1 + SSD_HEADS
_S3 = _S2 + SC_WIDTH
_S4 = _S3 + SC_WIDTH
_S5 = _S4 + SC_WIDTH
IN_DIM = _S5 + N_BRANCHES * D_MODEL
IN_SPLITS = (_S0, _S1, _S2, _S3, _S4, _S5)

N_EXPERTS = 32
TOP_K = 4
EXPERT_FF = D_MODEL
SWIGLU_LIMIT = 7.0
SWIGLU_ALPHA = 1.702

DN_ALPHA = (2.0 * DEPTH) ** 0.25
DN_BETA = (8.0 * DEPTH) ** -0.25

LN_EPS = 1e-5
RMS_EPS = 1e-5
N_ADA = 6

kernel_name = 'hybrid_ssd_shortconv_moe_deepnorm'

def layer_norm(x, g=None, b=None):
    xf = x.astype(jnp.float32)
    mu = jnp.mean(xf, axis=-1, keepdims=True)
    var = jnp.mean(jnp.square(xf - mu), axis=-1, keepdims=True)
    y = ((xf - mu) * lax.rsqrt(var + LN_EPS)).astype(x.dtype)
    if g is not None:
        y = y * g + b
    return y

def rms_norm(x, g):
    xf = x.astype(jnp.float32)
    y = xf * lax.rsqrt(jnp.mean(jnp.square(xf), axis=-1, keepdims=True) + RMS_EPS)
    return y.astype(x.dtype) * g

def causal_dwconv(u, w):
    k, ch = w.shape
    return lax.conv_general_dilated(
        u, w[:, None, :], window_strides=(1,), padding=[(k - 1, 0)],
        dimension_numbers=('NWC', 'WIO', 'NWC'), feature_group_count=ch)

def ssd_chunked(x, dt, a, bm, cm):
    b, s, h, p = x.shape
    g, n = bm.shape[-2:]
    k = h // g
    nc = s // CHUNK
    dtype = x.dtype
    xd = (x * dt[..., None]).reshape(b, nc, CHUNK, g, k, p)
    la = (dt * a).astype(jnp.float32).reshape(b, nc, CHUNK, g, k)
    la = jnp.moveaxis(la, 2, -1)
    a_cum = jnp.cumsum(la, axis=-1)
    bc = bm.reshape(b, nc, CHUNK, g, n)
    cc = cm.reshape(b, nc, CHUNK, g, n)
    causal = jnp.tril(jnp.ones((CHUNK, CHUNK), dtype=bool))
    seg = a_cum[..., :, None] - a_cum[..., None, :]
    l_dec = jnp.exp(jnp.where(causal, seg, -jnp.inf)).astype(dtype)
    cb = jnp.einsum('bclgn,bcsgn->bcgls', cc, bc)
    y_diag = jnp.einsum('bcgls,bcgkls,bcsgkp->bclgkp', cb, l_dec, xd)
    decay_states = jnp.exp(a_cum[..., -1:] - a_cum).astype(dtype)
    states = jnp.einsum('bcsgn,bcgks,bcsgkp->bcgkpn', bc, decay_states, xd)
    chunk_decay = jnp.exp(a_cum[..., -1]).astype(dtype)

    def step(carry, inp):
        st, dec = inp
        return carry * dec[..., None, None] + st, carry

    init = jnp.zeros((b, g, k, p, n), dtype=states.dtype)
    _, prev = lax.scan(step, init, (jnp.moveaxis(states, 1, 0), jnp.moveaxis(chunk_decay, 1, 0)))
    prev = jnp.moveaxis(prev, 0, 1)
    y_off = jnp.einsum('bclgn,bcgkpn,bcgkl->bclgkp', cc, prev, jnp.exp(a_cum).astype(dtype))
    return (y_diag + y_off).reshape(b, s, h, p)

def hybrid_mixer(h, w_in, conv_ssd_w, conv_ssd_b, dt_bias, a_log, d_skip, ssd_norm_w,
                 w_ssd_out, conv_short_w, w_short_out, b_gate, w_o):
    b, s, _ = h.shape
    u = h @ w_in
    z, xbc, dt_raw, sc_b, sc_c, sc_x, gate_logits = jnp.split(u, IN_SPLITS, axis=-1)
    xbc = jax.nn.silu(causal_dwconv(xbc, conv_ssd_w) + conv_ssd_b)
    xs, bm, cm = jnp.split(xbc, (SSD_INNER, SSD_INNER + SSD_GROUPS * SSD_STATE), axis=-1)
    xs = xs.reshape(b, s, SSD_HEADS, SSD_HEADDIM)
    bm = bm.reshape(b, s, SSD_GROUPS, SSD_STATE)
    cm = cm.reshape(b, s, SSD_GROUPS, SSD_STATE)
    dt = jax.nn.softplus(dt_raw + dt_bias)
    a = -jnp.exp(a_log)
    y = ssd_chunked(xs, dt, a, bm, cm) + xs * d_skip[:, None]
    y = rms_norm(y.reshape(b, s, SSD_INNER) * jax.nn.silu(z), ssd_norm_w)
    u_a = y @ w_ssd_out
    v = causal_dwconv(sc_c * sc_x, conv_short_w)
    u_b = (sc_b * v) @ w_short_out
    g_a, g_b = jnp.split(jax.nn.sigmoid(gate_logits + b_gate), N_BRANCHES, axis=-1)
    return (g_a * u_a + g_b * u_b) @ w_o

def moe_ffn(h, w_router, b_router, w_gu, b_gu, w_down, b_down):
    b, s, d = h.shape
    t = h.reshape(b * s, d)
    logits = (t @ w_router + b_router).astype(jnp.float32)
    top_vals, top_idx = lax.top_k(logits, TOP_K)
    probs = jax.nn.softmax(top_vals, axis=-1).astype(h.dtype)
    flat_e = top_idx.reshape(-1)
    order = jnp.argsort(flat_e)
    e_sorted = flat_e[order]
    tok_sorted = order // TOP_K
    group_sizes = jnp.bincount(flat_e, length=N_EXPERTS).astype(jnp.int32)
    xs = t[tok_sorted]
    gu = lax.ragged_dot(xs, w_gu, group_sizes) + b_gu[e_sorted]
    gate, up = jnp.split(gu, 2, axis=-1)
    gate = jnp.minimum(gate, SWIGLU_LIMIT)
    up = jnp.clip(up, -SWIGLU_LIMIT, SWIGLU_LIMIT)
    act = (up + 1.0) * gate * jax.nn.sigmoid(SWIGLU_ALPHA * gate)
    out = lax.ragged_dot(act, w_down, group_sizes) + b_down[e_sorted]
    slots = jnp.zeros_like(out).at[order].set(out).reshape(b * s, TOP_K, d)
    return jnp.einsum('tkd,tk->td', slots, probs).reshape(b, s, d)

def modulate(x, shift, scale):
    return layer_norm(x) * (1.0 + scale) + shift

def setup_inputs(seed: int = 0) -> dict:
    key = jax.random.key(seed)
    ks = jax.random.split(key, 26)
    L, D = DEPTH, D_MODEL

    def nrm(k, shape, scale):
        return jax.random.normal(k, shape, jnp.float32) * scale

    dt0 = jnp.exp(jax.random.uniform(ks[7], (L, SSD_HEADS), jnp.float32,
                                     minval=math.log(DT_MIN), maxval=math.log(DT_MAX)))
    return {
        'x': nrm(ks[0], (BATCH, SEQ, D), 1.0),
        'c': nrm(ks[1], (BATCH, D), 1.0),
        'w_ada': nrm(ks[2], (L, D, N_ADA * D), D ** -0.5),
        'b_ada': nrm(ks[3], (L, N_ADA * D), 0.02),
        'w_in': nrm(ks[4], (L, D, IN_DIM), D ** -0.5),
        'conv_ssd_w': nrm(ks[5], (L, SSD_CONV, SSD_CONV_DIM), SSD_CONV ** -0.5),
        'conv_ssd_b': nrm(ks[6], (L, SSD_CONV_DIM), 0.02),
        'dt_bias': dt0 + jnp.log(-jnp.expm1(-dt0)),
        'a_log': jnp.log(jax.random.uniform(ks[8], (L, SSD_HEADS), jnp.float32, minval=1.0, maxval=16.0)),
        'd_skip': 1.0 + nrm(ks[9], (L, SSD_HEADS), 0.02),
        'ssd_norm_w': 1.0 + nrm(ks[10], (L, SSD_INNER), 0.02),
        'w_ssd_out': nrm(ks[11], (L, SSD_INNER, D), DN_BETA * SSD_INNER ** -0.5),
        'conv_short_w': nrm(ks[12], (L, SC_CONV, SC_WIDTH), SC_CONV ** -0.5),
        'w_short_out': nrm(ks[13], (L, SC_WIDTH, D), DN_BETA * SC_WIDTH ** -0.5),
        'b_gate': nrm(ks[14], (L, N_BRANCHES * D), 0.02),
        'w_o': nrm(ks[15], (L, D, D), DN_BETA * D ** -0.5),
        'ln1_g': 1.0 + nrm(ks[16], (L, D), 0.02),
        'ln1_b': nrm(ks[17], (L, D), 0.02),
        'w_router': nrm(ks[18], (L, D, N_EXPERTS), D ** -0.5),
        'b_router': nrm(ks[19], (L, N_EXPERTS), 0.01),
        'w_gu': nrm(ks[20], (L, N_EXPERTS, D, 2 * EXPERT_FF), D ** -0.5),
        'b_gu': nrm(ks[21], (L, N_EXPERTS, 2 * EXPERT_FF), 0.02),
        'w_down': nrm(ks[22], (L, N_EXPERTS, EXPERT_FF, D), DN_BETA * EXPERT_FF ** -0.5),
        'b_down': nrm(ks[23], (L, N_EXPERTS, D), 0.02),
        'ln2_g': 1.0 + nrm(ks[24], (L, D), 0.02),
        'ln2_b': nrm(ks[25], (L, D), 0.02),
    }

def reference(x, c, w_ada, b_ada, w_in, conv_ssd_w, conv_ssd_b, dt_bias, a_log, d_skip,
              ssd_norm_w, w_ssd_out, conv_short_w, w_short_out, b_gate, w_o, ln1_g, ln1_b,
              w_router, b_router, w_gu, b_gu, w_down, b_down, ln2_g, ln2_b):
    for l in range(DEPTH):
        mod = jax.nn.silu(c) @ w_ada[l] + b_ada[l]
        sh1, sc1, g1, sh2, sc2, g2 = jnp.split(mod[:, None, :], N_ADA, axis=-1)
        h = modulate(x, sh1, sc1)
        mix = hybrid_mixer(h, w_in[l], conv_ssd_w[l], conv_ssd_b[l], dt_bias[l], a_log[l],
                           d_skip[l], ssd_norm_w[l], w_ssd_out[l], conv_short_w[l],
                           w_short_out[l], b_gate[l], w_o[l])
        x = layer_norm(DN_ALPHA * x + g1 * mix, ln1_g[l], ln1_b[l])
        h = modulate(x, sh2, sc2)
        ffn = moe_ffn(h, w_router[l], b_router[l], w_gu[l], b_gu[l], w_down[l], b_down[l])
        x = layer_norm(DN_ALPHA * x + g2 * ffn, ln2_g[l], ln2_b[l])
    return x


_drawn_inputs = setup_inputs


def setup_inputs(seed=0):
    import zlib

    import numpy as np

    out = dict(_drawn_inputs(seed))
    spreads = {}
    factors = {'conv_ssd_b': 8.0,
     'd_skip': 25.625,
     'ssd_norm_w': 24.592,
     'b_gate': 8.0,
     'b_router': 4.356,
     'b_gu': 8.0,
     'b_down': 8.0,
     'ln2_g': 8.285,
     'ln2_b': 8.033}
    for name, (base, spread) in spreads.items():
        noise = np.random.default_rng([zlib.crc32(name.encode()), seed]).standard_normal(out[name].shape)
        drawn = base * np.exp(spread * noise) if base else spread * noise
        out[name] = __import__('jax').numpy.asarray(drawn.astype(out[name].dtype))
    for name, factor in factors.items():
        out[name] = (out[name] * factor).astype(out[name].dtype)
    return out
```

```python
from contextlib import ExitStack

import concourse.bass as bass
from concourse import mybir

F32 = mybir.dt.float32
F32R = mybir.dt.float32r
I32 = mybir.dt.int32
U32 = mybir.dt.uint32
ALU = mybir.AluOpType
ACT = mybir.ActivationFunctionType
AX = mybir.AxisListType

P = 128
D = 1024
SEQ = 2048
KD = D // P
TT = SEQ // P
INNER = 2 * D
HEADS = 32
HD = 64
GROUPS = 4
HG = HEADS // GROUPS
NSTATE = 128
CONV = 4
SCONV = 3
EXPERTS = 32
TOPK = 4
FF = D
LIMIT = 7.0
SWIGLU_ALPHA = 1.702
DN_ALPHA = 2.0 ** 0.25
EPS = 1e-5
BANK = 512

N_Z = INNER // P
N_XBC = (INNER + 2 * GROUPS * NSTATE) // P
N_SC = D // P
N_GATE = 2 * D // P
N_PROJ = N_Z + N_XBC + 3 * N_SC + N_GATE
ROW_Z = 0
ROW_XBC = N_Z
ROW_Q = ROW_XBC + N_XBC
ROW_GATE = ROW_Q + N_SC
N_ROWS = ROW_GATE + N_GATE

MOE_TILES = SEQ * TOPK // P + EXPERTS
SLOTS = MOE_TILES * P
SKIP = float(1 << 20)
SH1, SC1, SH2, SC2 = 0, KD, 3 * KD, 4 * KD


class Shared:
    pass


def wait(eng, sem, value):
    if isinstance(value, int) and value <= 0:
        return
    eng.wait_ge(sem, value)


def apart(eng, S):
    eng.sem_inc(S.passed, 1)


def pipeline(eng, n, unroll, stages):
    most = max(lag for lag, _ in stages)
    rounds = -(-(n + most) // unroll)
    lead = -(-most // unroll) + 1
    full = n // unroll

    def one(r):
        for s in range(unroll):
            for lag, fn in stages:
                q, slot = (s - lag) // unroll, (s - lag) % unroll
                if isinstance(r, int) and not 0 <= (r + q) * unroll + slot < n:
                    continue
                fn(r + q, slot)

    if full - lead < 2:
        for r in range(rounds):
            one(r)
        return
    for r in range(lead):
        one(r)
    with eng.Fori(lead, full) as r:
        one(r)
    for r in range(full, rounds):
        one(r)


class Chain:

    def __init__(self, eng, sem):
        self.eng, self.sem, self.n, self.k = eng, sem, 0, 0

    def item(self, i, per_item):
        self.n, self.k, self.per = i * per_item, 0, per_item

    def step(self, ins):
        self.k += 1
        ins.then_inc(self.sem, 1)
        self.eng.wait_ge(self.sem, self.n + self.k)

    def end(self):
        assert self.k == self.per, (self.k, self.per)



def stack(ctx, nc, phase):
    def sb(name, shape, dt=F32):
        return ctx.enter_context(nc.sbuf_tensor(f"{phase}_{name}", shape, dt))

    def ps(name, shape, dt=F32):
        return ctx.enter_context(nc.psum_tensor(f"{phase}_ps_{name}", shape, dt))
    return sb, ps


def product(pe, out, lhs, rhs, steps):
    parts = ((0, 0), (0, 1), (1, 0))
    for k in range(steps):
        for n, (a, b) in enumerate(parts):
            last = pe.matmul(out, lhs[a](k), rhs[b](k), start=(k == 0 and n == 0), stop=(k == steps - 1 and n == 2))
    return last


def modulation(nc, A, S, sem, sems):
    with ExitStack() as ctx:
        sb, ps = stack(ctx, nc, "mod")
        NB = 6 * D // BANK
        cT = sb("cT", [P, KD])
        sc = sb("silu_c", [P, KD])
        sc_rep = sb("silu_c_rep", [P, KD, P])
        bT = sb("bT", [P, 6 * KD])
        wa = [sb(f"w{i}", [P, KD, BANK]) for i in range(3)]
        psT = ps("cols", [P, BANK])
        psG = [ps(f"gate{i}", [P, BANK]) for i in range(4)]
        small_in, consts, silu_done, rep_done = sem("mod_small_in"), sem("mod_consts"), sem("mod_silu"), sem("mod_rep")
        w_in = sems("mod_w", 3)
        w_used, bias_added = sem("mod_w_used"), sem("mod_bias")
        gate_of = {4: 0, 5: 1, 10: 2, 11: 3}

        with nc.Block() as block:
            @block.sync
            def _(sp):
                sp.dma_start(cT[:], A["cT"]).then_inc(small_in, 16)
                sp.dma_start(bT[:], A["b_adaT"]).then_inc(small_in, 16)
                sp.dma_start(S.g1[:], A["b_ada"][0, 2 * D:3 * D].partition_broadcast(P)).then_inc(small_in, 16)
                sp.dma_start(S.g2[:], A["b_ada"][0, 5 * D:6 * D].partition_broadcast(P)).then_inc(small_in, 16)
                for b in range(NB):
                    wait(sp, w_used, b - 2)
                    apart(sp, S)
                    sp.dma_start(wa[b % 3][:], A["w_ada_t"][b].rearrange("p (k n) -> p k n", k=KD)).then_inc(w_in[b % 3], 16)

            @block.gpsimd
            def _(pool):
                pool.memset(S.ones[:], 1.0).then_inc(consts, 1)
                pool.memset(S.eps[:], EPS).then_inc(consts, 1)
                pool.wait_ge(consts, 2)
                pool.affine_select(out=S.tri[:], in_=S.ones[:], pattern=[[1, P]], compare_op=ALU.is_ge, fill=0.0,
                                   base=0, channel_multiplier=-1).then_inc(consts, 1)
                pool.affine_select(out=S.ident[:], in_=S.ones[:], pattern=[[1, P]], compare_op=ALU.is_equal, fill=0.0,
                                   base=0, channel_multiplier=-1).then_inc(consts, 1)
                pool.wait_ge(consts, 4)

            @block.scalar
            def _(act):
                act.wait_ge(small_in, 64)
                act.activation(sc[:], cT[:], ACT.Silu).then_inc(silu_done, 1)

            @block.tensor
            def _(pe):
                pe.wait_ge(silu_done, 1)
                pe.wait_ge(rep_done, 1)
                for b in range(NB):
                    pe.wait_ge(w_in[b % 3], 16 * (b // 3 + 1))
                    if b in gate_of:
                        for k in range(KD):
                            last = pe.matmul(psG[gate_of[b]][:], sc_rep[:, k, :], wa[b % 3][:, k, :],
                                             start=(k == 0), stop=(k == KD - 1))
                    else:
                        for j in range(BANK // P):
                            col = b * (BANK // P) + j
                            for k in range(KD):
                                last = pe.matmul(psT[:, col:col + 1], wa[b % 3][:, k, j * P:(j + 1) * P],
                                                 sc[:, k:k + 1], start=(k == 0), stop=(k == KD - 1))
                    last.then_inc(w_used, 1)

            @block.vector
            def _(dve):
                dve.wait_ge(silu_done, 1)
                dve.tensor_copy(sc_rep[:], sc[:].unsqueeze(2).to_broadcast([P, KD, P])).then_inc(rep_done, 1)
                dve.wait_ge(small_in, 64)
                dve.wait_ge(w_used, NB)
                for first in (SH1, SH2):
                    dve.tensor_tensor(S.modT[:, first:first + KD], psT[:, first:first + KD],
                                      bT[:, first:first + KD], ALU.add).then_inc(bias_added, 1)
                for first in (SC1, SC2):
                    dve.scalar_tensor_tensor(out=S.modT[:, first:first + KD], in0=psT[:, first:first + KD], scalar=1.0,
                                             in1=bT[:, first:first + KD], op0=ALU.add, op1=ALU.add).then_inc(bias_added, 1)
                for i, row in enumerate((S.g1, S.g1, S.g2, S.g2)):
                    half = slice(i % 2 * BANK, (i % 2 + 1) * BANK)
                    dve.tensor_tensor(row[:, half], psG[i][:], row[:, half], ALU.add).then_inc(bias_added, 1)
                dve.wait_ge(bias_added, 8)


def norm_in(nc, A, S, sem, sems, h_hi, h_lo):
    with ExitStack() as ctx:
        sb, ps = stack(ctx, nc, "nin")
        xt = [sb(f"x{i}", [P, D]) for i in range(2)]
        xn = [sb(f"xn{i}", [P, D]) for i in range(2)]
        st = [sb(f"st{i}", [P, 2, 6]) for i in range(2)]
        mv = [sb(f"mv{i}", [P, 2]) for i in range(2)]
        sd = [sb(f"sd{i}", [P, 1]) for i in range(2)]
        rs = [sb(f"rs{i}", [P, 1]) for i in range(2)]
        ht = [sb(f"h{i}", [P, KD, P]) for i in range(2)]
        psT = [ps(f"t{i}", [P, KD, P]) for i in range(2)]
        x_in = sems("nin_x", 2)
        halves, stats, sqrt_done, inverse, normed, transposed, modulated, rounded, split = (
            sem("nin_halves"), sem("nin_stats"), sem("nin_sqrt"), sem("nin_inverse"), sem("nin_normed"),
            sem("nin_transposed"), sem("nin_modulated"), sem("nin_rounded"), sem("nin_split"))

        with nc.Block() as block:
            @block.sync
            def _(sp):
                def load(q, s):
                    wait(sp, normed, 2 * q + s - 1)
                    apart(sp, S)
                    sp.dma_start(xt[s][:], A["x"][bass.ds((2 * q + s) * P, P), :]).then_inc(x_in[s], 16)
                pipeline(sp, TT, 2, [(0, load)])

            @block.vector
            def _(dve):
                def norm(q, s):
                    t = 2 * q + s
                    dve.wait_ge(x_in[s], 16 * (q + 1))
                    for half in range(2):
                        dve.bn_stats(st[s][:, half, :], xt[s][:, half * BANK:(half + 1) * BANK]).then_inc(halves, 1)
                    dve.wait_ge(halves, 2 * (t + 1))
                    apart(dve, S)
                    dve.bn_aggr(mv[s][:], st[s][:]).then_inc(stats, 1)
                    dve.wait_ge(sqrt_done, t + 1)
                    dve.reciprocal(rs[s][:], sd[s][:]).then_inc(inverse, 1)
                    dve.wait_ge(inverse, t + 1)
                    wait(dve, transposed, t - 1)
                    dve.tensor_scalar(xn[s][:], xt[s][:], mv[s][:, 0:1], rs[s][:], ALU.subtract,
                                      ALU.mult).then_inc(normed, 1)

                def low(q, s):
                    t = 2 * q + s
                    dve.wait_ge(rounded, t + 1)
                    cols = bass.ds(t * P, P)
                    dve.tensor_tensor(h_lo[:, :, cols], ht[s][:], h_hi[:, :, cols].bitcast(F32),
                                      ALU.subtract).then_inc(split, 1)
                pipeline(dve, TT, 2, [(0, norm), (1, low)])
                dve.wait_ge(split, TT)

            @block.tensor
            def _(pe):
                def turn(q, s):
                    t = 2 * q + s
                    pe.wait_ge(normed, t + 1)
                    wait(pe, modulated, t - 1)
                    for k in range(KD):
                        last = pe.transpose(psT[s][:, k, :], xn[s][:, k * P:(k + 1) * P], S.ident[:])
                    last.then_inc(transposed, 1)
                pipeline(pe, TT, 2, [(0, turn)])

            @block.scalar
            def _(act):
                def root(q, s):
                    act.wait_ge(stats, 2 * q + s + 1)
                    act.activation(sd[s][:], mv[s][:, 1:2], ACT.Sqrt, bias=S.eps[:]).then_inc(sqrt_done, 1)

                def modulate(q, s):
                    t = 2 * q + s
                    act.wait_ge(transposed, t + 1)
                    wait(act, split, t - 1)
                    for k in range(KD):
                        last = act.activation(ht[s][:, k, :], psT[s][:, k, :], ACT.Identity,
                                              bias=S.modT[:, SH1 + k:SH1 + k + 1], scale=S.modT[:, SC1 + k:SC1 + k + 1])
                    last.then_inc(modulated, 1)
                    act.wait_ge(modulated, t + 1)
                    act.copy(h_hi[:, :, bass.ds(t * P, P)], ht[s][:]).then_inc(rounded, 1)
                pipeline(act, TT, 2, [(0, root), (1, modulate)])


def decay(nc, A, S, sem, sems, h_hi, h_lo):
    with ExitStack() as ctx:
        sb, ps = stack(ctx, nc, "dec")
        W = TT * HEADS
        w = sb("w", [P, KD, HEADS])
        w_hi = sb("w_hi", [P, KD, HEADS], F32R)
        w_lo = sb("w_lo", [P, KD, HEADS], F32R)
        bias = sb("bias", [P, HEADS])
        alog = sb("alog", [P, HEADS])
        a = sb("a", [P, HEADS])
        v = sb("v", [P, W])
        av = sb("av", [P, W])
        e = sb("e", [P, W])
        u = sb("u", [P, W])
        um = sb("um", [P, W])
        zero = sb("zero", [P, W])
        ln = sb("ln", [P, W])
        la = sb("la", [P, W])
        acT = sb("acT", [HEADS, SEQ])
        psD = ps("dt", [P, W])
        psA = ps("acum", [P, W])
        psE = ps("total", [P, W])
        psAT = ps("acumT", [HEADS, SEQ])
        loads, w_rounded, w_split, dt_done, link, exp_a, exp_v, ln_u, la_ready, sums, turned, copied, stored, tail = (
            sem("dec_loads"), sem("dec_w_rounded"), sem("dec_w_split"), sem("dec_dt"), sem("dec_link"), sem("dec_exp_a"),
            sem("dec_exp_v"), sem("dec_ln"), sem("dec_la"), sem("dec_sums"), sem("dec_turned"), sem("dec_copied"),
            sem("dec_stored"), sem("dec_tail"))

        def per_tile(t):
            return t[:].rearrange("p (t h) -> p t h", h=HEADS)

        with nc.Block() as block:
            @block.sync
            def _(sp):
                sp.dma_start(w[:], A["w_dt"].rearrange("p (k n) -> p k n", k=KD)).then_inc(loads, 16)
                sp.dma_start(bias[:], A["dt_bias"][0].partition_broadcast(P)).then_inc(loads, 16)
                sp.dma_start(alog[:], A["a_log"][0].partition_broadcast(P)).then_inc(loads, 16)
                sp.wait_ge(copied, 1)
                apart(sp, S)
                sp.dma_start(S.acum_d, acT[:]).then_inc(stored, 16)
                sp.wait_ge(stored, 16)

            @block.tensor
            def _(pe):
                pe.wait_ge(w_split, 1)
                for t in range(TT):
                    last = product(pe, psD[:, t * HEADS:(t + 1) * HEADS],
                                   [lambda k, x=x: x[:, k, t * P:(t + 1) * P] for x in (h_hi, h_lo)],
                                   [lambda k, x=x: x[:, k, :] for x in (w_hi, w_lo)], KD)
                last.then_inc(dt_done, 1)
                pe.wait_ge(la_ready, 1)
                pe.matmul(psA[:], S.tri[:], la[:], start=True, stop=True)
                pe.matmul(psE[:], S.ones[:], la[:], start=True, stop=True).then_inc(sums, 1)
                for t in range(TT):
                    last = pe.matmul(psAT[:, t * P:(t + 1) * P], la[:, t * HEADS:(t + 1) * HEADS], S.tri[:],
                                     start=True, stop=True)
                last.then_inc(turned, 1)

            @block.scalar
            def _(act):
                act.wait_ge(loads, 48)
                act.copy(w_hi[:], w[:]).then_inc(w_rounded, 1)
                act.activation(a[:], alog[:], ACT.Exp).then_inc(exp_a, 1)
                act.wait_ge(link, 2)
                act.activation(e[:], av[:], ACT.Exp, scale=-1.0).then_inc(exp_v, 1)
                act.wait_ge(link, 3)
                act.activation(ln[:], u[:], ACT.Ln).then_inc(ln_u, 1)
                act.wait_ge(sums, 1)
                act.activation(S.chunk_decay[:], psE[:], ACT.Exp).then_inc(tail, 1)
                act.wait_ge(link, 12)
                act.activation(S.decay[:], v[:], ACT.Exp).then_inc(tail, 1)
                act.wait_ge(turned, 1)
                act.copy(acT[:], psAT[:]).then_inc(copied, 1)
                act.wait_ge(tail, 2)

            @block.vector
            def _(dve):
                dve.wait_ge(w_rounded, 1)
                dve.tensor_tensor(w_lo[:], w[:], w_hi[:].bitcast(F32), ALU.subtract).then_inc(w_split, 1)
                chain = Chain(dve, link)
                dve.wait_ge(loads, 48)
                dve.wait_ge(dt_done, 1)
                chain.step(dve.tensor_tensor(per_tile(v), per_tile(psD), bias[:].unsqueeze(1).to_broadcast([P, TT, HEADS]), ALU.add))
                chain.step(dve.scalar_tensor_tensor(out=av[:], in0=v[:], scalar=-1.0, in1=v[:], op0=ALU.mult, op1=ALU.max))
                dve.wait_ge(exp_v, 1)
                chain.step(dve.tensor_scalar(u[:], e[:], 1.0, None, ALU.add))
                chain.step(dve.tensor_scalar(um[:], u[:], -1.0, None, ALU.add))
                chain.step(dve.tensor_scalar(zero[:], um[:], 0.0, None, ALU.is_equal))
                chain.step(dve.tensor_tensor(um[:], um[:], zero[:], ALU.add))
                dve.wait_ge(ln_u, 1)
                chain.step(dve.tensor_tensor(ln[:], ln[:], zero[:], ALU.add))
                chain.step(dve.reciprocal(um[:], um[:]))
                chain.step(dve.tensor_tensor(ln[:], ln[:], um[:], ALU.mult))
                chain.step(dve.tensor_tensor(ln[:], ln[:], e[:], ALU.mult))
                chain.step(dve.scalar_tensor_tensor(out=S.dt[:], in0=v[:], scalar=0.0, in1=ln[:], op0=ALU.max, op1=ALU.add))
                dve.wait_ge(exp_a, 1)
                dve.scalar_tensor_tensor(out=per_tile(la), in0=per_tile(S.dt), scalar=-1.0,
                                         in1=a[:].unsqueeze(1).to_broadcast([P, TT, HEADS]), op0=ALU.mult,
                                         op1=ALU.mult).then_inc(la_ready, 1)
                dve.wait_ge(sums, 1)
                dve.tensor_copy(S.acum[:], psA[:]).then_inc(la_ready, 1)
                dve.wait_ge(la_ready, 2)
                dve.wait_ge(tail, 1)
                chain.step(dve.tensor_tensor(v[:], psE[:], S.acum[:], ALU.subtract))


def project(nc, A, S, sem, sems, h_hi, h_lo):
    with ExitStack() as ctx:
        sb, ps = stack(ctx, nc, "prj")
        TB = SEQ // BANK
        w = [sb(f"w{i}", [P, KD, P]) for i in range(2)]
        w_hi = [sb(f"w_hi{i}", [P, KD, P], F32R) for i in range(2)]
        w_lo = [sb(f"w_lo{i}", [P, KD, P], F32R) for i in range(2)]
        ob = [sb(f"out{i}", [P, SEQ]) for i in range(2)]
        c_sb = sb("c", [P, SEQ])
        cx = sb("cx", [P, SEQ])
        cw = sb("conv_w", [P, N_XBC * CONV])
        cb = sb("conv_b", [P, N_XBC])
        sw = sb("short_w", [P, N_SC * SCONV])
        gb = sb("gate_b", [P, N_GATE])
        psP = [ps(f"p{i}", [P, SEQ]) for i in range(2)]
        w_in = sems("prj_w", 2)
        stored = sems("prj_stored", 2)
        params, w_rounded, w_split, done, act_out, act_part, drained, link = (
            sem("prj_params"), sem("prj_w_rounded"), sem("prj_w_split"), sem("prj_done"), sem("prj_act_out"),
            sem("prj_act_part"), sem("prj_drained"), sem("prj_link"))
        X0, C0, G0 = N_Z, N_Z + N_XBC, N_Z + N_XBC + 3 * N_SC

        def kinds(eng, z, xbc, short, gate):
            for s in range(2):
                z(s, s, s)
            with eng.Fori(1, N_Z // 2) as r:
                for s in range(2):
                    z(r * 2 + s, r * 2 + s, s)
            with eng.Fori(0, N_XBC // 2) as r:
                for s in range(2):
                    xbc(X0 + r * 2 + s, r * 2 + s, s)
            with eng.Fori(0, N_SC // 2) as r:
                for s in range(2):
                    for part in range(3):
                        short(C0 + r * 6 + s * 3 + part, r * 2 + s, s, part)
            with eng.Fori(0, N_GATE // 2 - 1) as r:
                for s in range(2):
                    gate(G0 + r * 2 + s, r * 2 + s, s)
            for s in range(2):
                gate(N_PROJ - 2 + s, N_GATE - 2 + s, s)

        with nc.Block() as block:
            @block.sync
            def _(sp):
                apart(sp, S)
                for dst, name in ((cw, "conv_w"), (cb, "conv_b"), (sw, "short_w"), (gb, "b_gateT")):
                    sp.dma_start(dst[:], A[name]).then_inc(params, 16)

                def load(q, s):
                    n = 2 * q + s
                    wait(sp, w_split, n - 1)
                    apart(sp, S)
                    sp.dma_start(w[s][:], A["w_in_t"][bass.ds(n * P, P), :].rearrange("p (k m) -> p k m", k=KD)).then_inc(w_in[s], 16)
                pipeline(sp, N_PROJ, 2, [(0, load)])

            @block.tensor
            def _(pe):
                def tile(q, s):
                    n = 2 * q + s
                    pe.wait_ge(w_split, n + 1)
                    wait(pe, drained, n - 1)
                    for b in range(TB):
                        last = product(pe, psP[s][:, b * BANK:(b + 1) * BANK],
                                       [lambda k, x=x: x[:, k, :] for x in (w_hi[s], w_lo[s])],
                                       [lambda k, x=x: x[:, k, b * BANK:(b + 1) * BANK] for x in (h_hi, h_lo)], KD)
                    last.then_inc(done, 1)
                pipeline(pe, N_PROJ, 2, [(0, tile)])

            @block.scalar
            def _(act):
                def round_w(n, s):
                    act.wait_ge(w_in[s], 8 * (n - s) + 16)
                    wait(act, done, n - 1)
                    act.copy(w_hi[s][:], w[s][:]).then_inc(w_rounded, 1)

                def ahead(n, s):
                    if not (isinstance(n, int) and n + 1 >= N_PROJ):
                        round_w(n + 1, 1 - s)
                    act.wait_ge(done, n + 1)

                def z(n, i, s):
                    ahead(n, s % 2)
                    wait(act, stored[s], 8 * (ROW_Z + i - s))
                    act.activation(ob[s][:], psP[s][:], ACT.Silu).then_inc(act_out, 1)

                def xbc(n, i, s):
                    ahead(n, s)
                    act.wait_ge(stored[s], 8 * (ROW_XBC + i - s))
                    act.activation(ob[s][:], psP[s][:], ACT.Identity, bias=cb[:, bass.ds(i, 1)],
                                   scale=cw[:, bass.ds(i * CONV + CONV - 1, 1)]).then_inc(act_part, 1)
                    act.wait_ge(drained, n + 1)
                    act.activation(ob[s][:], ob[s][:], ACT.Silu).then_inc(act_out, 1)

                def short(n, i, s, part):
                    slot = (3 * s + part) % 2
                    ahead(n, slot)
                    if part == 0:
                        act.wait_ge(drained, n - 1)
                        act.copy(c_sb[:], psP[slot][:]).then_inc(act_part, 1)

                def gate(n, i, s):
                    ahead(n, s)
                    act.wait_ge(stored[s], 8 * (ROW_GATE + i - s))
                    act.activation(ob[s][:], psP[s][:], ACT.Sigmoid, bias=gb[:, bass.ds(i, 1)]).then_inc(act_out, 1)

                act.wait_ge(params, 64)
                round_w(0, 0)
                kinds(act, z, xbc, short, gate)

            @block.vector
            def _(dve):
                chain = Chain(dve, link)

                def split_w(n, s):
                    dve.wait_ge(w_rounded, n + 1)
                    dve.tensor_tensor(w_lo[s][:], w[s][:], w_hi[s][:].bitcast(F32), ALU.subtract).then_inc(w_split, 1)

                def ahead(n, s):
                    if not (isinstance(n, int) and n + 1 >= N_PROJ):
                        split_w(n + 1, 1 - s)

                def z(n, i, s):
                    ahead(n, s)
                    dve.wait_ge(act_out, n + 1)
                    wait(dve, drained, n)
                    dve.sem_inc(drained, 1)

                def xbc(n, i, s):
                    ahead(n, s)
                    dve.wait_ge(act_part, i + 1)
                    chain.item(i, CONV - 2)
                    for shift in range(1, CONV):
                        ins = dve.scalar_tensor_tensor(out=ob[s][:, shift:], in0=psP[s][:, :SEQ - shift],
                                                       scalar=cw[:, bass.ds(i * CONV + CONV - 1 - shift, 1)],
                                                       in1=ob[s][:, shift:], op0=ALU.mult, op1=ALU.add)
                        if shift < CONV - 1:
                            chain.step(ins)
                        else:
                            ins.then_inc(drained, 1)
                    chain.end()

                def short(n, i, s, part):
                    slot = (3 * s + part) % 2
                    ahead(n, slot)
                    first = N_XBC * (CONV - 2)
                    if part == 0:
                        dve.wait_ge(act_part, N_XBC + i + 1)
                        dve.wait_ge(drained, n)
                        dve.sem_inc(drained, 1)
                    if part == 1:
                        dve.wait_ge(done, n + 1)
                        dve.tensor_tensor(cx[:], psP[slot][:], c_sb[:], ALU.mult).then_inc(drained, 1)
                        dve.wait_ge(drained, n + 1)
                        dve.wait_ge(stored[s], 8 * (ROW_Q + i - s))
                        chain.item(i, SCONV)
                        chain.n = chain.n + first
                        chain.step(dve.tensor_scalar(ob[s][:], cx[:], sw[:, bass.ds(i * SCONV + SCONV - 1, 1)], None, ALU.mult))
                        for shift in range(1, SCONV):
                            chain.step(dve.scalar_tensor_tensor(out=ob[s][:, shift:], in0=cx[:, :SEQ - shift],
                                                                scalar=sw[:, bass.ds(i * SCONV + SCONV - 1 - shift, 1)],
                                                                in1=ob[s][:, shift:], op0=ALU.mult, op1=ALU.add))
                        chain.end()
                    if part == 2:
                        dve.wait_ge(done, n + 1)
                        dve.tensor_tensor(ob[s][:], psP[slot][:], ob[s][:], ALU.mult).then_inc(drained, 1)

                def gate(n, i, s):
                    ahead(n, s)
                    dve.wait_ge(act_out, N_Z + N_XBC + i + 1)
                    dve.wait_ge(drained, n)
                    dve.sem_inc(drained, 1)

                dve.wait_ge(params, 64)
                split_w(0, 0)
                kinds(dve, z, xbc, short, gate)

            @block.gpsimd
            def _(pool):
                def store(m, s):
                    apart(pool, S)
                    pool.dma_start(S.rows_d[bass.ds(m * P, P), :], ob[s][:]).then_inc(stored[s], 16)

                def by_act(n, i, s, row, count):
                    pool.wait_ge(act_out, count)
                    store(row + i, s)

                def short(n, i, s, part):
                    if part == 2:
                        pool.wait_ge(drained, n + 1)
                        store(ROW_Q + i, s)

                kinds(pool, lambda n, i, s: by_act(n, i, s, ROW_Z, i + 1),
                      lambda n, i, s: by_act(n, i, s, ROW_XBC, i + N_Z + 1), short,
                      lambda n, i, s: by_act(n, i, s, ROW_GATE, i + N_Z + N_XBC + 1))
                for s in range(2):
                    pool.wait_ge(stored[s], 8 * N_ROWS)


def ssd(nc, A, S, sem, sems):
    with ExitStack() as ctx:
        sb, ps = stack(ctx, nc, "ssd")
        GT = HG * HD // P
        LOADS = 5
        xT = [sb(f"xT{i}", [P, GT, P]) for i in range(4)]
        zT = [sb(f"zT{i}", [P, GT, P]) for i in range(4)]
        bT = [sb(f"bT{i}", [P, P]) for i in range(4)]
        cT = [sb(f"cT{i}", [P, P]) for i in range(4)]
        ab = [sb(f"acum{i}", [P, HG, P]) for i in range(4)]
        xd = [sb(f"xd{i}", [P, HG, HD]) for i in range(2)]
        xdd = [sb(f"xdd{i}", [P, HG, HD]) for i in range(2)]
        b_tok = [sb(f"b{i}", [P, P]) for i in range(2)]
        cbm = [sb(f"cbm{i}", [P, P]) for i in range(2)]
        seg = [sb(f"seg{i}", [P, HG, P]) for i in range(2)]
        ldec = [sb(f"ldec{i}", [P, HG, P]) for i in range(2)]
        m = [sb(f"m{i}", [P, HG, P]) for i in range(2)]
        ea = [sb(f"ea{i}", [P, HG, P]) for i in range(2)]
        cs = [sb(f"cs{i}", [P, HG, P]) for i in range(2)]
        xs = [sb(f"xs{i}", [P, GT, P]) for i in range(2)]
        yo = [sb(f"y{i}", [P, GT, P]) for i in range(4)]
        prev = [sb(f"state{i}", [P, HG, HD]) for i in range(4)]
        dsk = sb("d_skip", [P, INNER // P])
        psX = [ps(f"x{i}", [P, GT * P]) for i in range(2)]
        psB = [ps(f"b{i}", [P, BANK]) for i in range(2)]
        psY = [ps(f"y{i}", [P, GT * P]) for i in range(2)]
        psS = [ps(f"s{i}", [P, HG * HD]) for i in range(2)]
        loaded = sems("ssd_in", 4)
        stored = sems("ssd_stored", 4)
        d_in, zeroed, turned, x_ready, seg_ready, m_ready, ea_ready, b_ready, l_ready, xdd_ready, cs_ready, xs_ready, \
            y_done, skipped, decayed, state_ready, y_ready, masked = (sem(f"ssd_{n}") for n in (
                "d", "zeroed", "turned", "x", "seg", "m", "ea", "b", "l", "xdd", "cs", "xs", "y_done", "skipped",
                "decayed", "state", "y", "masked"))

        def heads(t, c, g):
            return t[:, bass.ds(c * HEADS + g * HG, HG)]

        with nc.Block() as block:
            @block.sync
            def _(sp):
                def store(c, g):
                    sp.wait_ge(y_ready, 4 * c + g + 1)
                    apart(sp, S)
                    sp.dma_start(S.y_d[g * GT * P:(g + 1) * GT * P, bass.ds(c * P, P)].rearrange("(a p) t -> p a t", p=P),
                                 yo[g][:]).then_inc(stored[g], 16)

                def load(c, g):
                    cols = bass.ds(c * P, P)
                    for dst, row, tiles in ((xT[g], ROW_XBC + g * GT, GT), (zT[g], ROW_Z + g * GT, GT)):
                        sp.dma_start(dst[:], S.rows_d[row * P:(row + tiles) * P, cols].rearrange(
                            "(a p) t -> p a t", p=P)).then_inc(loaded[g], 16)
                    for dst, row in ((bT[g], ROW_XBC + N_Z + g), (cT[g], ROW_XBC + N_Z + GROUPS + g)):
                        sp.dma_start(dst[:], S.rows_d[row * P:(row + 1) * P, cols]).then_inc(loaded[g], 16)
                    sp.dma_start(ab[g][:], S.acum_d[g * HG:(g + 1) * HG, cols].partition_broadcast(P)).then_inc(loaded[g], 16)

                sp.dma_start(dsk[:], A["d_skipT"]).then_inc(d_in, 16)
                pipeline(sp, 4 * TT, 4, [(4, store), (0, load)])
                for g in range(4):
                    sp.wait_ge(stored[g], 16 * TT)

            @block.tensor
            def _(pe):
                def front(c, g):
                    u, s = 4 * c + g, g % 2
                    pe.wait_ge(loaded[g], 16 * LOADS * (c + 1))
                    wait(pe, x_ready, u - 1)
                    wait(pe, b_ready, u - 1)
                    wait(pe, masked, u - 1)
                    for a in range(GT):
                        pe.transpose(psX[s][:, a * P:(a + 1) * P], xT[g][:, a, :], S.ident[:])
                    pe.transpose(psB[s][:, 0:P], bT[g][:], S.ident[:])
                    pe.matmul(psB[s][:, P:2 * P], bT[g][:], cT[g][:], start=True, stop=True).then_inc(turned, 1)

                def back(c, g):
                    u, s = 4 * c + g, g % 2
                    pe.wait_ge(x_ready, u + 1)
                    pe.wait_ge(m_ready, u + 1)
                    pe.wait_ge(cs_ready, u + 1)
                    pe.wait_ge(zeroed, 4)
                    wait(pe, state_ready, u - 3)
                    wait(pe, skipped, u - 1)
                    for h in range(HG):
                        rows, cols = slice(h % 2 * HD, (h % 2 + 1) * HD), slice(h // 2 * P, (h // 2 + 1) * P)
                        pe.matmul(psY[s][rows, cols], xd[s][:, h, :], m[s][:, h, :], start=True, stop=False)
                        last = pe.matmul(psY[s][rows, cols], prev[g][:, h, :], cs[s][:, h, :], start=False, stop=True)
                    pe.wait_ge(b_ready, u + 1)
                    pe.wait_ge(xdd_ready, u + 1)
                    wait(pe, state_ready, u - 1)
                    pe.matmul(psS[s][:], b_tok[s][:], xdd[s][:].rearrange("p h d -> p (h d)"),
                              start=True, stop=True).then_inc(y_done, 1)
                pipeline(pe, 4 * TT, 4, [(0, front), (1, back)])

            @block.scalar
            def _(act):
                def front(c, g):
                    u, s = 4 * c + g, g % 2
                    act.wait_ge(loaded[g], 16 * LOADS * (c + 1))
                    wait(act, cs_ready, u - 1)
                    act.activation(ea[s][:], ab[g][:], ACT.Exp).then_inc(ea_ready, 1)
                    act.wait_ge(turned, u + 1)
                    wait(act, y_done, u - 1)
                    act.copy(b_tok[s][:], psB[s][:, 0:P]).then_inc(b_ready, 1)
                    act.wait_ge(seg_ready, u + 1)
                    wait(act, m_ready, u - 1)
                    act.activation(ldec[s][:], seg[s][:], ACT.Exp).then_inc(l_ready, 1)
                pipeline(act, 4 * TT, 4, [(0, front)])

            @block.vector
            def _(dve):
                def front(c, g):
                    u, s = 4 * c + g, g % 2
                    dve.wait_ge(loaded[g], 16 * LOADS * (c + 1))
                    wait(dve, l_ready, u - 1)
                    for h in range(HG):
                        last = dve.tensor_scalar(seg[s][:, h, :], ab[g][:, h, :], S.acum[:, bass.ds(c * HEADS + g * HG + h, 1)],
                                                 0.0, ALU.subtract, ALU.min)
                    last.then_inc(seg_ready, 1)
                    dve.wait_ge(turned, u + 1)
                    wait(dve, y_done, u - 1)
                    wait(dve, xdd_ready, u - 1)
                    dve.tensor_tensor(xd[s][:], psX[s][:].rearrange("p (h d) -> p h d", h=HG),
                                      heads(S.dt, c, g).unsqueeze(2).to_broadcast([P, HG, HD]), ALU.mult).then_inc(x_ready, 1)
                    dve.wait_ge(b_ready, u + 1)
                    dve.tensor_tensor(cbm[s][:], psB[s][:, P:2 * P], S.tri[:], ALU.mult).then_inc(masked, 1)

                def back(c, g):
                    u, s = 4 * c + g, g % 2
                    dve.wait_ge(y_done, u + 1)
                    dve.tensor_tensor(prev[g][:], prev[g][:], heads(S.chunk_decay, c, g).unsqueeze(2).to_broadcast([P, HG, HD]),
                                      ALU.mult).then_inc(decayed, 1)
                    dve.wait_ge(xs_ready, u + 1)
                    wait(dve, stored[g], 16 * c)
                    dve.tensor_tensor(yo[g][:], psY[s][:].rearrange("p (a t) -> p a t", a=GT), xs[s][:], ALU.add).then_inc(skipped, 1)
                    dve.wait_ge(decayed, u + 1)
                    dve.tensor_tensor(prev[g][:], psS[s][:].rearrange("p (h d) -> p h d", h=HG), prev[g][:],
                                      ALU.add).then_inc(state_ready, 1)
                    dve.wait_ge(skipped, u + 1)
                    dve.tensor_tensor(yo[g][:], yo[g][:], zT[g][:], ALU.mult).then_inc(y_ready, 1)

                def decayed_scores(c, g):
                    u, s = 4 * c + g, g % 2
                    dve.wait_ge(l_ready, u + 1)
                    dve.wait_ge(masked, u + 1)
                    dve.tensor_tensor(m[s][:], ldec[s][:], cbm[s][:].unsqueeze(1).to_broadcast([P, HG, P]),
                                      ALU.mult).then_inc(m_ready, 1)

                for g in range(4):
                    dve.memset(prev[g][:], 0.0).then_inc(zeroed, 1)
                dve.wait_ge(zeroed, 4)
                pipeline(dve, 4 * TT, 4, [(0, front), (1, back), (0, decayed_scores)])

            @block.gpsimd
            def _(pool):
                def unit(c, g):
                    u, s = 4 * c + g, g % 2
                    pool.wait_ge(ea_ready, u + 1)
                    wait(pool, y_done, u - 1)
                    pool.tensor_tensor(cs[s][:], ea[s][:], cT[g][:].unsqueeze(1).to_broadcast([P, HG, P]), ALU.mult).then_inc(cs_ready, 1)
                    pool.wait_ge(x_ready, u + 1)
                    pool.tensor_tensor(xdd[s][:], xd[s][:], heads(S.decay, c, g).unsqueeze(2).to_broadcast([P, HG, HD]),
                                       ALU.mult).then_inc(xdd_ready, 1)
                    wait(pool, skipped, u - 1)
                    pool.tensor_tensor(xs[s][:], xT[g][:], dsk[:, g * GT:(g + 1) * GT].unsqueeze(2).to_broadcast([P, GT, P]),
                                       ALU.mult).then_inc(xs_ready, 1)
                pool.wait_ge(d_in, 16)
                pipeline(pool, 4 * TT, 4, [(0, unit)])


def branches(nc, A, S, sem, sems):
    with ExitStack() as ctx:
        sb, ps = stack(ctx, nc, "brn")
        KY, KQ = INNER // P, KD
        ITEMS = KY + KQ
        NU = D // P
        TB = SEQ // BANK
        raw = [sb(f"raw{i}", [P, BANK]) for i in range(4)]
        hi = sb("hi", [P, ITEMS, BANK], F32R)
        lo = sb("lo", [P, ITEMS, BANK], F32R)
        sq = [sb(f"sq{i}", [P, BANK]) for i in range(2)]
        sqs = sb("sq_sum", [P, BANK])
        rstd = sb("rstd", [P, BANK])
        w = sb("w", [P, ITEMS, P])
        w_hi = [sb(f"w_hi{i}", [P, ITEMS, P], F32R) for i in range(2)]
        w_lo = [sb(f"w_lo{i}", [P, ITEMS, P], F32R) for i in range(2)]
        ga = [sb(f"ga{i}", [P, BANK]) for i in range(2)]
        gb = [sb(f"gb{i}", [P, BANK]) for i in range(2)]
        ta = [sb(f"ta{i}", [P, BANK]) for i in range(2)]
        tb_ = [sb(f"tb{i}", [P, BANK]) for i in range(2)]
        nw = sb("norm_w", [P, KY])
        psA = [ps(f"a{i}", [P, BANK]) for i in range(2)]
        psB = [ps(f"b{i}", [P, BANK]) for i in range(2)]
        psQ = ps("squares", [P, BANK])
        raw_in, w_in, stored = sems("brn_raw", 4), sems("brn_w", 2), sems("brn_stored", 2)
        nw_in, rounded, squared, low, item_done, w_rounded, w_split, unit_done, ss_done, root_done, rstd_ready, part_a, \
            part_b, scaled, combined = (sem(f"brn_{n}") for n in (
                "nw", "rounded", "squared", "low", "item", "w_rounded", "w_split", "unit", "ss", "root", "rstd", "part_a",
                "part_b", "scaled", "combined"))

        def units(eng, tb, fn):
            for s in range(2):
                fn(tb * NU + s, s, s)
            with eng.Fori(1, NU // 2) as r:
                for s in range(2):
                    fn(r * 2 + (tb * NU + s), r * 2 + s, s)

        with nc.Block() as block:
            @block.sync
            def _(sp):
                sp.dma_start(nw[:], A["ssd_norm_wT"]).then_inc(nw_in, 16)

                def load(u, n, s, tb):
                    wait(sp, w_split, u)
                    apart(sp, S)
                    wait(sp, combined, u - 1)
                    apart(sp, S)
                    sp.dma_start(w[:], A["w_branch_t"][bass.ds(n * P, P), :].rearrange("p (k m) -> p k m", k=ITEMS)).then_inc(w_in[s], 16)
                    for dst, row in ((ga, ROW_GATE), (gb, ROW_GATE + NU)):
                        sp.dma_start(dst[s][:], S.rows_d[bass.ds((n + row) * P, P), tb * BANK:(tb + 1) * BANK]).then_inc(w_in[s], 16)

                for tb in range(TB):
                    for j in range(ITEMS):
                        i = tb * ITEMS + j
                        src = S.y_d[j * P:(j + 1) * P] if j < KY else S.rows_d[(ROW_Q + j - KY) * P:(ROW_Q + j - KY + 1) * P]
                        wait(sp, item_done, i - 3)
                        apart(sp, S)
                        sp.dma_start(raw[j % 4][:], src[:, tb * BANK:(tb + 1) * BANK]).then_inc(raw_in[j % 4], 16)
                    units(sp, tb, lambda u, n, s: load(u, n, s, tb))

            @block.gpsimd
            def _(pool):
                for tb in range(TB):
                    def store(u, n, s):
                        pool.wait_ge(combined, u + 1)
                        apart(pool, S)
                        pool.dma_start(S.mixin_d[bass.ds(n * P, P), tb * BANK:(tb + 1) * BANK], ta[s][:]).then_inc(stored[s], 16)
                    units(pool, tb, store)
                for s in range(2):
                    pool.wait_ge(stored[s], 16 * TB * NU // 2)

            @block.scalar
            def _(act):
                def round_w(u, n, s):
                    act.wait_ge(w_in[s], 24 * (u - s) + 48)
                    wait(act, unit_done, u - 1)
                    act.copy(w_hi[s][:], w[:]).then_inc(w_rounded, 1)
                    if isinstance(u, int) and u % NU == 1:
                        act.wait_ge(ss_done, u // NU + 1)
                        act.activation(rstd[:], psQ[:], ACT.Sqrt, bias=S.eps[:], scale=1.0 / INNER).then_inc(root_done, 1)

                act.wait_ge(nw_in, 16)
                for tb in range(TB):
                    wait(act, unit_done, tb * NU)
                    wait(act, combined, tb * NU)
                    for j in range(ITEMS):
                        act.wait_ge(raw_in[j % 4], 16 * ((tb * ITEMS + j) // 4 + 1))
                        if j < KY:
                            act.activation(hi[:, j, :], raw[j % 4][:], ACT.Identity, scale=nw[:, j:j + 1]).then_inc(rounded, 1)
                            wait(act, item_done, tb * ITEMS + j - 1 if j >= 2 else 0)
                            act.activation(sq[j % 2][:], raw[j % 4][:], ACT.Square).then_inc(squared, 1)
                        else:
                            act.copy(hi[:, j, :], raw[j % 4][:]).then_inc(rounded, 1)
                    units(act, tb, round_w)

            @block.vector
            def _(dve):
                def split_w(u, n, s):
                    dve.wait_ge(w_rounded, u + 1)
                    dve.tensor_tensor(w_lo[s][:], w[:], w_hi[s][:].bitcast(F32), ALU.subtract).then_inc(w_split, 1)

                def combine(u, n, s):
                    dve.wait_ge(unit_done, u + 1)
                    wait(dve, stored[s], 8 * (u - s))
                    dve.tensor_tensor(ta[s][:], psA[s][:], rstd[:], ALU.mult).then_inc(part_a, 1)
                    dve.tensor_tensor(tb_[s][:], psB[s][:], gb[s][:], ALU.mult).then_inc(part_b, 1)
                    dve.wait_ge(part_a, u + 1)
                    dve.tensor_tensor(ta[s][:], ta[s][:], ga[s][:], ALU.mult).then_inc(scaled, 1)
                    dve.wait_ge(part_b, u + 1)
                    dve.wait_ge(scaled, u + 1)
                    dve.tensor_tensor(ta[s][:], ta[s][:], tb_[s][:], ALU.add).then_inc(combined, 1)

                dve.wait_ge(nw_in, 16)
                for tb in range(TB):
                    for j in range(ITEMS):
                        i = tb * ITEMS + j
                        dve.wait_ge(rounded, i + 1)
                        if j < KY:
                            dve.scalar_tensor_tensor(out=lo[:, j, :], in0=raw[j % 4][:], scalar=nw[:, j:j + 1],
                                                     in1=hi[:, j, :].bitcast(F32), op0=ALU.mult, op1=ALU.subtract).then_inc(low, 1)
                            dve.wait_ge(low, tb * KY + j + 1)
                            dve.wait_ge(squared, tb * KY + j + 1)
                            if j == 0:
                                wait(dve, ss_done, tb)
                                dve.tensor_copy(sqs[:], sq[0][:]).then_inc(item_done, 1)
                            else:
                                dve.wait_ge(item_done, i)
                                dve.tensor_tensor(sqs[:], sqs[:], sq[j % 2][:], ALU.add).then_inc(item_done, 1)
                        else:
                            dve.tensor_tensor(lo[:, j, :], raw[j % 4][:], hi[:, j, :].bitcast(F32), ALU.subtract).then_inc(item_done, 1)
                    split_w(tb * NU, 0, 0)
                    split_w(tb * NU + 1, 1, 1)
                    dve.wait_ge(root_done, tb + 1)
                    dve.reciprocal(rstd[:], rstd[:]).then_inc(rstd_ready, 1)
                    dve.wait_ge(rstd_ready, tb + 1)
                    with dve.Fori(0, NU // 2 - 1) as r:
                        for s in range(2):
                            combine(r * 2 + (tb * NU + s), r * 2 + s, s)
                            split_w(r * 2 + (tb * NU + s + 2), r * 2 + s + 2, s)
                    for s in range(2):
                        combine(tb * NU + NU - 2 + s, NU - 2 + s, s)

            @block.tensor
            def _(pe):
                for tb in range(TB):
                    def unit(u, n, s):
                        if isinstance(n, int) and n == 0:
                            pe.wait_ge(item_done, (tb + 1) * ITEMS)
                        pe.wait_ge(w_split, u + 1)
                        wait(pe, combined, u - 1)
                        product(pe, psA[s][:], [lambda k, x=x: x[:, k, :] for x in (w_hi[s], w_lo[s])],
                                [lambda k, x=x: x[:, k, :] for x in (hi, lo)], KY)
                        product(pe, psB[s][:], [lambda k, x=x: x[:, KY + k, :] for x in (w_hi[s], w_lo[s])],
                                [lambda k, x=x: x[:, KY + k, :] for x in (hi, lo)], KQ).then_inc(unit_done, 1)
                        if isinstance(n, int) and n == 0:
                            wait(pe, rstd_ready, tb)
                            pe.matmul(psQ[:], S.ones[:], sqs[:], start=True, stop=True).then_inc(ss_done, 1)
                    units(pe, tb, unit)


def mix_out(nc, A, S, sem, sems):
    with ExitStack() as ctx:
        sb, ps = stack(ctx, nc, "mix")
        wo_hi = sb("wo_hi", [P, KD, D], F32R)
        wo_lo = sb("wo_lo", [P, KD, D], F32R)
        wr = sb("w_router", [P, KD, EXPERTS])
        br = sb("b_router", [P, EXPERTS])
        lg = sb("ln_g", [P, D])
        lb = sb("ln_b", [P, D])
        wo = [sb(f"wo{i}", [P, D]) for i in range(2)]

        def pair(name, shape, dt=F32):
            return [sb(f"{name}{i}", shape, dt) for i in range(2)]
        mt, mt_hi, mt_lo = pair("m", [P, KD, P]), pair("m_hi", [P, KD, P], F32R), pair("m_lo", [P, KD, P], F32R)
        xt, r, x1, xn = pair("x", [P, D]), pair("r", [P, D]), pair("x1", [P, D]), pair("xn", [P, D])
        st, mv, sd, rs = pair("st", [P, 2, 6]), pair("mv", [P, 2]), pair("sd", [P, 1]), pair("rs", [P, 1])
        st2, mv2, sd2, rs2 = pair("st2", [P, 2, 6]), pair("mv2", [P, 2]), pair("sd2", [P, 1]), pair("rs2", [P, 1])
        hT = pair("hT", [P, KD, P])
        psM = [ps(f"m{i}", [P, D]) for i in range(2)]
        psT = ps("t", [P, KD, P])
        psL = ps("logits", [P, BANK])
        par_in, wo_rounded, wo_split = sem("mix_params"), sem("mix_wo_rounded"), sem("mix_wo_split")
        wo_in, t_in, x1_out, xn_out = sems("mix_wo", 2), sems("mix_in", 2), sems("mix_x1_out", 2), sems("mix_xn_out", 2)
        m_rounded, m_split, mixed, gated, summed, halves, stats, root1, inv1, normed, scaled, x1_ready, halves2, stats2, \
            root2, inv2, xn_ready, turned, modulated, routed, logits = (sem(f"mix_{n}") for n in (
                "m_rounded", "m_split", "mixed", "gated", "summed", "halves", "stats", "root1", "inv1", "normed", "scaled",
                "x1", "halves2", "stats2", "root2", "inv2", "xn", "turned", "modulated", "routed", "logits"))

        with nc.Block() as block:
            @block.sync
            def _(sp):
                sp.dma_start(wr[:], A["w_router_t"].rearrange("p (k n) -> p k n", k=KD)).then_inc(par_in, 16)
                for dst, name in ((br, "b_router"), (lg, "ln1_g"), (lb, "ln1_b")):
                    sp.dma_start(dst[:], A[name][0].partition_broadcast(P)).then_inc(par_in, 16)
                for k in range(KD):
                    wait(sp, wo_split, k - 1)
                    apart(sp, S)
                    sp.dma_start(wo[k % 2][:], A["w_o"][k * P:(k + 1) * P, :]).then_inc(wo_in[k % 2], 16)

                def load(q, s):
                    t = 2 * q + s
                    wait(sp, summed, t - 1)
                    apart(sp, S)
                    sp.dma_start(mt[s][:], S.mixin_d[:, bass.ds(t * P, P)].rearrange("(k p) t -> p k t", p=P)).then_inc(t_in[s], 16)
                    sp.dma_start(xt[s][:], A["x"][bass.ds(t * P, P), :]).then_inc(t_in[s], 16)
                pipeline(sp, TT, 2, [(0, load)])

            @block.gpsimd
            def _(pool):
                def affine(q, s):
                    t = 2 * q + s
                    pool.wait_ge(normed, t + 1)
                    wait(pool, x1_out[s], 16 * q)
                    wait(pool, stats2, t - 1)
                    wait(pool, xn_ready, t - 1)
                    pool.tensor_tensor(x1[s][:], r[s][:], lg[:], ALU.mult).then_inc(scaled, 1)
                    pool.wait_ge(scaled, t + 1)
                    pool.tensor_tensor(x1[s][:], x1[s][:], lb[:], ALU.add).then_inc(x1_ready, 1)

                def store(q, s):
                    t = 2 * q + s
                    pool.wait_ge(x1_ready, t + 1)
                    apart(pool, S)
                    pool.dma_start(S.x1_d[bass.ds(t * P, P), :], x1[s][:]).then_inc(x1_out[s], 16)
                    pool.wait_ge(xn_ready, t + 1)
                    apart(pool, S)
                    pool.dma_start(S.xn2_d[bass.ds(t * P, P), :], xn[s][:]).then_inc(xn_out[s], 16)
                pool.wait_ge(par_in, 64)
                pipeline(pool, TT, 2, [(0, affine), (1, store)])
                for s in range(2):
                    pool.wait_ge(x1_out[s], 8 * TT)
                    pool.wait_ge(xn_out[s], 8 * TT)

            @block.scalar
            def _(act):
                for k in range(KD):
                    act.wait_ge(wo_in[k % 2], 16 * (k // 2 + 1))
                    act.copy(wo_hi[:, k, :], wo[k % 2][:]).then_inc(wo_rounded, 1)

                def round_m(q, s):
                    t = 2 * q + s
                    act.wait_ge(t_in[s], 32 * (q + 1))
                    wait(act, mixed, t - 1)
                    act.copy(mt_hi[s][:], mt[s][:]).then_inc(m_rounded, 1)

                def first_root(q, s):
                    act.wait_ge(stats, 2 * q + s + 1)
                    act.activation(sd[s][:], mv[s][:, 1:2], ACT.Sqrt, bias=S.eps[:]).then_inc(root1, 1)

                def second_root(q, s):
                    act.wait_ge(stats2, 2 * q + s + 1)
                    act.activation(sd2[s][:], mv2[s][:, 1:2], ACT.Sqrt, bias=S.eps[:]).then_inc(root2, 1)

                def modulate(q, s):
                    t = 2 * q + s
                    act.wait_ge(turned, t + 1)
                    wait(act, routed, t - 1)
                    for k in range(KD):
                        last = act.activation(hT[s][:, k, :], psT[:, k, :], ACT.Identity,
                                              bias=S.modT[:, SH2 + k:SH2 + k + 1], scale=S.modT[:, SC2 + k:SC2 + k + 1])
                    last.then_inc(modulated, 1)
                pipeline(act, TT, 2, [(0, round_m), (1, first_root), (2, second_root), (3, modulate)])

            @block.tensor
            def _(pe):
                def mix(q, s):
                    t = 2 * q + s
                    pe.wait_ge(m_split, t + 1)
                    wait(pe, gated, t - 1)
                    for half in range(2):
                        cols = slice(half * BANK, (half + 1) * BANK)
                        last = product(pe, psM[s][:, cols], [lambda k, x=x: x[:, k, :] for x in (mt_hi[s], mt_lo[s])],
                                       [lambda k, x=x: x[:, k, cols] for x in (wo_hi, wo_lo)], KD)
                    last.then_inc(mixed, 1)

                def turn(q, s):
                    t = 2 * q + s
                    pe.wait_ge(xn_ready, t + 1)
                    wait(pe, modulated, t)
                    for k in range(KD):
                        last = pe.transpose(psT[:, k, :], xn[s][:, k * P:(k + 1) * P], S.ident[:])
                    last.then_inc(turned, 1)

                def route(q, s):
                    t = 2 * q + s
                    pe.wait_ge(modulated, t + 1)
                    wait(pe, logits, t)
                    for k in range(KD):
                        last = pe.matmul(psL[:, 0:EXPERTS], hT[s][:, k, :], wr[:, k, :], start=(k == 0), stop=(k == KD - 1))
                    last.then_inc(routed, 1)
                pe.wait_ge(wo_split, KD)
                pe.wait_ge(par_in, 64)
                pipeline(pe, TT, 2, [(3, turn), (0, mix), (3, route)])

            @block.vector
            def _(dve):
                for k in range(KD):
                    dve.wait_ge(wo_rounded, k + 1)
                    dve.tensor_tensor(wo_lo[:, k, :], wo[k % 2][:], wo_hi[:, k, :].bitcast(F32), ALU.subtract).then_inc(wo_split, 1)
                dve.wait_ge(par_in, 64)

                def split_m(q, s):
                    dve.wait_ge(m_rounded, 2 * q + s + 1)
                    dve.tensor_tensor(mt_lo[s][:], mt[s][:], mt_hi[s][:].bitcast(F32), ALU.subtract).then_inc(m_split, 1)

                def residual(q, s):
                    t = 2 * q + s
                    dve.wait_ge(mixed, t + 1)
                    wait(dve, x1_ready, t - 1)
                    dve.tensor_tensor(r[s][:], psM[s][:], S.g1[:], ALU.mult).then_inc(gated, 1)
                    dve.wait_ge(gated, t + 1)
                    dve.scalar_tensor_tensor(out=r[s][:], in0=xt[s][:], scalar=DN_ALPHA, in1=r[s][:], op0=ALU.mult,
                                             op1=ALU.add).then_inc(summed, 1)
                    dve.wait_ge(summed, t + 1)
                    for half in range(2):
                        dve.bn_stats(st[s][:, half, :], r[s][:, half * BANK:(half + 1) * BANK]).then_inc(halves, 1)
                    dve.wait_ge(halves, 2 * (t + 1))
                    apart(dve, S)
                    dve.bn_aggr(mv[s][:], st[s][:]).then_inc(stats, 1)

                def normalise(q, s):
                    t = 2 * q + s
                    dve.wait_ge(root1, t + 1)
                    dve.reciprocal(rs[s][:], sd[s][:]).then_inc(inv1, 1)
                    dve.wait_ge(inv1, t + 1)
                    dve.tensor_scalar(r[s][:], r[s][:], mv[s][:, 0:1], rs[s][:], ALU.subtract, ALU.mult).then_inc(normed, 1)

                def second_stats(q, s):
                    t = 2 * q + s
                    dve.wait_ge(x1_ready, t + 1)
                    for half in range(2):
                        dve.bn_stats(st2[s][:, half, :], x1[s][:, half * BANK:(half + 1) * BANK]).then_inc(halves2, 1)
                    dve.wait_ge(halves2, 2 * (t + 1))
                    apart(dve, S)
                    dve.bn_aggr(mv2[s][:], st2[s][:]).then_inc(stats2, 1)

                def second_norm(q, s):
                    t = 2 * q + s
                    dve.wait_ge(root2, t + 1)
                    dve.reciprocal(rs2[s][:], sd2[s][:]).then_inc(inv2, 1)
                    dve.wait_ge(inv2, t + 1)
                    wait(dve, xn_out[s], 16 * q)
                    wait(dve, turned, t - 1)
                    dve.tensor_scalar(xn[s][:], x1[s][:], mv2[s][:, 0:1], rs2[s][:], ALU.subtract, ALU.mult).then_inc(xn_ready, 1)

                def keep_logits(q, s):
                    t = 2 * q + s
                    dve.wait_ge(routed, t + 1)
                    dve.tensor_tensor(S.logits[:, bass.ds(t * EXPERTS, EXPERTS)], psL[:, 0:EXPERTS], br[:], ALU.add).then_inc(logits, 1)
                pipeline(dve, TT, 2, [(0, split_m), (1, residual), (1, normalise), (2, second_stats), (2, second_norm), (4, keep_logits)])
                dve.wait_ge(logits, TT)


def route(nc, A, S, sem, sems):
    with ExitStack() as ctx:
        sb, ps = stack(ctx, nc, "rt")
        E = EXPERTS
        top = sb("top", [P, TT, 8])
        idx = sb("idx", [P, TT, 8], U32)
        idxf = sb("idxf", [P, TT, TOPK])
        iota_e = sb("iota_e", [P, E])
        iota_t = sb("iota_t", [P, MOE_TILES])
        iota_p = sb("iota_p", [P, 1])
        token = sb("token", [P, TT], I32)
        zero_i = sb("zero_i", [P, MOE_TILES], I32)
        hot = sb("hot", [P, TT, TOPK, E])
        chosen = sb("chosen", [P, TT, E])
        strict = sb("strict", [P, P])
        rank = sb("rank", [P, TT, E])
        count = sb("count", [P, TT, E])
        base = sb("base", [P, TT + 1, E])
        cnt_i = sb("cnt_i", [P, E], I32)
        tiles = sb("tiles", [P, E])
        cum = [sb(f"cum{i}", [P, E]) for i in range(2)]
        place = sb("place", [P, TT, E])
        posf = sb("posf", [P, TT, TOPK])
        cmp = sb("cmp", [P, MOE_TILES, E])
        te = sb("te", [P, MOE_TILES])
        same = sb("same", [P, MOE_TILES])
        rowf = sb("rowf", [P, MOE_TILES])
        sums = sb("sums", [P, TT])
        inv = sb("inv", [P, TT])
        psR = ps("rank", [P, TT * E])
        psC = ps("count", [P, TT * E])
        iotas, zeroed, tops, link, chosen_ready, ranked, diffs, exped, placed, cleared, scattered, listed = (
            sem(f"rt_{n}") for n in ("iotas", "zeroed", "tops", "link", "chosen", "ranked", "diffs", "exp", "placed",
                                     "cleared", "scattered", "listed"))

        with nc.Block() as block:
            @block.gpsimd
            def _(pool):
                pool.iota(iota_e[:], [[1, E]], base=0, channel_multiplier=0, allow_small_or_imprecise_dtypes=True).then_inc(iotas, 1)
                pool.iota(iota_t[:], [[1, MOE_TILES]], base=0, channel_multiplier=0, allow_small_or_imprecise_dtypes=True).then_inc(iotas, 1)
                pool.iota(iota_p[:], [[0, 1]], base=0, channel_multiplier=1, allow_small_or_imprecise_dtypes=True).then_inc(iotas, 1)
                pool.iota(token[:], [[P, TT]], base=0, channel_multiplier=1).then_inc(iotas, 1)
                pool.affine_select(out=strict[:], in_=S.ones[:], pattern=[[1, P]], compare_op=ALU.is_gt, fill=0.0,
                                   base=0, channel_multiplier=-1).then_inc(iotas, 1)
                pool.memset(zero_i[:], 0).then_inc(zeroed, 1)
                pool.wait_ge(iotas, 5)
                pool.wait_ge(placed, 1)
                pool.wait_ge(cleared, 16)
                for t in range(TT):
                    for k in range(TOPK):
                        apart(pool, S)
                        pool.indirect_dma_start(S.slot_token_d, bass.IndirectOffsetOnAxis(ap=S.pos[:, t * TOPK + k:t * TOPK + k + 1], axis=0),
                                                token[:, t:t + 1], None).then_inc(scattered, 16)
                pool.wait_ge(scattered, 16 * TT * TOPK)

            @block.sync
            def _(sp):
                sp.wait_ge(zeroed, 1)
                apart(sp, S)
                sp.dma_start(S.slot_token_d.rearrange("(p t) o -> p (t o)", p=P), zero_i[:]).then_inc(cleared, 16)
                sp.wait_ge(scattered, 16 * TT * TOPK)
                with nc.allow_non_contiguous_dma(reason="a table of 48 KB"):
                    apart(sp, S)
                    sp.dma_start(S.slot_token[:], S.slot_token_d.rearrange("(t p) o -> p (t o)", p=P)).then_inc(listed, 16)
                sp.wait_ge(listed, 16)

            @block.tensor
            def _(pe):
                pe.wait_ge(iotas, 5)
                pe.wait_ge(chosen_ready, 1)
                rhs = chosen[:].rearrange("p t e -> p (t e)")
                pe.matmul(psR[:], strict[:], rhs, start=True, stop=True)
                pe.matmul(psC[:], S.ones[:], rhs, start=True, stop=True).then_inc(ranked, 1)

            @block.scalar
            def _(act):
                act.wait_ge(diffs, 1)
                act.activation(S.probs[:], S.probs[:], ACT.Exp).then_inc(exped, 1)

            @block.vector
            def _(dve):
                for t in range(TT):
                    dve.max(top[:, t, :], S.logits[:, t * E:(t + 1) * E]).then_inc(tops, 1)
                dve.wait_ge(tops, TT)
                for t in range(TT):
                    dve.max_index(idx[:, t, :], top[:, t, :], S.logits[:, t * E:(t + 1) * E]).then_inc(tops, 1)
                chain = Chain(dve, link)
                probs = S.probs[:].rearrange("p (t k) -> p t k", k=TOPK)
                dve.tensor_tensor(probs, top[:, :, 0:TOPK], top[:, :, 0:1].to_broadcast([P, TT, TOPK]), ALU.subtract).then_inc(diffs, 1)
                dve.wait_ge(tops, 2 * TT)
                dve.wait_ge(iotas, 5)
                chain.step(dve.tensor_copy(idxf[:], idx[:, :, 0:TOPK]))
                hot3 = hot[:].rearrange("p t k e -> p (t k) e")
                chain.step(dve.tensor_tensor(hot3, idxf[:].rearrange("p t k -> p (t k)").unsqueeze(2).to_broadcast([P, TT * TOPK, E]),
                                             iota_e[:].unsqueeze(1).to_broadcast([P, TT * TOPK, E]), ALU.is_equal))
                dve.tensor_reduce(chosen[:], hot[:].rearrange("p t k e -> p t e k"), AX.X, ALU.add).then_inc(chosen_ready, 1)
                dve.wait_ge(exped, 1)
                chain.step(dve.tensor_reduce(sums[:], probs, AX.X, ALU.add))
                chain.step(dve.reciprocal(inv[:], sums[:]))
                chain.step(dve.tensor_tensor(probs, probs, inv[:].unsqueeze(2).to_broadcast([P, TT, TOPK]), ALU.mult))
                dve.wait_ge(ranked, 1)
                chain.step(dve.tensor_copy(rank[:].rearrange("p t e -> p (t e)"), psR[:]))
                chain.step(dve.tensor_copy(count[:].rearrange("p t e -> p (t e)"), psC[:]))
                chain.step(dve.memset(base[:, 0, :], 0.0))
                for t in range(TT):
                    chain.step(dve.tensor_tensor(base[:, t + 1, :], base[:, t, :], count[:, t, :], ALU.add))
                chain.step(dve.tensor_scalar(cum[0][:], base[:, TT, :], float(P - 1), None, ALU.add))
                chain.step(dve.tensor_copy(cnt_i[:], cum[0][:]))
                chain.step(dve.tensor_scalar(cnt_i[:], cnt_i[:], 7, None, ALU.arith_shift_right))
                chain.step(dve.tensor_copy(tiles[:], cnt_i[:]))
                chain.step(dve.tensor_copy(cum[0][:], tiles[:]))
                a = 0
                for shift in (1, 2, 4, 8, 16):
                    chain.step(dve.tensor_copy(cum[1 - a][:, 0:shift], cum[a][:, 0:shift]))
                    chain.step(dve.tensor_tensor(cum[1 - a][:, shift:], cum[a][:, shift:], cum[a][:, :E - shift], ALU.add))
                    a = 1 - a
                chain.step(dve.tensor_tensor(tiles[:], cum[a][:], tiles[:], ALU.subtract))
                chain.step(dve.tensor_scalar(tiles[:], tiles[:], float(P), None, ALU.mult))
                chain.step(dve.tensor_tensor(place[:], rank[:], base[:, 0:TT, :], ALU.add))
                chain.step(dve.tensor_tensor(place[:], place[:], tiles[:].unsqueeze(1).to_broadcast([P, TT, E]), ALU.add))
                for k in range(TOPK):
                    chain.step(dve.tensor_tensor(hot[:, :, k, :], hot[:, :, k, :], place[:], ALU.mult))
                chain.step(dve.tensor_reduce(posf[:], hot[:], AX.X, ALU.add))
                dve.tensor_copy(S.pos[:], posf[:].rearrange("p t k -> p (t k)")).then_inc(placed, 1)
                chain.step(dve.tensor_tensor(cmp[:], iota_t[:].unsqueeze(2).to_broadcast([P, MOE_TILES, E]),
                                             cum[a][:].unsqueeze(1).to_broadcast([P, MOE_TILES, E]), ALU.is_ge))
                chain.step(dve.tensor_reduce(te[:], cmp[:], AX.X, ALU.add))
                chain.step(dve.tensor_scalar(te[:], te[:], float(E - 1), None, ALU.min))
                chain.step(dve.memset(same[:, 0:1], 0.0))
                chain.step(dve.tensor_tensor(same[:, 1:], te[:, 1:], te[:, :MOE_TILES - 1], ALU.is_equal))
                chain.step(dve.tensor_scalar(same[:], same[:], SKIP, None, ALU.mult))
                chain.step(dve.tensor_tensor(rowf[:], te[:], same[:], ALU.add))
                chain.step(dve.tensor_copy(S.expert_row[:], rowf[:]))
                chain.step(dve.scalar_tensor_tensor(out=rowf[:], in0=te[:], scalar=float(D), in1=same[:], op0=ALU.mult, op1=ALU.add))
                chain.step(dve.tensor_scalar(rowf[:], rowf[:], iota_p[:], None, ALU.add))
                chain.step(dve.tensor_copy(S.weight_row[:], rowf[:]))
                dve.wait_ge(placed, 1)


def experts(nc, A, S, sem, sems):
    with ExitStack() as ctx:
        sb, ps = stack(ctx, nc, "moe")
        F2 = 2 * FF
        KF = FF // P

        def pair(name, shape, dt=F32):
            return [sb(f"{name}{i}", shape, dt) for i in range(2)]
        w_gu = [sb(f"w_gu{k}", [P, F2]) for k in range(KD)]
        w_dn = [sb(f"w_dn{k}", [P, D]) for k in range(KF)]
        b_gu = sb("b_gu", [P, F2])
        b_dn = sb("b_dn", [P, D])
        xs, hT = pair("xs", [P, D]), pair("hT", [P, KD, P])
        gate, up, sig, av = sb("gate", [P, FF]), sb("up", [P, FF]), sb("sig", [P, FF]), sb("act", [P, FF])
        aT = sb("aT", [P, KF, P])
        os_ = pair("out", [P, D])
        tok_i, gu_i, gue_i, dn_i, dne_i = (pair(n, [P, 1], I32) for n in ("tok_i", "gu_i", "gue_i", "dn_i", "dne_i"))
        psG = ps("gu", [P, F2])
        psD = ps("down", [P, D])
        psT = ps("t", [P, KD, P])
        x_in, stored = sems("moe_x", 2), sems("moe_stored", 2)
        gu_in, dn_in = sems("moe_gu_in", KD), sems("moe_dn_in", KF)
        bgu_in, bdn_in, picked, picked_gu, picked_dn, gu_used, dn_used, h_turned, h_ready, g_added, u_added, g_cut, u_cut, \
            gated, sig_done, act_ready, a_turned, a_ready, out_ready = (sem(f"moe_{n}") for n in (
                "bgu_in", "bdn_in", "picked", "picked_gu", "picked_dn", "gu_used", "dn_used", "h_turned", "h_ready",
                "g_added", "u_added", "g_cut", "u_cut", "gated", "sig", "act", "a_turned", "a_ready", "out"))

        with nc.Block() as block:
            @block.gpsimd
            def _(pool):
                def fetch_tokens(q, s):
                    i = 2 * q + s
                    wait(pool, h_turned, i - 1)
                    apart(pool, S)
                    pool.tensor_copy(tok_i[s][:], S.slot_token[:, bass.ds(i, 1)]).then_inc(picked, 1)
                    pool.wait_ge(picked, i + 1)
                    apart(pool, S)
                    pool.indirect_dma_start(xs[s][:], None, S.xn2_d, bass.IndirectOffsetOnAxis(ap=tok_i[s][:], axis=0)).then_inc(x_in[s], 16)

                def fetch(q, s, picks, idx, rows, chunks, used, landed, table, b_idx, bias, b_used, b_landed, b_table):
                    i = 2 * q + s
                    wait(pool, used, len(chunks) * (i - 1))
                    apart(pool, S)
                    pool.tensor_copy(idx[s][:], S.weight_row[:, bass.ds(i, 1)]).then_inc(picks, 1)
                    pool.wait_ge(picks, 2 * i + 1)
                    wait(pool, b_landed, 16 * (i - 1))
                    apart(pool, S)
                    pool.tensor_copy(b_idx[s][:], S.expert_row[:, bass.ds(i, 1)]).then_inc(picks, 1)
                    pool.wait_ge(picks, 2 * i + 2)
                    for k, chunk in enumerate(chunks):
                        wait(pool, used, len(chunks) * (i - 1) + k + 1)
                        wait(pool, landed[k], 16 * i)
                        apart(pool, S)
                        pool.indirect_dma_start(chunk[:], None, table, bass.IndirectOffsetOnAxis(ap=idx[s][:], axis=0),
                                                element_offset=k * P * rows, bounds_check=EXPERTS * D - 1,
                                                oob_is_err=False).then_inc(landed[k], 16)
                    wait(pool, b_used, i)
                    wait(pool, b_landed, 16 * i)
                    apart(pool, S)
                    pool.indirect_dma_start(bias[:], None, b_table, bass.IndirectOffsetOnAxis(ap=b_idx[s][:], axis=0),
                                            bounds_check=EXPERTS - 1, oob_is_err=False).then_inc(b_landed, 16)

                def fetch_gu(q, s):
                    fetch(q, s, picked_gu, gu_i, F2, w_gu, gu_used, gu_in, A["w_gu"], gue_i, b_gu, u_added, bgu_in, A["b_gu"])

                def fetch_dn(q, s):
                    fetch(q, s, picked_dn, dn_i, D, w_dn, dn_used, dn_in, A["w_down"], dne_i, b_dn, out_ready, bdn_in, A["b_down"])
                pipeline(pool, MOE_TILES, 2, [(0, fetch_tokens), (1, fetch_gu), (2, fetch_dn)])

            @block.tensor
            def _(pe):
                def turn_act(q, s):
                    i = 2 * q + s
                    pe.wait_ge(act_ready, i + 1)
                    wait(pe, h_ready, i + 2 if not isinstance(i, int) else min(i + 2, MOE_TILES))
                    for k in range(KF):
                        last = pe.transpose(psT[:, k, :], av[:, k * P:(k + 1) * P], S.ident[:])
                    last.then_inc(a_turned, 1)

                def gate_up(q, s):
                    i = 2 * q + s
                    pe.wait_ge(h_ready, i + 1)
                    wait(pe, u_added, i)
                    for k in range(KD):
                        pe.wait_ge(gu_in[k], 16 * (i + 1))
                        for b in range(F2 // BANK):
                            last = pe.matmul(psG[:, b * BANK:(b + 1) * BANK], hT[s][:, k, :],
                                             w_gu[k][:, b * BANK:(b + 1) * BANK], start=(k == 0), stop=(k == KD - 1))
                        last.then_inc(gu_used, 1)

                def turn_h(q, s):
                    i = 2 * q + s
                    pe.wait_ge(x_in[s], 16 * (q + 1))
                    wait(pe, a_ready, i - 1)
                    for k in range(KD):
                        last = pe.transpose(psT[:, k, :], xs[s][:, k * P:(k + 1) * P], S.ident[:])
                    last.then_inc(h_turned, 1)

                def down(q, s):
                    i = 2 * q + s
                    pe.wait_ge(a_ready, i + 1)
                    wait(pe, out_ready, i)
                    for k in range(KF):
                        pe.wait_ge(dn_in[k], 16 * (i + 1))
                        for b in range(D // BANK):
                            last = pe.matmul(psD[:, b * BANK:(b + 1) * BANK], aT[:, k, :],
                                             w_dn[k][:, b * BANK:(b + 1) * BANK], start=(k == 0), stop=(k == KF - 1))
                        last.then_inc(dn_used, 1)

                pipeline(pe, MOE_TILES, 2, [(3, turn_act), (2, gate_up), (1, turn_h), (3, down)])

            @block.scalar
            def _(act):
                def keep_act(q, s):
                    i = 2 * q + s
                    act.wait_ge(a_turned, i + 1)
                    wait(act, dn_used, KF * i)
                    act.copy(aT[:], psT[:]).then_inc(a_ready, 1)

                def modulate(q, s):
                    i = 2 * q + s
                    act.wait_ge(h_turned, i + 1)
                    wait(act, gu_used, KD * (i - 1))
                    for k in range(KD):
                        last = act.activation(hT[s][:, k, :], psT[:, k, :], ACT.Identity,
                                              bias=S.modT[:, SH2 + k:SH2 + k + 1], scale=S.modT[:, SC2 + k:SC2 + k + 1])
                    last.then_inc(h_ready, 1)

                def sigmoid(q, s):
                    i = 2 * q + s
                    act.wait_ge(g_cut, i + 1)
                    wait(act, act_ready, i)
                    act.activation(sig[:], gate[:], ACT.Sigmoid, scale=SWIGLU_ALPHA).then_inc(sig_done, 1)
                pipeline(act, MOE_TILES, 2, [(3, keep_act), (1, modulate), (2, sigmoid)])

            @block.vector
            def _(dve):
                def swiglu(q, s):
                    i = 2 * q + s
                    dve.wait_ge(gu_used, KD * (i + 1))
                    dve.wait_ge(bgu_in, 16 * (i + 1))
                    dve.tensor_tensor(gate[:], psG[:, 0:FF], b_gu[:, 0:FF], ALU.add).then_inc(g_added, 1)
                    dve.tensor_tensor(up[:], psG[:, FF:F2], b_gu[:, FF:F2], ALU.add).then_inc(u_added, 1)
                    dve.wait_ge(g_added, i + 1)
                    dve.tensor_scalar(gate[:], gate[:], LIMIT, None, ALU.min).then_inc(g_cut, 1)
                    dve.wait_ge(u_added, i + 1)
                    dve.tensor_scalar(up[:], up[:], LIMIT, -LIMIT, ALU.min, ALU.max).then_inc(u_cut, 1)
                    dve.wait_ge(g_cut, i + 1)
                    dve.wait_ge(u_cut, i + 1)
                    dve.scalar_tensor_tensor(out=up[:], in0=up[:], scalar=1.0, in1=gate[:], op0=ALU.add, op1=ALU.mult).then_inc(gated, 1)
                    dve.wait_ge(gated, i + 1)
                    dve.wait_ge(sig_done, i + 1)
                    wait(dve, a_turned, i)
                    dve.tensor_tensor(av[:], up[:], sig[:], ALU.mult).then_inc(act_ready, 1)

                def finish(q, s):
                    i = 2 * q + s
                    dve.wait_ge(dn_used, KF * (i + 1))
                    dve.wait_ge(bdn_in, 16 * (i + 1))
                    wait(dve, stored[s], 16 * q)
                    dve.tensor_tensor(os_[s][:], psD[:], b_dn[:], ALU.add).then_inc(out_ready, 1)
                pipeline(dve, MOE_TILES, 2, [(2, swiglu), (3, finish)])

            @block.sync
            def _(sp):
                def store(q, s):
                    i = 2 * q + s
                    sp.wait_ge(out_ready, i + 1)
                    apart(sp, S)
                    sp.dma_start(S.slot_out_d[bass.ds(i * P, P), :], os_[s][:]).then_inc(stored[s], 16)
                pipeline(sp, MOE_TILES, 2, [(0, store)])
                for s in range(2):
                    sp.wait_ge(stored[s], 8 * MOE_TILES)


def combine(nc, A, S, sem, sems, out):
    with ExitStack() as ctx:
        sb, _ = stack(ctx, nc, "fin")

        def pair(name, shape, dt=F32):
            return [sb(f"{name}{i}", shape, dt) for i in range(2)]
        rows = [pair(f"rows{k}_", [P, D]) for k in range(TOPK)]
        idx = pair("idx", [P, TOPK], I32)
        x1, acc, yo = pair("x1", [P, D]), pair("acc", [P, D]), pair("y", [P, D])
        st, mv, sd, rs = pair("st", [P, 2, 6]), pair("mv", [P, 2]), pair("sd", [P, 1]), pair("rs", [P, 1])
        lg, lb = sb("ln_g", [P, D]), sb("ln_b", [P, D])
        par_in, picked, link, stats, root, normed, scaled, ready = (sem(f"fin_{n}") for n in (
            "params", "picked", "link", "stats", "root", "normed", "scaled", "ready"))
        rows_in, x1_in, stored = sems("fin_rows", 2), sems("fin_x1", 2), sems("fin_stored", 2)
        STEPS = 8

        with nc.Block() as block:
            @block.gpsimd
            def _(pool):
                def gather(q, s):
                    t = 2 * q + s
                    wait(pool, stats, t - 1)
                    apart(pool, S)
                    pool.tensor_copy(idx[s][:], S.pos[:, bass.ds(t * TOPK, TOPK)]).then_inc(picked, 1)
                    pool.wait_ge(picked, t + 1)
                    for k in range(TOPK):
                        apart(pool, S)
                        pool.indirect_dma_start(rows[k][s][:], None, S.slot_out_d,
                                                bass.IndirectOffsetOnAxis(ap=idx[s][:, k:k + 1], axis=0)).then_inc(rows_in[s], 16)

                def affine(q, s):
                    t = 2 * q + s
                    pool.wait_ge(normed, t + 1)
                    wait(pool, stored[s], 16 * q)
                    pool.tensor_tensor(yo[s][:], acc[s][:], lg[:], ALU.mult).then_inc(scaled, 1)
                    pool.wait_ge(scaled, t + 1)
                    pool.tensor_tensor(yo[s][:], yo[s][:], lb[:], ALU.add).then_inc(ready, 1)
                pool.wait_ge(par_in, 32)
                pipeline(pool, TT, 2, [(0, gather), (1, affine)])

            @block.sync
            def _(sp):
                apart(sp, S)
                for dst, name in ((lg, "ln2_g"), (lb, "ln2_b")):
                    sp.dma_start(dst[:], A[name][0].partition_broadcast(P)).then_inc(par_in, 16)

                def load(q, s):
                    t = 2 * q + s
                    wait(sp, stats, t - 1)
                    apart(sp, S)
                    sp.dma_start(x1[s][:], S.x1_d[bass.ds(t * P, P), :]).then_inc(x1_in[s], 16)

                def store(q, s):
                    t = 2 * q + s
                    sp.wait_ge(ready, t + 1)
                    apart(sp, S)
                    sp.dma_start(out[bass.ds(t * P, P), :], yo[s][:]).then_inc(stored[s], 16)
                pipeline(sp, TT, 2, [(0, load), (2, store)])
                for s in range(2):
                    sp.wait_ge(stored[s], 8 * TT)

            @block.scalar
            def _(act):
                def first_root(q, s):
                    act.wait_ge(stats, 2 * q + s + 1)
                    act.activation(sd[s][:], mv[s][:, 1:2], ACT.Sqrt, bias=S.eps[:]).then_inc(root, 1)
                pipeline(act, TT, 2, [(0, first_root)])

            @block.vector
            def _(dve):
                chain = Chain(dve, link)

                def blend(q, s):
                    t = 2 * q + s
                    chain.item(t, STEPS)
                    dve.wait_ge(rows_in[s], 16 * TOPK * (q + 1))
                    wait(dve, ready, t - 1)
                    chain.step(dve.tensor_scalar(acc[s][:], rows[0][s][:], S.probs[:, bass.ds(t * TOPK, 1)], None, ALU.mult))
                    for k in range(1, TOPK):
                        chain.step(dve.scalar_tensor_tensor(out=acc[s][:], in0=rows[k][s][:], scalar=S.probs[:, bass.ds(t * TOPK + k, 1)],
                                                            in1=acc[s][:], op0=ALU.mult, op1=ALU.add))
                    chain.step(dve.tensor_tensor(acc[s][:], acc[s][:], S.g2[:], ALU.mult))
                    dve.wait_ge(x1_in[s], 16 * (q + 1))
                    chain.step(dve.scalar_tensor_tensor(out=acc[s][:], in0=x1[s][:], scalar=DN_ALPHA, in1=acc[s][:], op0=ALU.mult, op1=ALU.add))
                    dve.bn_stats(st[s][:, 0, :], acc[s][:, 0:BANK])
                    chain.step(dve.bn_stats(st[s][:, 1, :], acc[s][:, BANK:D]))
                    apart(dve, S)
                    dve.bn_aggr(mv[s][:], st[s][:]).then_inc(stats, 1)
                    dve.wait_ge(root, t + 1)
                    chain.step(dve.reciprocal(rs[s][:], sd[s][:]))
                    dve.tensor_scalar(acc[s][:], acc[s][:], mv[s][:, 0:1], rs[s][:], ALU.subtract, ALU.mult).then_inc(normed, 1)
                    chain.end()
                pipeline(dve, TT, 2, [(0, blend)])


def build(nc, A, out):
    with ExitStack() as top:
        in_use = []

        def sem(name):
            in_use.append(nc.alloc_semaphore(name=name))
            return in_use[-1]

        def release_semaphores():
            nc.clear_and_free_semaphores(in_use)
            in_use.clear()
            nc.all_engine_barrier()

        def sems(name, n):
            return [sem(f"{name}{i}") for i in range(n)]

        def dram(name, shape, dt=F32):
            return nc.dram_tensor(name, shape, dt).ap()

        S = Shared()
        S.passed = nc.alloc_semaphore(name="passed")
        S.rows_d = dram("rows_scratch", (N_ROWS * P, SEQ))
        S.acum_d = dram("acum_scratch", (HEADS, SEQ))
        S.y_d = dram("y_scratch", (INNER, SEQ))
        S.mixin_d = dram("mixin_scratch", (D, SEQ))
        S.x1_d = dram("x1_scratch", (SEQ, D))
        S.xn2_d = dram("xn2_scratch", (SEQ, D))
        S.slot_token_d = dram("slot_token_scratch", (SLOTS, 1), I32)
        S.slot_out_d = dram("slot_out_scratch", (SLOTS, D))

        sb, _ = stack(top, nc, "keep")
        S.ident = sb("ident", [P, P])
        S.tri = sb("tri", [P, P])
        S.ones = sb("ones", [P, P])
        S.eps = sb("eps", [P, 1])
        S.modT = sb("modT", [P, 6 * KD])
        S.g1 = sb("g1", [P, D])
        S.g2 = sb("g2", [P, D])
        S.logits = sb("logits", [P, TT * EXPERTS])
        S.probs = sb("probs", [P, TT * TOPK])
        S.pos = sb("pos", [P, TT * TOPK], I32)
        S.slot_token = sb("slot_token", [P, MOE_TILES], I32)
        S.weight_row = sb("weight_row", [P, MOE_TILES], I32)
        S.expert_row = sb("expert_row", [P, MOE_TILES], I32)

        modulation(nc, A, S, sem, sems)
        with ExitStack() as ctx:
            sb, _ = stack(ctx, nc, "table")
            S.dt = sb("dt", [P, TT * HEADS])
            S.acum = sb("acum", [P, TT * HEADS])
            S.decay = sb("decay", [P, TT * HEADS])
            S.chunk_decay = sb("chunk_decay", [P, TT * HEADS])
            with ExitStack() as hctx:
                sb, _ = stack(hctx, nc, "h")
                h_hi = sb("hi", [P, KD, SEQ], F32R)
                h_lo = sb("lo", [P, KD, SEQ], F32R)
                norm_in(nc, A, S, sem, sems, h_hi, h_lo)
                decay(nc, A, S, sem, sems, h_hi, h_lo)
                project(nc, A, S, sem, sems, h_hi, h_lo)
            ssd(nc, A, S, sem, sems)
        release_semaphores()
        branches(nc, A, S, sem, sems)
        mix_out(nc, A, S, sem, sems)
        route(nc, A, S, sem, sems)
        experts(nc, A, S, sem, sems)
        combine(nc, A, S, sem, sems, out)
        in_use.append(S.passed)
        release_semaphores()


def layouts(i):
    import numpy as np
    z1 = INNER
    s1 = z1 + N_XBC * P
    s2 = s1 + HEADS
    w_in = i["w_in"][0]
    cols = [w_in[:, 0:s1]]
    short = w_in[:, s2:s2 + 3 * D].reshape(D, 3, N_SC, P)[:, [1, 2, 0]]
    cols.append(short.transpose(0, 2, 1, 3).reshape(D, 3 * D))
    cols.append(w_in[:, s2 + 3 * D:])
    w_main = np.concatenate(cols, axis=1)

    def col_tiles(w, width=P):
        rows, n = w.shape
        return w.reshape(rows // P, P, n // width, width).transpose(2, 1, 0, 3).reshape(n // width * P, rows // P * width)

    def columns(v):
        return v.reshape(-1, P).T
    return {
        "x": i["x"][0],
        "cT": columns(i["c"][0]),
        "w_ada_t": col_tiles(i["w_ada"][0], BANK).reshape(6 * D // BANK, P, KD * BANK),
        "b_adaT": columns(i["b_ada"][0]),
        "b_ada": i["b_ada"],
        "w_in_t": col_tiles(w_main),
        "w_dt": col_tiles(w_in[:, s1:s2], HEADS),
        "conv_w": i["conv_ssd_w"][0].reshape(CONV, N_XBC, P).transpose(2, 1, 0).reshape(P, N_XBC * CONV),
        "conv_b": columns(i["conv_ssd_b"][0]),
        "short_w": i["conv_short_w"][0].reshape(SCONV, N_SC, P).transpose(2, 1, 0).reshape(P, N_SC * SCONV),
        "b_gateT": columns(i["b_gate"][0]),
        "dt_bias": i["dt_bias"],
        "a_log": i["a_log"],
        "d_skipT": columns(np.repeat(i["d_skip"][0], HD)),
        "ssd_norm_wT": columns(i["ssd_norm_w"][0]),
        "w_branch_t": col_tiles(np.concatenate([i["w_ssd_out"][0], i["w_short_out"][0]], axis=0)),
        "w_o": i["w_o"][0],
        "ln1_g": i["ln1_g"], "ln1_b": i["ln1_b"],
        "w_router_t": col_tiles(i["w_router"][0], EXPERTS),
        "b_router": i["b_router"],
        "w_gu": i["w_gu"][0].reshape(EXPERTS * D, 2 * FF),
        "b_gu": i["b_gu"][0],
        "w_down": i["w_down"][0].reshape(EXPERTS * FF, D),
        "b_down": i["b_down"][0],
        "ln2_g": i["ln2_g"], "ln2_b": i["ln2_b"],
    }


def kernel(**inputs):
    import numpy as np
    from concourse import bacc
    from concourse.bass_utils import run_bass_kernel_spmd

    nc = bacc.Bacc("TRN2", target_bir_lowering=False, num_devices=1)
    arrays, A = {}, {}
    for name, a in layouts({k: np.asarray(v) for k, v in inputs.items()}).items():
        a = np.ascontiguousarray(a)
        arrays[f"in_{name}"] = a
        A[name] = nc.dram_tensor(f"in_{name}", a.shape, mybir.dt.from_np(a.dtype), kind="ExternalInput").ap()
    out = nc.dram_tensor("out_x", (SEQ, D), F32, kind="ExternalOutput").ap()
    build(nc, A, out)
    r = run_bass_kernel_spmd(nc, [arrays], core_ids=[0])
    return r.results[0]["out_x"].reshape(1, SEQ, D)
```

```python
from contextlib import ExitStack

import concourse.bass as bass
from concourse import mybir

F32 = mybir.dt.float32
F32R = mybir.dt.float32r
I32 = mybir.dt.int32
U32 = mybir.dt.uint32
ALU = mybir.AluOpType
ACT = mybir.ActivationFunctionType
AX = mybir.AxisListType

P = 128
D = 1024
SEQ = 2048
KD = D // P
TT = SEQ // P
INNER = 2 * D
HEADS = 32
HD = 64
GROUPS = 4
HG = HEADS // GROUPS
NSTATE = 128
CONV = 4
SCONV = 3
EXPERTS = 32
TOPK = 4
FF = D
LIMIT = 7.0
SWIGLU_ALPHA = 1.702
DN_ALPHA = 2.0 ** 0.25
EPS = 1e-5
BANK = 512

N_Z = INNER // P
N_XBC = (INNER + 2 * GROUPS * NSTATE) // P
N_SC = D // P
N_GATE = 2 * D // P
N_PROJ = N_Z + N_XBC + 3 * N_SC + N_GATE
ROW_Z = 0
ROW_XBC = N_Z
ROW_Q = ROW_XBC + N_XBC
ROW_GATE = ROW_Q + N_SC
N_ROWS = ROW_GATE + N_GATE

MOE_TILES = SEQ * TOPK // P + EXPERTS
MOE_ROUNDS = (MOE_TILES + 4) // 2
MOE_COLS = 2 * MOE_ROUNDS
SLOTS = MOE_COLS * P
GU_ROWS = D * 2 * FF // 4096
DN_ROWS = FF * D // 4096
SKIP = float(1 << 20)
SH1, SC1, SH2, SC2 = 0, KD, 3 * KD, 4 * KD


class Shared:
    pass


def wait(eng, sem, value):
    if isinstance(value, int) and value <= 0:
        return
    eng.wait_ge(sem, value)


def apart(eng, S):
    eng.sem_inc(S.passed, 1)


def pipeline(eng, n, unroll, stages):
    most = max(lag for lag, _ in stages)
    rounds = -(-(n + most) // unroll)
    lead = -(-most // unroll) + 1
    full = n // unroll

    def one(r):
        for s in range(unroll):
            for lag, fn in stages:
                q, slot = (s - lag) // unroll, (s - lag) % unroll
                if isinstance(r, int) and not 0 <= (r + q) * unroll + slot < n:
                    continue
                fn(r + q, slot)

    if full - lead < 2:
        for r in range(rounds):
            one(r)
        return
    for r in range(lead):
        one(r)
    with eng.Fori(lead, full) as r:
        one(r)
    for r in range(full, rounds):
        one(r)


class Chain:

    def __init__(self, eng, sem):
        self.eng, self.sem, self.n, self.k = eng, sem, 0, 0

    def item(self, i, per_item):
        self.n, self.k, self.per = i * per_item, 0, per_item

    def step(self, ins):
        self.k += 1
        ins.then_inc(self.sem, 1)
        self.eng.wait_ge(self.sem, self.n + self.k)

    def end(self):
        assert self.k == self.per, (self.k, self.per)



def stack(ctx, nc, phase):
    def sb(name, shape, dt=F32):
        return ctx.enter_context(nc.sbuf_tensor(f"{phase}_{name}", shape, dt))

    def ps(name, shape, dt=F32):
        return ctx.enter_context(nc.psum_tensor(f"{phase}_ps_{name}", shape, dt))
    return sb, ps


def product(pe, out, lhs, rhs, steps):
    parts = ((0, 0), (0, 1), (1, 0))
    for k in range(steps):
        for n, (a, b) in enumerate(parts):
            last = pe.matmul(out, lhs[a](k), rhs[b](k), start=(k == 0 and n == 0), stop=(k == steps - 1 and n == 2))
    return last


def modulation(nc, A, S, sem, sems):
    with ExitStack() as ctx:
        sb, ps = stack(ctx, nc, "mod")
        NB = 6 * D // BANK
        cT = sb("cT", [P, KD])
        sc = sb("silu_c", [P, KD])
        sc_rep = sb("silu_c_rep", [P, KD, P])
        bT = sb("bT", [P, 6 * KD])
        wa = [sb(f"w{i}", [P, KD, BANK]) for i in range(3)]
        psT = ps("cols", [P, BANK])
        psG = [ps(f"gate{i}", [P, BANK]) for i in range(4)]
        small_in, consts, silu_done, rep_done = sem("mod_small_in"), sem("mod_consts"), sem("mod_silu"), sem("mod_rep")
        w_in = sems("mod_w", 3)
        w_used, bias_added = sem("mod_w_used"), sem("mod_bias")
        gate_of = {4: 0, 5: 1, 10: 2, 11: 3}

        with nc.Block() as block:
            @block.sync
            def _(sp):
                sp.dma_start(cT[:], A["cT"]).then_inc(small_in, 16)
                sp.dma_start(bT[:], A["b_adaT"]).then_inc(small_in, 16)
                sp.dma_start(S.g1[:], A["b_ada"][0, 2 * D:3 * D].partition_broadcast(P)).then_inc(small_in, 16)
                sp.dma_start(S.g2[:], A["b_ada"][0, 5 * D:6 * D].partition_broadcast(P)).then_inc(small_in, 16)
                for b in range(NB):
                    wait(sp, w_used, b - 2)
                    apart(sp, S)
                    sp.dma_start(wa[b % 3][:], A["w_ada_t"][b].rearrange("p (k n) -> p k n", k=KD)).then_inc(w_in[b % 3], 16)

            @block.gpsimd
            def _(pool):
                pool.memset(S.ones[:], 1.0).then_inc(consts, 1)
                pool.memset(S.eps[:], EPS).then_inc(consts, 1)
                pool.wait_ge(consts, 2)
                pool.affine_select(out=S.tri[:], in_=S.ones[:], pattern=[[1, P]], compare_op=ALU.is_ge, fill=0.0,
                                   base=0, channel_multiplier=-1).then_inc(consts, 1)
                pool.affine_select(out=S.ident[:], in_=S.ones[:], pattern=[[1, P]], compare_op=ALU.is_equal, fill=0.0,
                                   base=0, channel_multiplier=-1).then_inc(consts, 1)
                pool.wait_ge(consts, 4)

            @block.scalar
            def _(act):
                act.wait_ge(small_in, 64)
                act.activation(sc[:], cT[:], ACT.Silu).then_inc(silu_done, 1)

            @block.tensor
            def _(pe):
                pe.wait_ge(silu_done, 1)
                pe.wait_ge(rep_done, 1)
                for b in range(NB):
                    pe.wait_ge(w_in[b % 3], 16 * (b // 3 + 1))
                    if b in gate_of:
                        for k in range(KD):
                            last = pe.matmul(psG[gate_of[b]][:], sc_rep[:, k, :], wa[b % 3][:, k, :],
                                             start=(k == 0), stop=(k == KD - 1))
                    else:
                        for j in range(BANK // P):
                            col = b * (BANK // P) + j
                            for k in range(KD):
                                last = pe.matmul(psT[:, col:col + 1], wa[b % 3][:, k, j * P:(j + 1) * P],
                                                 sc[:, k:k + 1], start=(k == 0), stop=(k == KD - 1))
                    last.then_inc(w_used, 1)

            @block.vector
            def _(dve):
                dve.wait_ge(silu_done, 1)
                dve.tensor_copy(sc_rep[:], sc[:].unsqueeze(2).to_broadcast([P, KD, P])).then_inc(rep_done, 1)
                dve.wait_ge(small_in, 64)
                dve.wait_ge(w_used, NB)
                for first in (SH1, SH2):
                    dve.tensor_tensor(S.modT[:, first:first + KD], psT[:, first:first + KD],
                                      bT[:, first:first + KD], ALU.add).then_inc(bias_added, 1)
                for first in (SC1, SC2):
                    dve.scalar_tensor_tensor(out=S.modT[:, first:first + KD], in0=psT[:, first:first + KD], scalar=1.0,
                                             in1=bT[:, first:first + KD], op0=ALU.add, op1=ALU.add).then_inc(bias_added, 1)
                for i, row in enumerate((S.g1, S.g1, S.g2, S.g2)):
                    half = slice(i % 2 * BANK, (i % 2 + 1) * BANK)
                    dve.tensor_tensor(row[:, half], psG[i][:], row[:, half], ALU.add).then_inc(bias_added, 1)
                dve.wait_ge(bias_added, 8)


def norm_in(nc, A, S, sem, sems, h_hi, h_lo):
    with ExitStack() as ctx:
        sb, ps = stack(ctx, nc, "nin")
        xt = [sb(f"x{i}", [P, D]) for i in range(2)]
        xn = [sb(f"xn{i}", [P, D]) for i in range(2)]
        st = [sb(f"st{i}", [P, 2, 6]) for i in range(2)]
        mv = [sb(f"mv{i}", [P, 2]) for i in range(2)]
        sd = [sb(f"sd{i}", [P, 1]) for i in range(2)]
        rs = [sb(f"rs{i}", [P, 1]) for i in range(2)]
        ht = [sb(f"h{i}", [P, KD, P]) for i in range(2)]
        psT = [ps(f"t{i}", [P, KD, P]) for i in range(2)]
        x_in = sems("nin_x", 2)
        halves, stats, sqrt_done, inverse, normed, transposed, modulated, rounded, split = (
            sem("nin_halves"), sem("nin_stats"), sem("nin_sqrt"), sem("nin_inverse"), sem("nin_normed"),
            sem("nin_transposed"), sem("nin_modulated"), sem("nin_rounded"), sem("nin_split"))

        with nc.Block() as block:
            @block.sync
            def _(sp):
                def load(q, s):
                    wait(sp, normed, 2 * q + s - 1)
                    apart(sp, S)
                    sp.dma_start(xt[s][:], A["x"][bass.ds((2 * q + s) * P, P), :]).then_inc(x_in[s], 16)
                pipeline(sp, TT, 2, [(0, load)])

            @block.vector
            def _(dve):
                def norm(q, s):
                    t = 2 * q + s
                    dve.wait_ge(x_in[s], 16 * (q + 1))
                    for half in range(2):
                        dve.bn_stats(st[s][:, half, :], xt[s][:, half * BANK:(half + 1) * BANK]).then_inc(halves, 1)
                    dve.wait_ge(halves, 2 * (t + 1))
                    apart(dve, S)
                    dve.bn_aggr(mv[s][:], st[s][:]).then_inc(stats, 1)
                    dve.wait_ge(sqrt_done, t + 1)
                    dve.reciprocal(rs[s][:], sd[s][:]).then_inc(inverse, 1)
                    dve.wait_ge(inverse, t + 1)
                    wait(dve, transposed, t - 1)
                    dve.tensor_scalar(xn[s][:], xt[s][:], mv[s][:, 0:1], rs[s][:], ALU.subtract,
                                      ALU.mult).then_inc(normed, 1)

                def low(q, s):
                    t = 2 * q + s
                    dve.wait_ge(rounded, t + 1)
                    cols = bass.ds(t * P, P)
                    dve.tensor_tensor(h_lo[:, :, cols], ht[s][:], h_hi[:, :, cols].bitcast(F32),
                                      ALU.subtract).then_inc(split, 1)
                pipeline(dve, TT, 2, [(0, norm), (1, low)])
                dve.wait_ge(split, TT)

            @block.tensor
            def _(pe):
                def turn(q, s):
                    t = 2 * q + s
                    pe.wait_ge(normed, t + 1)
                    wait(pe, modulated, t - 1)
                    for k in range(KD):
                        last = pe.transpose(psT[s][:, k, :], xn[s][:, k * P:(k + 1) * P], S.ident[:])
                    last.then_inc(transposed, 1)
                pipeline(pe, TT, 2, [(0, turn)])

            @block.scalar
            def _(act):
                def root(q, s):
                    act.wait_ge(stats, 2 * q + s + 1)
                    act.activation(sd[s][:], mv[s][:, 1:2], ACT.Sqrt, bias=S.eps[:]).then_inc(sqrt_done, 1)

                def modulate(q, s):
                    t = 2 * q + s
                    act.wait_ge(transposed, t + 1)
                    wait(act, split, t - 1)
                    for k in range(KD):
                        last = act.activation(ht[s][:, k, :], psT[s][:, k, :], ACT.Identity,
                                              bias=S.modT[:, SH1 + k:SH1 + k + 1], scale=S.modT[:, SC1 + k:SC1 + k + 1])
                    last.then_inc(modulated, 1)
                    act.wait_ge(modulated, t + 1)
                    act.copy(h_hi[:, :, bass.ds(t * P, P)], ht[s][:]).then_inc(rounded, 1)
                pipeline(act, TT, 2, [(0, root), (1, modulate)])


def decay(nc, A, S, sem, sems, h_hi, h_lo):
    with ExitStack() as ctx:
        sb, ps = stack(ctx, nc, "dec")
        W = TT * HEADS
        w = sb("w", [P, KD, HEADS])
        w_hi = sb("w_hi", [P, KD, HEADS], F32R)
        w_lo = sb("w_lo", [P, KD, HEADS], F32R)
        bias = sb("bias", [P, HEADS])
        alog = sb("alog", [P, HEADS])
        a = sb("a", [P, HEADS])
        v = sb("v", [P, W])
        av = sb("av", [P, W])
        e = sb("e", [P, W])
        u = sb("u", [P, W])
        um = sb("um", [P, W])
        zero = sb("zero", [P, W])
        ln = sb("ln", [P, W])
        la = sb("la", [P, W])
        acT = sb("acT", [HEADS, SEQ])
        psD = ps("dt", [P, W])
        psA = ps("acum", [P, W])
        psE = ps("total", [P, W])
        psAT = ps("acumT", [HEADS, SEQ])
        loads, w_rounded, w_split, dt_done, link, exp_a, exp_v, ln_u, la_ready, sums, turned, copied, stored, tail = (
            sem("dec_loads"), sem("dec_w_rounded"), sem("dec_w_split"), sem("dec_dt"), sem("dec_link"), sem("dec_exp_a"),
            sem("dec_exp_v"), sem("dec_ln"), sem("dec_la"), sem("dec_sums"), sem("dec_turned"), sem("dec_copied"),
            sem("dec_stored"), sem("dec_tail"))

        def per_tile(t):
            return t[:].rearrange("p (t h) -> p t h", h=HEADS)

        with nc.Block() as block:
            @block.sync
            def _(sp):
                sp.dma_start(w[:], A["w_dt"].rearrange("p (k n) -> p k n", k=KD)).then_inc(loads, 16)
                sp.dma_start(bias[:], A["dt_bias"][0].partition_broadcast(P)).then_inc(loads, 16)
                sp.dma_start(alog[:], A["a_log"][0].partition_broadcast(P)).then_inc(loads, 16)
                sp.wait_ge(copied, 1)
                apart(sp, S)
                sp.dma_start(S.acum_d, acT[:]).then_inc(stored, 16)
                sp.wait_ge(stored, 16)

            @block.tensor
            def _(pe):
                pe.wait_ge(w_split, 1)
                for t in range(TT):
                    last = product(pe, psD[:, t * HEADS:(t + 1) * HEADS],
                                   [lambda k, x=x: x[:, k, t * P:(t + 1) * P] for x in (h_hi, h_lo)],
                                   [lambda k, x=x: x[:, k, :] for x in (w_hi, w_lo)], KD)
                last.then_inc(dt_done, 1)
                pe.wait_ge(la_ready, 1)
                pe.matmul(psA[:], S.tri[:], la[:], start=True, stop=True)
                pe.matmul(psE[:], S.ones[:], la[:], start=True, stop=True).then_inc(sums, 1)
                for t in range(TT):
                    last = pe.matmul(psAT[:, t * P:(t + 1) * P], la[:, t * HEADS:(t + 1) * HEADS], S.tri[:],
                                     start=True, stop=True)
                last.then_inc(turned, 1)

            @block.scalar
            def _(act):
                act.wait_ge(loads, 48)
                act.copy(w_hi[:], w[:]).then_inc(w_rounded, 1)
                act.activation(a[:], alog[:], ACT.Exp).then_inc(exp_a, 1)
                act.wait_ge(link, 2)
                act.activation(e[:], av[:], ACT.Exp, scale=-1.0).then_inc(exp_v, 1)
                act.wait_ge(link, 3)
                act.activation(ln[:], u[:], ACT.Ln).then_inc(ln_u, 1)
                act.wait_ge(sums, 1)
                act.activation(S.chunk_decay[:], psE[:], ACT.Exp).then_inc(tail, 1)
                act.wait_ge(link, 12)
                act.activation(S.decay[:], v[:], ACT.Exp).then_inc(tail, 1)
                act.wait_ge(turned, 1)
                act.copy(acT[:], psAT[:]).then_inc(copied, 1)
                act.wait_ge(tail, 2)

            @block.vector
            def _(dve):
                dve.wait_ge(w_rounded, 1)
                dve.tensor_tensor(w_lo[:], w[:], w_hi[:].bitcast(F32), ALU.subtract).then_inc(w_split, 1)
                chain = Chain(dve, link)
                dve.wait_ge(loads, 48)
                dve.wait_ge(dt_done, 1)
                chain.step(dve.tensor_tensor(per_tile(v), per_tile(psD), bias[:].unsqueeze(1).to_broadcast([P, TT, HEADS]), ALU.add))
                chain.step(dve.scalar_tensor_tensor(out=av[:], in0=v[:], scalar=-1.0, in1=v[:], op0=ALU.mult, op1=ALU.max))
                dve.wait_ge(exp_v, 1)
                chain.step(dve.tensor_scalar(u[:], e[:], 1.0, None, ALU.add))
                chain.step(dve.tensor_scalar(um[:], u[:], -1.0, None, ALU.add))
                chain.step(dve.tensor_scalar(zero[:], um[:], 0.0, None, ALU.is_equal))
                chain.step(dve.tensor_tensor(um[:], um[:], zero[:], ALU.add))
                dve.wait_ge(ln_u, 1)
                chain.step(dve.tensor_tensor(ln[:], ln[:], zero[:], ALU.add))
                chain.step(dve.reciprocal(um[:], um[:]))
                chain.step(dve.tensor_tensor(ln[:], ln[:], um[:], ALU.mult))
                chain.step(dve.tensor_tensor(ln[:], ln[:], e[:], ALU.mult))
                chain.step(dve.scalar_tensor_tensor(out=S.dt[:], in0=v[:], scalar=0.0, in1=ln[:], op0=ALU.max, op1=ALU.add))
                dve.wait_ge(exp_a, 1)
                dve.scalar_tensor_tensor(out=per_tile(la), in0=per_tile(S.dt), scalar=-1.0,
                                         in1=a[:].unsqueeze(1).to_broadcast([P, TT, HEADS]), op0=ALU.mult,
                                         op1=ALU.mult).then_inc(la_ready, 1)
                dve.wait_ge(sums, 1)
                dve.tensor_copy(S.acum[:], psA[:]).then_inc(la_ready, 1)
                dve.wait_ge(la_ready, 2)
                dve.wait_ge(tail, 1)
                chain.step(dve.tensor_tensor(v[:], psE[:], S.acum[:], ALU.subtract))


def project(nc, A, S, sem, sems, h_hi, h_lo):
    with ExitStack() as ctx:
        sb, ps = stack(ctx, nc, "prj")
        TB = SEQ // BANK
        w = [sb(f"w{i}", [P, KD, P]) for i in range(2)]
        w_hi = [sb(f"w_hi{i}", [P, KD, P], F32R) for i in range(2)]
        w_lo = [sb(f"w_lo{i}", [P, KD, P], F32R) for i in range(2)]
        ob = [sb(f"out{i}", [P, SEQ]) for i in range(2)]
        c_sb = sb("c", [P, SEQ])
        cx = sb("cx", [P, SEQ])
        cw = sb("conv_w", [P, N_XBC * CONV])
        cb = sb("conv_b", [P, N_XBC])
        sw = sb("short_w", [P, N_SC * SCONV])
        gb = sb("gate_b", [P, N_GATE])
        psP = [ps(f"p{i}", [P, SEQ]) for i in range(2)]
        w_in = sems("prj_w", 2)
        stored = sems("prj_stored", 2)
        params, w_rounded, w_split, done, act_out, act_part, drained, link = (
            sem("prj_params"), sem("prj_w_rounded"), sem("prj_w_split"), sem("prj_done"), sem("prj_act_out"),
            sem("prj_act_part"), sem("prj_drained"), sem("prj_link"))
        X0, C0, G0 = N_Z, N_Z + N_XBC, N_Z + N_XBC + 3 * N_SC

        def kinds(eng, z, xbc, short, gate):
            for s in range(2):
                z(s, s, s)
            with eng.Fori(1, N_Z // 2) as r:
                for s in range(2):
                    z(r * 2 + s, r * 2 + s, s)
            with eng.Fori(0, N_XBC // 2) as r:
                for s in range(2):
                    xbc(X0 + r * 2 + s, r * 2 + s, s)
            with eng.Fori(0, N_SC // 2) as r:
                for s in range(2):
                    for part in range(3):
                        short(C0 + r * 6 + s * 3 + part, r * 2 + s, s, part)
            with eng.Fori(0, N_GATE // 2 - 1) as r:
                for s in range(2):
                    gate(G0 + r * 2 + s, r * 2 + s, s)
            for s in range(2):
                gate(N_PROJ - 2 + s, N_GATE - 2 + s, s)

        with nc.Block() as block:
            @block.sync
            def _(sp):
                apart(sp, S)
                for dst, name in ((cw, "conv_w"), (cb, "conv_b"), (sw, "short_w"), (gb, "b_gateT")):
                    sp.dma_start(dst[:], A[name]).then_inc(params, 16)

                def load(q, s):
                    n = 2 * q + s
                    wait(sp, w_split, n - 1)
                    apart(sp, S)
                    sp.dma_start(w[s][:], A["w_in_t"][bass.ds(n * P, P), :].rearrange("p (k m) -> p k m", k=KD)).then_inc(w_in[s], 16)
                pipeline(sp, N_PROJ, 2, [(0, load)])

            @block.tensor
            def _(pe):
                def tile(q, s):
                    n = 2 * q + s
                    pe.wait_ge(w_split, n + 1)
                    wait(pe, drained, n - 1)
                    for b in range(TB):
                        last = product(pe, psP[s][:, b * BANK:(b + 1) * BANK],
                                       [lambda k, x=x: x[:, k, :] for x in (w_hi[s], w_lo[s])],
                                       [lambda k, x=x: x[:, k, b * BANK:(b + 1) * BANK] for x in (h_hi, h_lo)], KD)
                    last.then_inc(done, 1)
                pipeline(pe, N_PROJ, 2, [(0, tile)])

            @block.scalar
            def _(act):
                def round_w(n, s):
                    act.wait_ge(w_in[s], 8 * (n - s) + 16)
                    wait(act, done, n - 1)
                    act.copy(w_hi[s][:], w[s][:]).then_inc(w_rounded, 1)

                def ahead(n, s):
                    if not (isinstance(n, int) and n + 1 >= N_PROJ):
                        round_w(n + 1, 1 - s)
                    act.wait_ge(done, n + 1)

                def z(n, i, s):
                    ahead(n, s % 2)
                    wait(act, stored[s], 8 * (ROW_Z + i - s))
                    act.activation(ob[s][:], psP[s][:], ACT.Silu).then_inc(act_out, 1)

                def xbc(n, i, s):
                    ahead(n, s)
                    act.wait_ge(stored[s], 8 * (ROW_XBC + i - s))
                    act.activation(ob[s][:], psP[s][:], ACT.Identity, bias=cb[:, bass.ds(i, 1)],
                                   scale=cw[:, bass.ds(i * CONV + CONV - 1, 1)]).then_inc(act_part, 1)
                    act.wait_ge(drained, n + 1)
                    act.activation(ob[s][:], ob[s][:], ACT.Silu).then_inc(act_out, 1)

                def short(n, i, s, part):
                    slot = (3 * s + part) % 2
                    ahead(n, slot)
                    if part == 0:
                        act.wait_ge(drained, n - 1)
                        act.copy(c_sb[:], psP[slot][:]).then_inc(act_part, 1)

                def gate(n, i, s):
                    ahead(n, s)
                    act.wait_ge(stored[s], 8 * (ROW_GATE + i - s))
                    act.activation(ob[s][:], psP[s][:], ACT.Sigmoid, bias=gb[:, bass.ds(i, 1)]).then_inc(act_out, 1)

                act.wait_ge(params, 64)
                round_w(0, 0)
                kinds(act, z, xbc, short, gate)

            @block.vector
            def _(dve):
                chain = Chain(dve, link)

                def split_w(n, s):
                    dve.wait_ge(w_rounded, n + 1)
                    dve.tensor_tensor(w_lo[s][:], w[s][:], w_hi[s][:].bitcast(F32), ALU.subtract).then_inc(w_split, 1)

                def ahead(n, s):
                    if not (isinstance(n, int) and n + 1 >= N_PROJ):
                        split_w(n + 1, 1 - s)

                def z(n, i, s):
                    ahead(n, s)
                    dve.wait_ge(act_out, n + 1)
                    wait(dve, drained, n)
                    dve.sem_inc(drained, 1)

                def xbc(n, i, s):
                    ahead(n, s)
                    dve.wait_ge(act_part, i + 1)
                    chain.item(i, CONV - 2)
                    for shift in range(1, CONV):
                        ins = dve.scalar_tensor_tensor(out=ob[s][:, shift:], in0=psP[s][:, :SEQ - shift],
                                                       scalar=cw[:, bass.ds(i * CONV + CONV - 1 - shift, 1)],
                                                       in1=ob[s][:, shift:], op0=ALU.mult, op1=ALU.add)
                        if shift < CONV - 1:
                            chain.step(ins)
                        else:
                            ins.then_inc(drained, 1)
                    chain.end()

                def short(n, i, s, part):
                    slot = (3 * s + part) % 2
                    ahead(n, slot)
                    first = N_XBC * (CONV - 2)
                    if part == 0:
                        dve.wait_ge(act_part, N_XBC + i + 1)
                        dve.wait_ge(drained, n)
                        dve.sem_inc(drained, 1)
                    if part == 1:
                        dve.wait_ge(done, n + 1)
                        dve.tensor_tensor(cx[:], psP[slot][:], c_sb[:], ALU.mult).then_inc(drained, 1)
                        dve.wait_ge(drained, n + 1)
                        dve.wait_ge(stored[s], 8 * (ROW_Q + i - s))
                        chain.item(i, SCONV)
                        chain.n = chain.n + first
                        chain.step(dve.tensor_scalar(ob[s][:], cx[:], sw[:, bass.ds(i * SCONV + SCONV - 1, 1)], None, ALU.mult))
                        for shift in range(1, SCONV):
                            chain.step(dve.scalar_tensor_tensor(out=ob[s][:, shift:], in0=cx[:, :SEQ - shift],
                                                                scalar=sw[:, bass.ds(i * SCONV + SCONV - 1 - shift, 1)],
                                                                in1=ob[s][:, shift:], op0=ALU.mult, op1=ALU.add))
                        chain.end()
                    if part == 2:
                        dve.wait_ge(done, n + 1)
                        dve.tensor_tensor(ob[s][:], psP[slot][:], ob[s][:], ALU.mult).then_inc(drained, 1)

                def gate(n, i, s):
                    ahead(n, s)
                    dve.wait_ge(act_out, N_Z + N_XBC + i + 1)
                    dve.wait_ge(drained, n)
                    dve.sem_inc(drained, 1)

                dve.wait_ge(params, 64)
                split_w(0, 0)
                kinds(dve, z, xbc, short, gate)

            @block.gpsimd
            def _(pool):
                def store(m, s):
                    apart(pool, S)
                    pool.dma_start(S.rows_d[bass.ds(m * P, P), :], ob[s][:]).then_inc(stored[s], 16)

                def by_act(n, i, s, row, count):
                    pool.wait_ge(act_out, count)
                    store(row + i, s)

                def short(n, i, s, part):
                    if part == 2:
                        pool.wait_ge(drained, n + 1)
                        store(ROW_Q + i, s)

                kinds(pool, lambda n, i, s: by_act(n, i, s, ROW_Z, i + 1),
                      lambda n, i, s: by_act(n, i, s, ROW_XBC, i + N_Z + 1), short,
                      lambda n, i, s: by_act(n, i, s, ROW_GATE, i + N_Z + N_XBC + 1))
                for s in range(2):
                    pool.wait_ge(stored[s], 8 * N_ROWS)


def ssd(nc, A, S, sem, sems):
    with ExitStack() as ctx:
        sb, ps = stack(ctx, nc, "ssd")
        GT = HG * HD // P
        LOADS = 5
        xT = [sb(f"xT{i}", [P, GT, P]) for i in range(4)]
        zT = [sb(f"zT{i}", [P, GT, P]) for i in range(4)]
        bT = [sb(f"bT{i}", [P, P]) for i in range(4)]
        cT = [sb(f"cT{i}", [P, P]) for i in range(4)]
        ab = [sb(f"acum{i}", [P, HG, P]) for i in range(4)]
        xd = [sb(f"xd{i}", [P, HG, HD]) for i in range(2)]
        xdd = [sb(f"xdd{i}", [P, HG, HD]) for i in range(2)]
        b_tok = [sb(f"b{i}", [P, P]) for i in range(2)]
        cbm = [sb(f"cbm{i}", [P, P]) for i in range(2)]
        seg = [sb(f"seg{i}", [P, HG, P]) for i in range(2)]
        ldec = [sb(f"ldec{i}", [P, HG, P]) for i in range(2)]
        m = [sb(f"m{i}", [P, HG, P]) for i in range(2)]
        ea = [sb(f"ea{i}", [P, HG, P]) for i in range(2)]
        cs = [sb(f"cs{i}", [P, HG, P]) for i in range(2)]
        xs = [sb(f"xs{i}", [P, GT, P]) for i in range(2)]
        yo = [sb(f"y{i}", [P, GT, P]) for i in range(4)]
        prev = [sb(f"state{i}", [P, HG, HD]) for i in range(4)]
        dsk = sb("d_skip", [P, INNER // P])
        psX = [ps(f"x{i}", [P, GT * P]) for i in range(2)]
        psB = [ps(f"b{i}", [P, BANK]) for i in range(2)]
        psY = [ps(f"y{i}", [P, GT * P]) for i in range(2)]
        psS = [ps(f"s{i}", [P, HG * HD]) for i in range(2)]
        loaded = sems("ssd_in", 4)
        stored = sems("ssd_stored", 4)
        d_in, zeroed, turned, x_ready, seg_ready, m_ready, ea_ready, b_ready, l_ready, xdd_ready, cs_ready, xs_ready, \
            y_done, skipped, decayed, state_ready, y_ready, masked = (sem(f"ssd_{n}") for n in (
                "d", "zeroed", "turned", "x", "seg", "m", "ea", "b", "l", "xdd", "cs", "xs", "y_done", "skipped",
                "decayed", "state", "y", "masked"))

        def heads(t, c, g):
            return t[:, bass.ds(c * HEADS + g * HG, HG)]

        with nc.Block() as block:
            @block.sync
            def _(sp):
                def store(c, g):
                    sp.wait_ge(y_ready, 4 * c + g + 1)
                    apart(sp, S)
                    sp.dma_start(S.y_d[g * GT * P:(g + 1) * GT * P, bass.ds(c * P, P)].rearrange("(a p) t -> p a t", p=P),
                                 yo[g][:]).then_inc(stored[g], 16)

                def load(c, g):
                    cols = bass.ds(c * P, P)
                    for dst, row, tiles in ((xT[g], ROW_XBC + g * GT, GT), (zT[g], ROW_Z + g * GT, GT)):
                        sp.dma_start(dst[:], S.rows_d[row * P:(row + tiles) * P, cols].rearrange(
                            "(a p) t -> p a t", p=P)).then_inc(loaded[g], 16)
                    for dst, row in ((bT[g], ROW_XBC + N_Z + g), (cT[g], ROW_XBC + N_Z + GROUPS + g)):
                        sp.dma_start(dst[:], S.rows_d[row * P:(row + 1) * P, cols]).then_inc(loaded[g], 16)
                    sp.dma_start(ab[g][:], S.acum_d[g * HG:(g + 1) * HG, cols].partition_broadcast(P)).then_inc(loaded[g], 16)

                sp.dma_start(dsk[:], A["d_skipT"]).then_inc(d_in, 16)
                pipeline(sp, 4 * TT, 4, [(4, store), (0, load)])
                for g in range(4):
                    sp.wait_ge(stored[g], 16 * TT)

            @block.tensor
            def _(pe):
                def front(c, g):
                    u, s = 4 * c + g, g % 2
                    pe.wait_ge(loaded[g], 16 * LOADS * (c + 1))
                    wait(pe, x_ready, u - 1)
                    wait(pe, b_ready, u - 1)
                    wait(pe, masked, u - 1)
                    for a in range(GT):
                        pe.transpose(psX[s][:, a * P:(a + 1) * P], xT[g][:, a, :], S.ident[:])
                    pe.transpose(psB[s][:, 0:P], bT[g][:], S.ident[:])
                    pe.matmul(psB[s][:, P:2 * P], bT[g][:], cT[g][:], start=True, stop=True).then_inc(turned, 1)

                def back(c, g):
                    u, s = 4 * c + g, g % 2
                    pe.wait_ge(x_ready, u + 1)
                    pe.wait_ge(m_ready, u + 1)
                    pe.wait_ge(cs_ready, u + 1)
                    pe.wait_ge(zeroed, 4)
                    wait(pe, state_ready, u - 3)
                    wait(pe, skipped, u - 1)
                    for h in range(HG):
                        rows, cols = slice(h % 2 * HD, (h % 2 + 1) * HD), slice(h // 2 * P, (h // 2 + 1) * P)
                        pe.matmul(psY[s][rows, cols], xd[s][:, h, :], m[s][:, h, :], start=True, stop=False)
                        last = pe.matmul(psY[s][rows, cols], prev[g][:, h, :], cs[s][:, h, :], start=False, stop=True)
                    pe.wait_ge(b_ready, u + 1)
                    pe.wait_ge(xdd_ready, u + 1)
                    wait(pe, state_ready, u - 1)
                    pe.matmul(psS[s][:], b_tok[s][:], xdd[s][:].rearrange("p h d -> p (h d)"),
                              start=True, stop=True).then_inc(y_done, 1)
                pipeline(pe, 4 * TT, 4, [(0, front), (1, back)])

            @block.scalar
            def _(act):
                def front(c, g):
                    u, s = 4 * c + g, g % 2
                    act.wait_ge(loaded[g], 16 * LOADS * (c + 1))
                    wait(act, cs_ready, u - 1)
                    act.activation(ea[s][:], ab[g][:], ACT.Exp).then_inc(ea_ready, 1)
                    act.wait_ge(turned, u + 1)
                    wait(act, y_done, u - 1)
                    act.copy(b_tok[s][:], psB[s][:, 0:P]).then_inc(b_ready, 1)
                    act.wait_ge(seg_ready, u + 1)
                    wait(act, m_ready, u - 1)
                    act.activation(ldec[s][:], seg[s][:], ACT.Exp).then_inc(l_ready, 1)
                pipeline(act, 4 * TT, 4, [(0, front)])

            @block.vector
            def _(dve):
                def front(c, g):
                    u, s = 4 * c + g, g % 2
                    dve.wait_ge(loaded[g], 16 * LOADS * (c + 1))
                    wait(dve, l_ready, u - 1)
                    for h in range(HG):
                        last = dve.tensor_scalar(seg[s][:, h, :], ab[g][:, h, :], S.acum[:, bass.ds(c * HEADS + g * HG + h, 1)],
                                                 0.0, ALU.subtract, ALU.min)
                    last.then_inc(seg_ready, 1)
                    dve.wait_ge(turned, u + 1)
                    wait(dve, y_done, u - 1)
                    wait(dve, xdd_ready, u - 1)
                    dve.tensor_tensor(xd[s][:], psX[s][:].rearrange("p (h d) -> p h d", h=HG),
                                      heads(S.dt, c, g).unsqueeze(2).to_broadcast([P, HG, HD]), ALU.mult).then_inc(x_ready, 1)
                    dve.wait_ge(b_ready, u + 1)
                    dve.tensor_tensor(cbm[s][:], psB[s][:, P:2 * P], S.tri[:], ALU.mult).then_inc(masked, 1)

                def back(c, g):
                    u, s = 4 * c + g, g % 2
                    dve.wait_ge(y_done, u + 1)
                    dve.tensor_tensor(prev[g][:], prev[g][:], heads(S.chunk_decay, c, g).unsqueeze(2).to_broadcast([P, HG, HD]),
                                      ALU.mult).then_inc(decayed, 1)
                    dve.wait_ge(xs_ready, u + 1)
                    wait(dve, stored[g], 16 * c)
                    dve.tensor_tensor(yo[g][:], psY[s][:].rearrange("p (a t) -> p a t", a=GT), xs[s][:], ALU.add).then_inc(skipped, 1)
                    dve.wait_ge(decayed, u + 1)
                    dve.tensor_tensor(prev[g][:], psS[s][:].rearrange("p (h d) -> p h d", h=HG), prev[g][:],
                                      ALU.add).then_inc(state_ready, 1)
                    dve.wait_ge(skipped, u + 1)
                    dve.tensor_tensor(yo[g][:], yo[g][:], zT[g][:], ALU.mult).then_inc(y_ready, 1)

                def decayed_scores(c, g):
                    u, s = 4 * c + g, g % 2
                    dve.wait_ge(l_ready, u + 1)
                    dve.wait_ge(masked, u + 1)
                    dve.tensor_tensor(m[s][:], ldec[s][:], cbm[s][:].unsqueeze(1).to_broadcast([P, HG, P]),
                                      ALU.mult).then_inc(m_ready, 1)

                for g in range(4):
                    dve.memset(prev[g][:], 0.0).then_inc(zeroed, 1)
                dve.wait_ge(zeroed, 4)
                pipeline(dve, 4 * TT, 4, [(0, front), (1, back), (0, decayed_scores)])

            @block.gpsimd
            def _(pool):
                def unit(c, g):
                    u, s = 4 * c + g, g % 2
                    pool.wait_ge(ea_ready, u + 1)
                    wait(pool, y_done, u - 1)
                    pool.tensor_tensor(cs[s][:], ea[s][:], cT[g][:].unsqueeze(1).to_broadcast([P, HG, P]), ALU.mult).then_inc(cs_ready, 1)
                    pool.wait_ge(x_ready, u + 1)
                    pool.tensor_tensor(xdd[s][:], xd[s][:], heads(S.decay, c, g).unsqueeze(2).to_broadcast([P, HG, HD]),
                                       ALU.mult).then_inc(xdd_ready, 1)
                    wait(pool, skipped, u - 1)
                    pool.tensor_tensor(xs[s][:], xT[g][:], dsk[:, g * GT:(g + 1) * GT].unsqueeze(2).to_broadcast([P, GT, P]),
                                       ALU.mult).then_inc(xs_ready, 1)
                pool.wait_ge(d_in, 16)
                pipeline(pool, 4 * TT, 4, [(0, unit)])


def branches(nc, A, S, sem, sems):
    with ExitStack() as ctx:
        sb, ps = stack(ctx, nc, "brn")
        KY, KQ = INNER // P, KD
        ITEMS = KY + KQ
        NU = D // P
        TB = SEQ // BANK
        raw = [sb(f"raw{i}", [P, BANK]) for i in range(4)]
        hi = sb("hi", [P, ITEMS, BANK], F32R)
        lo = sb("lo", [P, ITEMS, BANK], F32R)
        sq = [sb(f"sq{i}", [P, BANK]) for i in range(2)]
        sqs = sb("sq_sum", [P, BANK])
        rstd = sb("rstd", [P, BANK])
        w = sb("w", [P, ITEMS, P])
        w_hi = [sb(f"w_hi{i}", [P, ITEMS, P], F32R) for i in range(2)]
        w_lo = [sb(f"w_lo{i}", [P, ITEMS, P], F32R) for i in range(2)]
        ga = [sb(f"ga{i}", [P, BANK]) for i in range(2)]
        gb = [sb(f"gb{i}", [P, BANK]) for i in range(2)]
        ta = [sb(f"ta{i}", [P, BANK]) for i in range(2)]
        tb_ = [sb(f"tb{i}", [P, BANK]) for i in range(2)]
        nw = sb("norm_w", [P, KY])
        psA = [ps(f"a{i}", [P, BANK]) for i in range(2)]
        psB = [ps(f"b{i}", [P, BANK]) for i in range(2)]
        psQ = ps("squares", [P, BANK])
        raw_in, w_in, stored = sems("brn_raw", 4), sems("brn_w", 2), sems("brn_stored", 2)
        nw_in, rounded, squared, low, item_done, w_rounded, w_split, unit_done, ss_done, root_done, rstd_ready, part_a, \
            part_b, scaled, combined = (sem(f"brn_{n}") for n in (
                "nw", "rounded", "squared", "low", "item", "w_rounded", "w_split", "unit", "ss", "root", "rstd", "part_a",
                "part_b", "scaled", "combined"))

        def units(eng, tb, fn):
            for s in range(2):
                fn(tb * NU + s, s, s)
            with eng.Fori(1, NU // 2) as r:
                for s in range(2):
                    fn(r * 2 + (tb * NU + s), r * 2 + s, s)

        with nc.Block() as block:
            @block.sync
            def _(sp):
                sp.dma_start(nw[:], A["ssd_norm_wT"]).then_inc(nw_in, 16)

                def load(u, n, s, tb):
                    wait(sp, w_split, u)
                    apart(sp, S)
                    wait(sp, combined, u - 1)
                    apart(sp, S)
                    sp.dma_start(w[:], A["w_branch_t"][bass.ds(n * P, P), :].rearrange("p (k m) -> p k m", k=ITEMS)).then_inc(w_in[s], 16)
                    for dst, row in ((ga, ROW_GATE), (gb, ROW_GATE + NU)):
                        sp.dma_start(dst[s][:], S.rows_d[bass.ds((n + row) * P, P), tb * BANK:(tb + 1) * BANK]).then_inc(w_in[s], 16)

                for tb in range(TB):
                    for j in range(ITEMS):
                        i = tb * ITEMS + j
                        src = S.y_d[j * P:(j + 1) * P] if j < KY else S.rows_d[(ROW_Q + j - KY) * P:(ROW_Q + j - KY + 1) * P]
                        wait(sp, item_done, i - 3)
                        apart(sp, S)
                        sp.dma_start(raw[j % 4][:], src[:, tb * BANK:(tb + 1) * BANK]).then_inc(raw_in[j % 4], 16)
                    units(sp, tb, lambda u, n, s: load(u, n, s, tb))

            @block.gpsimd
            def _(pool):
                for tb in range(TB):
                    def store(u, n, s):
                        pool.wait_ge(combined, u + 1)
                        apart(pool, S)
                        pool.dma_start(S.mixin_d[bass.ds(n * P, P), tb * BANK:(tb + 1) * BANK], ta[s][:]).then_inc(stored[s], 16)
                    units(pool, tb, store)
                for s in range(2):
                    pool.wait_ge(stored[s], 16 * TB * NU // 2)

            @block.scalar
            def _(act):
                def round_w(u, n, s):
                    act.wait_ge(w_in[s], 24 * (u - s) + 48)
                    wait(act, unit_done, u - 1)
                    act.copy(w_hi[s][:], w[:]).then_inc(w_rounded, 1)
                    if isinstance(u, int) and u % NU == 1:
                        act.wait_ge(ss_done, u // NU + 1)
                        act.activation(rstd[:], psQ[:], ACT.Sqrt, bias=S.eps[:], scale=1.0 / INNER).then_inc(root_done, 1)

                act.wait_ge(nw_in, 16)
                for tb in range(TB):
                    wait(act, unit_done, tb * NU)
                    wait(act, combined, tb * NU)
                    for j in range(ITEMS):
                        act.wait_ge(raw_in[j % 4], 16 * ((tb * ITEMS + j) // 4 + 1))
                        if j < KY:
                            act.activation(hi[:, j, :], raw[j % 4][:], ACT.Identity, scale=nw[:, j:j + 1]).then_inc(rounded, 1)
                            wait(act, item_done, tb * ITEMS + j - 1 if j >= 2 else 0)
                            act.activation(sq[j % 2][:], raw[j % 4][:], ACT.Square).then_inc(squared, 1)
                        else:
                            act.copy(hi[:, j, :], raw[j % 4][:]).then_inc(rounded, 1)
                    units(act, tb, round_w)

            @block.vector
            def _(dve):
                def split_w(u, n, s):
                    dve.wait_ge(w_rounded, u + 1)
                    dve.tensor_tensor(w_lo[s][:], w[:], w_hi[s][:].bitcast(F32), ALU.subtract).then_inc(w_split, 1)

                def combine(u, n, s):
                    dve.wait_ge(unit_done, u + 1)
                    wait(dve, stored[s], 8 * (u - s))
                    dve.tensor_tensor(ta[s][:], psA[s][:], rstd[:], ALU.mult).then_inc(part_a, 1)
                    dve.tensor_tensor(tb_[s][:], psB[s][:], gb[s][:], ALU.mult).then_inc(part_b, 1)
                    dve.wait_ge(part_a, u + 1)
                    dve.tensor_tensor(ta[s][:], ta[s][:], ga[s][:], ALU.mult).then_inc(scaled, 1)
                    dve.wait_ge(part_b, u + 1)
                    dve.wait_ge(scaled, u + 1)
                    dve.tensor_tensor(ta[s][:], ta[s][:], tb_[s][:], ALU.add).then_inc(combined, 1)

                dve.wait_ge(nw_in, 16)
                for tb in range(TB):
                    for j in range(ITEMS):
                        i = tb * ITEMS + j
                        dve.wait_ge(rounded, i + 1)
                        if j < KY:
                            dve.scalar_tensor_tensor(out=lo[:, j, :], in0=raw[j % 4][:], scalar=nw[:, j:j + 1],
                                                     in1=hi[:, j, :].bitcast(F32), op0=ALU.mult, op1=ALU.subtract).then_inc(low, 1)
                            dve.wait_ge(low, tb * KY + j + 1)
                            dve.wait_ge(squared, tb * KY + j + 1)
                            if j == 0:
                                wait(dve, ss_done, tb)
                                dve.tensor_copy(sqs[:], sq[0][:]).then_inc(item_done, 1)
                            else:
                                dve.wait_ge(item_done, i)
                                dve.tensor_tensor(sqs[:], sqs[:], sq[j % 2][:], ALU.add).then_inc(item_done, 1)
                        else:
                            dve.tensor_tensor(lo[:, j, :], raw[j % 4][:], hi[:, j, :].bitcast(F32), ALU.subtract).then_inc(item_done, 1)
                    split_w(tb * NU, 0, 0)
                    split_w(tb * NU + 1, 1, 1)
                    dve.wait_ge(root_done, tb + 1)
                    dve.reciprocal(rstd[:], rstd[:]).then_inc(rstd_ready, 1)
                    dve.wait_ge(rstd_ready, tb + 1)
                    with dve.Fori(0, NU // 2 - 1) as r:
                        for s in range(2):
                            combine(r * 2 + (tb * NU + s), r * 2 + s, s)
                            split_w(r * 2 + (tb * NU + s + 2), r * 2 + s + 2, s)
                    for s in range(2):
                        combine(tb * NU + NU - 2 + s, NU - 2 + s, s)

            @block.tensor
            def _(pe):
                for tb in range(TB):
                    def unit(u, n, s):
                        if isinstance(n, int) and n == 0:
                            pe.wait_ge(item_done, (tb + 1) * ITEMS)
                        pe.wait_ge(w_split, u + 1)
                        wait(pe, combined, u - 1)
                        product(pe, psA[s][:], [lambda k, x=x: x[:, k, :] for x in (w_hi[s], w_lo[s])],
                                [lambda k, x=x: x[:, k, :] for x in (hi, lo)], KY)
                        product(pe, psB[s][:], [lambda k, x=x: x[:, KY + k, :] for x in (w_hi[s], w_lo[s])],
                                [lambda k, x=x: x[:, KY + k, :] for x in (hi, lo)], KQ).then_inc(unit_done, 1)
                        if isinstance(n, int) and n == 0:
                            wait(pe, rstd_ready, tb)
                            pe.matmul(psQ[:], S.ones[:], sqs[:], start=True, stop=True).then_inc(ss_done, 1)
                    units(pe, tb, unit)


def mix_out(nc, A, S, sem, sems):
    with ExitStack() as ctx:
        sb, ps = stack(ctx, nc, "mix")
        wo_hi = sb("wo_hi", [P, KD, D], F32R)
        wo_lo = sb("wo_lo", [P, KD, D], F32R)
        wr = sb("w_router", [P, KD, EXPERTS])
        br = sb("b_router", [P, EXPERTS])
        lg = sb("ln_g", [P, D])
        lb = sb("ln_b", [P, D])
        wo = [sb(f"wo{i}", [P, D]) for i in range(2)]

        def pair(name, shape, dt=F32):
            return [sb(f"{name}{i}", shape, dt) for i in range(2)]
        mt, mt_hi, mt_lo = pair("m", [P, KD, P]), pair("m_hi", [P, KD, P], F32R), pair("m_lo", [P, KD, P], F32R)
        xt, r, x1, xn = pair("x", [P, D]), pair("r", [P, D]), pair("x1", [P, D]), pair("xn", [P, D])
        st, mv, sd, rs = pair("st", [P, 2, 6]), pair("mv", [P, 2]), pair("sd", [P, 1]), pair("rs", [P, 1])
        st2, mv2, sd2, rs2 = pair("st2", [P, 2, 6]), pair("mv2", [P, 2]), pair("sd2", [P, 1]), pair("rs2", [P, 1])
        hT = pair("hT", [P, KD, P])
        psM = [ps(f"m{i}", [P, D]) for i in range(2)]
        psT = ps("t", [P, KD, P])
        psL = ps("logits", [P, BANK])
        par_in, wo_rounded, wo_split = sem("mix_params"), sem("mix_wo_rounded"), sem("mix_wo_split")
        wo_in, t_in, x1_out, xn_out = sems("mix_wo", 2), sems("mix_in", 2), sems("mix_x1_out", 2), sems("mix_xn_out", 2)
        m_rounded, m_split, mixed, gated, summed, halves, stats, root1, inv1, normed, scaled, x1_ready, halves2, stats2, \
            root2, inv2, xn_ready, turned, modulated, routed, logits = (sem(f"mix_{n}") for n in (
                "m_rounded", "m_split", "mixed", "gated", "summed", "halves", "stats", "root1", "inv1", "normed", "scaled",
                "x1", "halves2", "stats2", "root2", "inv2", "xn", "turned", "modulated", "routed", "logits"))

        with nc.Block() as block:
            @block.sync
            def _(sp):
                sp.dma_start(wr[:], A["w_router_t"].rearrange("p (k n) -> p k n", k=KD)).then_inc(par_in, 16)
                for dst, name in ((br, "b_router"), (lg, "ln1_g"), (lb, "ln1_b")):
                    sp.dma_start(dst[:], A[name][0].partition_broadcast(P)).then_inc(par_in, 16)
                for k in range(KD):
                    wait(sp, wo_split, k - 1)
                    apart(sp, S)
                    sp.dma_start(wo[k % 2][:], A["w_o"][k * P:(k + 1) * P, :]).then_inc(wo_in[k % 2], 16)

                def load(q, s):
                    t = 2 * q + s
                    wait(sp, summed, t - 1)
                    apart(sp, S)
                    sp.dma_start(mt[s][:], S.mixin_d[:, bass.ds(t * P, P)].rearrange("(k p) t -> p k t", p=P)).then_inc(t_in[s], 16)
                    sp.dma_start(xt[s][:], A["x"][bass.ds(t * P, P), :]).then_inc(t_in[s], 16)
                pipeline(sp, TT, 2, [(0, load)])

            @block.gpsimd
            def _(pool):
                def affine(q, s):
                    t = 2 * q + s
                    pool.wait_ge(normed, t + 1)
                    wait(pool, x1_out[s], 16 * q)
                    wait(pool, stats2, t - 1)
                    wait(pool, xn_ready, t - 1)
                    pool.tensor_tensor(x1[s][:], r[s][:], lg[:], ALU.mult).then_inc(scaled, 1)
                    pool.wait_ge(scaled, t + 1)
                    pool.tensor_tensor(x1[s][:], x1[s][:], lb[:], ALU.add).then_inc(x1_ready, 1)

                def store(q, s):
                    t = 2 * q + s
                    pool.wait_ge(x1_ready, t + 1)
                    apart(pool, S)
                    pool.dma_start(S.x1_d[bass.ds(t * P, P), :], x1[s][:]).then_inc(x1_out[s], 16)
                    pool.wait_ge(xn_ready, t + 1)
                    apart(pool, S)
                    pool.dma_start(S.xn2_d[bass.ds(t * P, P), :], xn[s][:]).then_inc(xn_out[s], 16)
                pool.wait_ge(par_in, 64)
                pipeline(pool, TT, 2, [(0, affine), (1, store)])
                for s in range(2):
                    pool.wait_ge(x1_out[s], 8 * TT)
                    pool.wait_ge(xn_out[s], 8 * TT)

            @block.scalar
            def _(act):
                for k in range(KD):
                    act.wait_ge(wo_in[k % 2], 16 * (k // 2 + 1))
                    act.copy(wo_hi[:, k, :], wo[k % 2][:]).then_inc(wo_rounded, 1)

                def round_m(q, s):
                    t = 2 * q + s
                    act.wait_ge(t_in[s], 32 * (q + 1))
                    wait(act, mixed, t - 1)
                    act.copy(mt_hi[s][:], mt[s][:]).then_inc(m_rounded, 1)

                def first_root(q, s):
                    act.wait_ge(stats, 2 * q + s + 1)
                    act.activation(sd[s][:], mv[s][:, 1:2], ACT.Sqrt, bias=S.eps[:]).then_inc(root1, 1)

                def second_root(q, s):
                    act.wait_ge(stats2, 2 * q + s + 1)
                    act.activation(sd2[s][:], mv2[s][:, 1:2], ACT.Sqrt, bias=S.eps[:]).then_inc(root2, 1)

                def modulate(q, s):
                    t = 2 * q + s
                    act.wait_ge(turned, t + 1)
                    wait(act, routed, t - 1)
                    for k in range(KD):
                        last = act.activation(hT[s][:, k, :], psT[:, k, :], ACT.Identity,
                                              bias=S.modT[:, SH2 + k:SH2 + k + 1], scale=S.modT[:, SC2 + k:SC2 + k + 1])
                    last.then_inc(modulated, 1)
                pipeline(act, TT, 2, [(0, round_m), (1, first_root), (2, second_root), (3, modulate)])

            @block.tensor
            def _(pe):
                def mix(q, s):
                    t = 2 * q + s
                    pe.wait_ge(m_split, t + 1)
                    wait(pe, gated, t - 1)
                    for half in range(2):
                        cols = slice(half * BANK, (half + 1) * BANK)
                        last = product(pe, psM[s][:, cols], [lambda k, x=x: x[:, k, :] for x in (mt_hi[s], mt_lo[s])],
                                       [lambda k, x=x: x[:, k, cols] for x in (wo_hi, wo_lo)], KD)
                    last.then_inc(mixed, 1)

                def turn(q, s):
                    t = 2 * q + s
                    pe.wait_ge(xn_ready, t + 1)
                    wait(pe, modulated, t)
                    for k in range(KD):
                        last = pe.transpose(psT[:, k, :], xn[s][:, k * P:(k + 1) * P], S.ident[:])
                    last.then_inc(turned, 1)

                def route(q, s):
                    t = 2 * q + s
                    pe.wait_ge(modulated, t + 1)
                    wait(pe, logits, t)
                    for k in range(KD):
                        last = pe.matmul(psL[:, 0:EXPERTS], hT[s][:, k, :], wr[:, k, :], start=(k == 0), stop=(k == KD - 1))
                    last.then_inc(routed, 1)
                pe.wait_ge(wo_split, KD)
                pe.wait_ge(par_in, 64)
                pipeline(pe, TT, 2, [(3, turn), (0, mix), (3, route)])

            @block.vector
            def _(dve):
                for k in range(KD):
                    dve.wait_ge(wo_rounded, k + 1)
                    dve.tensor_tensor(wo_lo[:, k, :], wo[k % 2][:], wo_hi[:, k, :].bitcast(F32), ALU.subtract).then_inc(wo_split, 1)
                dve.wait_ge(par_in, 64)

                def split_m(q, s):
                    dve.wait_ge(m_rounded, 2 * q + s + 1)
                    dve.tensor_tensor(mt_lo[s][:], mt[s][:], mt_hi[s][:].bitcast(F32), ALU.subtract).then_inc(m_split, 1)

                def residual(q, s):
                    t = 2 * q + s
                    dve.wait_ge(mixed, t + 1)
                    wait(dve, x1_ready, t - 1)
                    dve.tensor_tensor(r[s][:], psM[s][:], S.g1[:], ALU.mult).then_inc(gated, 1)
                    dve.wait_ge(gated, t + 1)
                    dve.scalar_tensor_tensor(out=r[s][:], in0=xt[s][:], scalar=DN_ALPHA, in1=r[s][:], op0=ALU.mult,
                                             op1=ALU.add).then_inc(summed, 1)
                    dve.wait_ge(summed, t + 1)
                    for half in range(2):
                        dve.bn_stats(st[s][:, half, :], r[s][:, half * BANK:(half + 1) * BANK]).then_inc(halves, 1)
                    dve.wait_ge(halves, 2 * (t + 1))
                    apart(dve, S)
                    dve.bn_aggr(mv[s][:], st[s][:]).then_inc(stats, 1)

                def normalise(q, s):
                    t = 2 * q + s
                    dve.wait_ge(root1, t + 1)
                    dve.reciprocal(rs[s][:], sd[s][:]).then_inc(inv1, 1)
                    dve.wait_ge(inv1, t + 1)
                    dve.tensor_scalar(r[s][:], r[s][:], mv[s][:, 0:1], rs[s][:], ALU.subtract, ALU.mult).then_inc(normed, 1)

                def second_stats(q, s):
                    t = 2 * q + s
                    dve.wait_ge(x1_ready, t + 1)
                    for half in range(2):
                        dve.bn_stats(st2[s][:, half, :], x1[s][:, half * BANK:(half + 1) * BANK]).then_inc(halves2, 1)
                    dve.wait_ge(halves2, 2 * (t + 1))
                    apart(dve, S)
                    dve.bn_aggr(mv2[s][:], st2[s][:]).then_inc(stats2, 1)

                def second_norm(q, s):
                    t = 2 * q + s
                    dve.wait_ge(root2, t + 1)
                    dve.reciprocal(rs2[s][:], sd2[s][:]).then_inc(inv2, 1)
                    dve.wait_ge(inv2, t + 1)
                    wait(dve, xn_out[s], 16 * q)
                    wait(dve, turned, t - 1)
                    dve.tensor_scalar(xn[s][:], x1[s][:], mv2[s][:, 0:1], rs2[s][:], ALU.subtract, ALU.mult).then_inc(xn_ready, 1)

                def keep_logits(q, s):
                    t = 2 * q + s
                    dve.wait_ge(routed, t + 1)
                    dve.tensor_tensor(S.logits[:, bass.ds(t * EXPERTS, EXPERTS)], psL[:, 0:EXPERTS], br[:], ALU.add).then_inc(logits, 1)
                pipeline(dve, TT, 2, [(0, split_m), (1, residual), (1, normalise), (2, second_stats), (2, second_norm), (4, keep_logits)])
                dve.wait_ge(logits, TT)


def route(nc, A, S, sem, sems):
    with ExitStack() as ctx:
        sb, ps = stack(ctx, nc, "rt")
        E = EXPERTS
        top = sb("top", [P, TT, 8])
        idx = sb("idx", [P, TT, 8], U32)
        idxf = sb("idxf", [P, TT, TOPK])
        iota_e = sb("iota_e", [P, E])
        iota_t = sb("iota_t", [P, MOE_COLS])
        iota_p = sb("iota_p", [P, 1])
        token = sb("token", [P, TT], I32)
        zero_i = sb("zero_i", [P, MOE_COLS], I32)
        hot = sb("hot", [P, TT, TOPK, E])
        chosen = sb("chosen", [P, TT, E])
        strict = sb("strict", [P, P])
        rank = sb("rank", [P, TT, E])
        count = sb("count", [P, TT, E])
        base = sb("base", [P, TT + 1, E])
        cnt_i = sb("cnt_i", [P, E], I32)
        tiles = sb("tiles", [P, E])
        cum = [sb(f"cum{i}", [P, E]) for i in range(2)]
        place = sb("place", [P, TT, E])
        posf = sb("posf", [P, TT, TOPK])
        cmp = sb("cmp", [P, MOE_COLS, E])
        te = sb("te", [P, MOE_COLS])
        same = sb("same", [P, MOE_COLS])
        rowf = sb("rowf", [P, MOE_COLS])
        sums = sb("sums", [P, TT])
        inv = sb("inv", [P, TT])
        psR = ps("rank", [P, TT * E])
        psC = ps("count", [P, TT * E])
        iotas, zeroed, tops, link, chosen_ready, ranked, diffs, exped, placed, cleared, scattered, listed = (
            sem(f"rt_{n}") for n in ("iotas", "zeroed", "tops", "link", "chosen", "ranked", "diffs", "exp", "placed",
                                     "cleared", "scattered", "listed"))

        with nc.Block() as block:
            @block.gpsimd
            def _(pool):
                pool.iota(iota_e[:], [[1, E]], base=0, channel_multiplier=0, allow_small_or_imprecise_dtypes=True).then_inc(iotas, 1)
                pool.iota(iota_t[:], [[1, MOE_COLS]], base=0, channel_multiplier=0, allow_small_or_imprecise_dtypes=True).then_inc(iotas, 1)
                pool.iota(iota_p[:], [[0, 1]], base=0, channel_multiplier=1, allow_small_or_imprecise_dtypes=True).then_inc(iotas, 1)
                pool.iota(token[:], [[P, TT]], base=0, channel_multiplier=1).then_inc(iotas, 1)
                pool.affine_select(out=strict[:], in_=S.ones[:], pattern=[[1, P]], compare_op=ALU.is_gt, fill=0.0,
                                   base=0, channel_multiplier=-1).then_inc(iotas, 1)
                pool.memset(zero_i[:], 0).then_inc(zeroed, 1)
                pool.wait_ge(iotas, 5)
                pool.wait_ge(placed, 1)
                pool.wait_ge(cleared, 16)
                for t in range(TT):
                    for k in range(TOPK):
                        apart(pool, S)
                        pool.indirect_dma_start(S.slot_token_d, bass.IndirectOffsetOnAxis(ap=S.pos[:, t * TOPK + k:t * TOPK + k + 1], axis=0),
                                                token[:, t:t + 1], None).then_inc(scattered, 16)
                pool.wait_ge(scattered, 16 * TT * TOPK)

            @block.sync
            def _(sp):
                sp.wait_ge(zeroed, 1)
                apart(sp, S)
                sp.dma_start(S.slot_token_d.rearrange("(p t) o -> p (t o)", p=P), zero_i[:]).then_inc(cleared, 16)
                sp.wait_ge(scattered, 16 * TT * TOPK)
                with nc.allow_non_contiguous_dma(reason="a table of 48 KB"):
                    apart(sp, S)
                    sp.dma_start(S.slot_token[:], S.slot_token_d.rearrange("(t p) o -> p (t o)", p=P)).then_inc(listed, 16)
                sp.wait_ge(listed, 16)

            @block.tensor
            def _(pe):
                pe.wait_ge(iotas, 5)
                pe.wait_ge(chosen_ready, 1)
                rhs = chosen[:].rearrange("p t e -> p (t e)")
                pe.matmul(psR[:], strict[:], rhs, start=True, stop=True)
                pe.matmul(psC[:], S.ones[:], rhs, start=True, stop=True).then_inc(ranked, 1)

            @block.scalar
            def _(act):
                act.wait_ge(diffs, 1)
                act.activation(S.probs[:], S.probs[:], ACT.Exp).then_inc(exped, 1)

            @block.vector
            def _(dve):
                for t in range(TT):
                    dve.max(top[:, t, :], S.logits[:, t * E:(t + 1) * E]).then_inc(tops, 1)
                dve.wait_ge(tops, TT)
                for t in range(TT):
                    dve.max_index(idx[:, t, :], top[:, t, :], S.logits[:, t * E:(t + 1) * E]).then_inc(tops, 1)
                chain = Chain(dve, link)
                probs = S.probs[:].rearrange("p (t k) -> p t k", k=TOPK)
                dve.tensor_tensor(probs, top[:, :, 0:TOPK], top[:, :, 0:1].to_broadcast([P, TT, TOPK]), ALU.subtract).then_inc(diffs, 1)
                dve.wait_ge(tops, 2 * TT)
                dve.wait_ge(iotas, 5)
                chain.step(dve.tensor_copy(idxf[:], idx[:, :, 0:TOPK]))
                hot3 = hot[:].rearrange("p t k e -> p (t k) e")
                chain.step(dve.tensor_tensor(hot3, idxf[:].rearrange("p t k -> p (t k)").unsqueeze(2).to_broadcast([P, TT * TOPK, E]),
                                             iota_e[:].unsqueeze(1).to_broadcast([P, TT * TOPK, E]), ALU.is_equal))
                dve.tensor_reduce(chosen[:], hot[:].rearrange("p t k e -> p t e k"), AX.X, ALU.add).then_inc(chosen_ready, 1)
                dve.wait_ge(exped, 1)
                chain.step(dve.tensor_reduce(sums[:], probs, AX.X, ALU.add))
                chain.step(dve.reciprocal(inv[:], sums[:]))
                chain.step(dve.tensor_tensor(probs, probs, inv[:].unsqueeze(2).to_broadcast([P, TT, TOPK]), ALU.mult))
                dve.wait_ge(ranked, 1)
                chain.step(dve.tensor_copy(rank[:].rearrange("p t e -> p (t e)"), psR[:]))
                chain.step(dve.tensor_copy(count[:].rearrange("p t e -> p (t e)"), psC[:]))
                chain.step(dve.memset(base[:, 0, :], 0.0))
                for t in range(TT):
                    chain.step(dve.tensor_tensor(base[:, t + 1, :], base[:, t, :], count[:, t, :], ALU.add))
                chain.step(dve.tensor_scalar(cum[0][:], base[:, TT, :], float(P - 1), None, ALU.add))
                chain.step(dve.tensor_copy(cnt_i[:], cum[0][:]))
                chain.step(dve.tensor_scalar(cnt_i[:], cnt_i[:], 7, None, ALU.arith_shift_right))
                chain.step(dve.tensor_copy(tiles[:], cnt_i[:]))
                chain.step(dve.tensor_copy(cum[0][:], tiles[:]))
                a = 0
                for shift in (1, 2, 4, 8, 16):
                    chain.step(dve.tensor_copy(cum[1 - a][:, 0:shift], cum[a][:, 0:shift]))
                    chain.step(dve.tensor_tensor(cum[1 - a][:, shift:], cum[a][:, shift:], cum[a][:, :E - shift], ALU.add))
                    a = 1 - a
                chain.step(dve.tensor_tensor(tiles[:], cum[a][:], tiles[:], ALU.subtract))
                chain.step(dve.tensor_scalar(tiles[:], tiles[:], float(P), None, ALU.mult))
                chain.step(dve.tensor_tensor(place[:], rank[:], base[:, 0:TT, :], ALU.add))
                chain.step(dve.tensor_tensor(place[:], place[:], tiles[:].unsqueeze(1).to_broadcast([P, TT, E]), ALU.add))
                for k in range(TOPK):
                    chain.step(dve.tensor_tensor(hot[:, :, k, :], hot[:, :, k, :], place[:], ALU.mult))
                chain.step(dve.tensor_reduce(posf[:], hot[:], AX.X, ALU.add))
                dve.tensor_copy(S.pos[:], posf[:].rearrange("p t k -> p (t k)")).then_inc(placed, 1)
                chain.step(dve.tensor_tensor(cmp[:], iota_t[:].unsqueeze(2).to_broadcast([P, MOE_COLS, E]),
                                             cum[a][:].unsqueeze(1).to_broadcast([P, MOE_COLS, E]), ALU.is_ge))
                chain.step(dve.tensor_reduce(te[:], cmp[:], AX.X, ALU.add))
                chain.step(dve.tensor_scalar(te[:], te[:], float(E - 1), None, ALU.min))
                chain.step(dve.memset(same[:, 0:1], 0.0))
                chain.step(dve.tensor_tensor(same[:, 1:], te[:, 1:], te[:, :MOE_COLS - 1], ALU.is_equal))
                chain.step(dve.tensor_scalar(same[:], same[:], SKIP, None, ALU.mult))
                chain.step(dve.tensor_tensor(rowf[:], te[:], same[:], ALU.add))
                chain.step(dve.tensor_copy(S.expert_row[:], rowf[:]))
                for rows, table in ((GU_ROWS, S.gu_row), (DN_ROWS, S.dn_row)):
                    chain.step(dve.scalar_tensor_tensor(out=rowf[:], in0=te[:], scalar=float(rows), in1=same[:], op0=ALU.mult, op1=ALU.add))
                    chain.step(dve.tensor_scalar(rowf[:], rowf[:], iota_p[:], None, ALU.add))
                    chain.step(dve.tensor_copy(table[:], rowf[:]))
                chain.step(dve.tensor_scalar(rowf[:, 0:1], cum[a][:, E - 1:E], 1.0, None, ALU.add))
                chain.step(dve.tensor_copy(cnt_i[:, 0:1], rowf[:, 0:1]))
                chain.step(dve.tensor_scalar(cnt_i[:, 0:1], cnt_i[:, 0:1], 1, None, ALU.arith_shift_right))
                chain.step(dve.tensor_copy(S.rounds[:], cnt_i[:, 0:1]))
                dve.wait_ge(placed, 1)


def experts(nc, A, S, sem, sems):
    with ExitStack() as ctx:
        sb, ps = stack(ctx, nc, "moe")
        F2 = 2 * FF
        KF = FF // P
        NBUF = 4
        GU, DN = 2 * KD, KF
        GL, DL = GU // NBUF, DN // NBUF
        W = 1024

        def pair(name, shape, dt=F32):
            return [sb(f"{name}{i}", shape, dt) for i in range(2)]
        w_gu = [sb(f"w_gu{k}", [P, NBUF * W]) for k in range(GL)]
        w_dn = [sb(f"w_dn{k}", [P, NBUF * W]) for k in range(DL)]
        b_gu = sb("b_gu", [P, F2])
        b_dn = sb("b_dn", [P, D])
        w_hi, w_lo = ([sb(f"{n}{i}", [P, W], F32R) for i in range(NBUF)] for n in ("w_hi", "w_lo"))
        xs = pair("xs", [P, D])
        hT, hT_hi, hT_lo = sb("hT", [P, KD, P]), sb("hT_hi", [P, KD, P], F32R), sb("hT_lo", [P, KD, P], F32R)
        aT_hi, aT_lo = sb("aT_hi", [P, KF, P], F32R), sb("aT_lo", [P, KF, P], F32R)
        gate, up, sig = sb("gate", [P, FF]), sb("up", [P, FF]), sb("sig", [P, FF])
        os_ = pair("out", [P, D])
        tok_i, gu_i, gue_i, dn_i, dne_i = (pair(n, [P, 1], I32) for n in ("tok_i", "gu_i", "gue_i", "dn_i", "dne_i"))
        psG = ps("gu", [P, F2])
        psD = ps("down", [P, D])
        psT = ps("t", [P, KD, P])
        x_in, stored = sems("moe_x", 2), sems("moe_stored", 2)
        gu_in, dn_in = sems("moe_gu_in", GL), sems("moe_dn_in", DL)
        bgu_in, bdn_in, picked, picked_gu, picked_dn, picked_bgu, picked_bdn, gu_hi, gu_lo, dn_hi, dn_lo, gu_used, dn_used, h_turned, modulated, \
            h_hi, h_lo, g_added, u_added, g_cut, u_cut, gated, sig_done, act_ready, a_turned, a_hi, a_lo, out_ready = (
                sem(f"moe_{n}") for n in (
                    "bgu_in", "bdn_in", "picked", "picked_gu", "picked_dn", "picked_bgu", "picked_bdn", "gu_hi", "gu_lo", "dn_hi", "dn_lo", "gu_used",
                    "dn_used", "h_turned", "modulated", "h_hi", "h_lo", "g_added", "u_added", "g_cut", "u_cut", "gated",
                    "sig", "act", "a_turned", "a_hi", "a_lo", "out"))
        LEAD = 3

        def tiles(eng, step, instead=None):
            rounds_less_2 = eng.value_load(S.rounds[0:1, 0:1], min_val=SEQ * TOPK // P // 2, max_val=MOE_ROUNDS - 2)

            def at(r, s, lag, fn, *more):
                q, slot = (s - lag) // 2, (s - lag) % 2
                if isinstance(r, int) and (r + q) * 2 + slot < 0:
                    return
                fn(2 * (r + q) + slot, r + q, slot, *more)

            for r in range(LEAD):
                for s in range(2):
                    step(lambda lag, fn, *more: at(r, s, lag, fn, *more))
            with eng.Fori(LEAD, MOE_ROUNDS) as r:
                with eng.If(r < rounds_less_2 + 2):
                    for s in range(2):
                        step(lambda lag, fn, *more: at(r, s, lag, fn, *more))
                if instead:
                    with eng.Else():
                        for s in range(2):
                            at(r, s, 4, instead)
            return rounds_less_2

        def raw(parts, n):
            return parts[n // NBUF][:, n % NBUF * W:(n % NBUF + 1) * W]

        with nc.Block() as block:
            @block.gpsimd
            def _(pool):
                def fetch_tokens(i, q, s):
                    wait(pool, h_turned, i - 1)
                    apart(pool, S)
                    pool.tensor_copy(tok_i[s][:], S.slot_token[:, bass.ds(i, 1)]).then_inc(picked, 1)
                    pool.wait_ge(picked, i + 1)
                    apart(pool, S)
                    pool.indirect_dma_start(xs[s][:], None, S.xn2_d, bass.IndirectOffsetOnAxis(ap=tok_i[s][:], axis=0)).then_inc(x_in[s], 16)

                def fetch(i, s, picks, idx, idx_table, parts, split, landed, table):
                    wait(pool, landed[-1], 16 * (i - 1))
                    apart(pool, S)
                    pool.tensor_copy(idx[s][:], idx_table[:, bass.ds(i, 1)]).then_inc(picks, 1)
                    pool.wait_ge(picks, i + 1)
                    n = len(parts)
                    for c, part in enumerate(parts):
                        wait(pool, split, NBUF * n * (i - 1) + NBUF * (c + 1))
                        wait(pool, landed[c], 16 * i)
                        apart(pool, S)
                        pool.indirect_dma_start(part[:], None, table, bass.IndirectOffsetOnAxis(ap=idx[s][:], axis=0),
                                                element_offset=c * P * NBUF * W, bounds_check=EXPERTS * n * P - 1,
                                                oob_is_err=False).then_inc(landed[c], 16)

                def fetch_bias(i, s, picks, idx, bias, used, landed, table):
                    wait(pool, landed, 16 * (i - 1))
                    apart(pool, S)
                    pool.tensor_copy(idx[s][:], S.expert_row[:, bass.ds(i, 1)]).then_inc(picks, 1)
                    pool.wait_ge(picks, i + 1)
                    wait(pool, used, i)
                    wait(pool, landed, 16 * i)
                    apart(pool, S)
                    pool.indirect_dma_start(bias[:], None, table, bass.IndirectOffsetOnAxis(ap=idx[s][:], axis=0),
                                            bounds_check=EXPERTS - 1, oob_is_err=False).then_inc(landed, 16)

                def fetch_gu(i, q, s):
                    fetch(i, s, picked_gu, gu_i, S.gu_row, w_gu, gu_lo, gu_in, A["w_gu_t"])
                    fetch_bias(i, s, picked_bgu, gue_i, b_gu, u_added, bgu_in, A["b_gu"])

                def fetch_dn(i, q, s):
                    fetch(i, s, picked_dn, dn_i, S.dn_row, w_dn, dn_lo, dn_in, A["w_down_t"])

                def fetch_bias_dn(i, q, s):
                    fetch_bias(i, s, picked_bdn, dne_i, b_dn, out_ready, bdn_in, A["b_down"])

                def activate(i, q, s):
                    pool.wait_ge(gated, i + 1)
                    pool.wait_ge(sig_done, i + 1)
                    pool.tensor_tensor(up[:], up[:], sig[:], ALU.mult).then_inc(act_ready, 1)

                def step(at):
                    at(0, fetch_tokens)
                    at(3, activate)
                    at(3, fetch_bias_dn)
                    at(1, fetch_gu)
                    at(2, fetch_dn)
                less_2 = tiles(pool, step)
                for s in range(2):
                    pool.wait_ge(x_in[s], 16 * less_2 + 32)
                for c in range(GL):
                    pool.wait_ge(gu_in[c], 32 * less_2 + 48)
                for c in range(DL):
                    pool.wait_ge(dn_in[c], 32 * less_2 + 32)
                pool.wait_ge(bgu_in, 32 * less_2 + 48)
                pool.wait_ge(bdn_in, 32 * less_2 + 16)
                apart(pool, S)

            @block.tensor
            def _(pe):
                def item(out, high, low, n, k, col):
                    for m, (x, w) in enumerate(((high, w_hi), (high, w_lo), (low, w_hi))):
                        for c in range(W // BANK):
                            ins = pe.matmul(out[:, col + c * BANK:col + (c + 1) * BANK], x[:, k, :],
                                            w[n % NBUF][:, c * BANK:(c + 1) * BANK],
                                            start=(k == 0 and m == 0), stop=(k == KD - 1 and m == 2))
                    return ins

                def gate_up(i, q, s, items):
                    for n in items:
                        if n == 0:
                            pe.wait_ge(h_lo, i + 1)
                            wait(pe, u_added, i)
                        pe.wait_ge(gu_lo, GU * i + n + 1)
                        item(psG, hT_hi, hT_lo, n, n // 2, n % 2 * W).then_inc(gu_used, 1)

                def turn_act(i, q, s):
                    pe.wait_ge(act_ready, i + 1)
                    pe.wait_ge(modulated, i + 2)
                    for k in range(KF):
                        last = pe.transpose(psT[:, k, :], up[:, k * P:(k + 1) * P], S.ident[:])
                    last.then_inc(a_turned, 1)

                def turn_h(i, q, s):
                    pe.wait_ge(x_in[s], 16 * (q + 1))
                    wait(pe, a_lo, i - 1)
                    for k in range(KD):
                        last = pe.transpose(psT[:, k, :], xs[s][:, k * P:(k + 1) * P], S.ident[:])
                    last.then_inc(h_turned, 1)

                def down(i, q, s):
                    wait(pe, out_ready, i)
                    pe.wait_ge(a_lo, i + 1)
                    for n in range(DN):
                        pe.wait_ge(dn_lo, DN * i + n + 1)
                        item(psD, aT_hi, aT_lo, n, n, 0).then_inc(dn_used, 1)

                def step(at):
                    at(2, gate_up, range(0, 8))
                    at(3, turn_act)
                    at(2, gate_up, range(8, 16))
                    at(1, turn_h)
                    at(3, down)
                tiles(pe, step)

            @block.scalar
            def _(act):
                def gu(i, q, s, items):
                    for n in items:
                        if n % NBUF == 0:
                            act.wait_ge(gu_in[n // NBUF], 16 * (i + 1))
                        if n >= NBUF:
                            act.wait_ge(gu_used, GU * i + n - NBUF + 1)
                        else:
                            wait(act, dn_used, DN * (i - 2) + DN - NBUF + n + 1)
                        act.copy(w_hi[n % NBUF][:], raw(w_gu, n)).then_inc(gu_hi, 1)

                def dn(i, q, s, items):
                    for n in items:
                        if n % NBUF == 0:
                            act.wait_ge(dn_in[n // NBUF], 16 * (i + 1))
                        if n >= NBUF:
                            act.wait_ge(dn_used, DN * i + n - NBUF + 1)
                        else:
                            act.wait_ge(gu_used, GU * (i + 1) + GU - NBUF + n + 1)
                        act.copy(w_hi[n % NBUF][:], raw(w_dn, n)).then_inc(dn_hi, 1)

                def keep_act(i, q, s):
                    act.wait_ge(a_turned, i + 1)
                    wait(act, dn_used, DN * i)
                    act.copy(aT_hi[:], psT[:]).then_inc(a_hi, 1)

                def modulate(i, q, s):
                    act.wait_ge(h_turned, i + 1)
                    wait(act, h_lo, i)
                    for k in range(KD):
                        last = act.activation(hT[:, k, :], psT[:, k, :], ACT.Identity,
                                              bias=S.modT[:, SH2 + k:SH2 + k + 1], scale=S.modT[:, SC2 + k:SC2 + k + 1])
                    last.then_inc(modulated, 1)
                    act.wait_ge(modulated, i + 1)
                    wait(act, gu_used, GU * i)
                    act.copy(hT_hi[:], hT[:]).then_inc(h_hi, 1)

                def sigmoid(i, q, s):
                    act.wait_ge(g_cut, i + 1)
                    wait(act, act_ready, i)
                    act.activation(sig[:], gate[:], ACT.Sigmoid, scale=SWIGLU_ALPHA).then_inc(sig_done, 1)

                def step(at):
                    at(2, gu, range(0, 5))
                    at(3, sigmoid)
                    at(2, gu, range(5, 12))
                    at(3, keep_act)
                    at(2, gu, range(12, 16))
                    at(3, dn, range(0, 6))
                    at(1, modulate)
                    at(3, dn, range(6, 8))
                tiles(act, step)

            @block.vector
            def _(dve):
                def gu(i, q, s, items):
                    for n in items:
                        dve.wait_ge(gu_hi, GU * i + n + 1)
                        dve.tensor_tensor(w_lo[n % NBUF][:], raw(w_gu, n), w_hi[n % NBUF][:].bitcast(F32), ALU.subtract).then_inc(gu_lo, 1)

                def dn(i, q, s, items):
                    for n in items:
                        dve.wait_ge(dn_hi, DN * i + n + 1)
                        dve.tensor_tensor(w_lo[n % NBUF][:], raw(w_dn, n), w_hi[n % NBUF][:].bitcast(F32), ALU.subtract).then_inc(dn_lo, 1)

                def add_bias(i, q, s):
                    dve.wait_ge(gu_used, GU * (i + 1))
                    dve.wait_ge(bgu_in, 16 * (i + 1))
                    wait(dve, a_turned, i)
                    dve.tensor_tensor(gate[:], psG[:, 0:FF], b_gu[:, 0:FF], ALU.add).then_inc(g_added, 1)
                    dve.tensor_tensor(up[:], psG[:, FF:F2], b_gu[:, FF:F2], ALU.add).then_inc(u_added, 1)

                def swiglu(i, q, s):
                    dve.wait_ge(g_added, i + 1)
                    dve.tensor_scalar(gate[:], gate[:], LIMIT, None, ALU.min).then_inc(g_cut, 1)
                    dve.wait_ge(u_added, i + 1)
                    dve.tensor_scalar(up[:], up[:], LIMIT, -LIMIT, ALU.min, ALU.max).then_inc(u_cut, 1)
                    dve.wait_ge(g_cut, i + 1)
                    dve.wait_ge(u_cut, i + 1)
                    dve.scalar_tensor_tensor(out=up[:], in0=up[:], scalar=1.0, in1=gate[:], op0=ALU.add, op1=ALU.mult).then_inc(gated, 1)

                def low_h(i, q, s):
                    dve.wait_ge(h_hi, i + 1)
                    dve.tensor_tensor(hT_lo[:], hT[:], hT_hi[:].bitcast(F32), ALU.subtract).then_inc(h_lo, 1)

                def low_act(i, q, s):
                    dve.wait_ge(a_hi, i + 1)
                    dve.tensor_tensor(aT_lo[:], psT[:], aT_hi[:].bitcast(F32), ALU.subtract).then_inc(a_lo, 1)

                def finish(i, q, s):
                    dve.wait_ge(dn_used, DN * (i + 1))
                    dve.wait_ge(bdn_in, 16 * (i + 1))
                    wait(dve, stored[s], 16 * q)
                    dve.tensor_tensor(os_[s][:], psD[:], b_dn[:], ALU.add).then_inc(out_ready, 1)

                def step(at):
                    at(2, gu, range(0, 2))
                    at(3, swiglu)
                    at(2, gu, range(2, 4))
                    at(4, finish)
                    at(2, gu, range(4, 12))
                    at(3, low_act)
                    at(2, gu, range(12, 16))
                    at(3, dn, range(0, 4))
                    at(2, add_bias)
                    at(3, dn, range(4, 6))
                    at(1, low_h)
                    at(3, dn, range(6, 8))
                tiles(dve, step)

            @block.sync
            def _(sp):
                def store(i, q, s):
                    sp.wait_ge(out_ready, i + 1)
                    apart(sp, S)
                    sp.dma_start(S.slot_out_d[bass.ds(i * P, P), :], os_[s][:]).then_inc(stored[s], 16)

                def fill(i, q, s):
                    sp.wait_ge(stored[s], 16 * q)
                    apart(sp, S)
                    sp.dma_start(S.slot_out_d[bass.ds(i * P, P), :], os_[s][:]).then_inc(stored[s], 16)
                tiles(sp, lambda at: at(4, store), fill)
                for s in range(2):
                    sp.wait_ge(stored[s], 8 * MOE_TILES)


def combine(nc, A, S, sem, sems, out):
    with ExitStack() as ctx:
        sb, _ = stack(ctx, nc, "fin")

        def pair(name, shape, dt=F32):
            return [sb(f"{name}{i}", shape, dt) for i in range(2)]
        rows = [pair(f"rows{k}_", [P, D]) for k in range(TOPK)]
        idx = pair("idx", [P, TOPK], I32)
        x1, acc, yo = pair("x1", [P, D]), pair("acc", [P, D]), pair("y", [P, D])
        st, mv, sd, rs = pair("st", [P, 2, 6]), pair("mv", [P, 2]), pair("sd", [P, 1]), pair("rs", [P, 1])
        lg, lb = sb("ln_g", [P, D]), sb("ln_b", [P, D])
        par_in, picked, link, stats, root, normed, scaled, ready = (sem(f"fin_{n}") for n in (
            "params", "picked", "link", "stats", "root", "normed", "scaled", "ready"))
        rows_in, x1_in, stored = sems("fin_rows", 2), sems("fin_x1", 2), sems("fin_stored", 2)
        STEPS = 8

        with nc.Block() as block:
            @block.gpsimd
            def _(pool):
                def gather(q, s):
                    t = 2 * q + s
                    wait(pool, stats, t - 1)
                    apart(pool, S)
                    pool.tensor_copy(idx[s][:], S.pos[:, bass.ds(t * TOPK, TOPK)]).then_inc(picked, 1)
                    pool.wait_ge(picked, t + 1)
                    for k in range(TOPK):
                        apart(pool, S)
                        pool.indirect_dma_start(rows[k][s][:], None, S.slot_out_d,
                                                bass.IndirectOffsetOnAxis(ap=idx[s][:, k:k + 1], axis=0)).then_inc(rows_in[s], 16)

                def affine(q, s):
                    t = 2 * q + s
                    pool.wait_ge(normed, t + 1)
                    wait(pool, stored[s], 16 * q)
                    pool.tensor_tensor(yo[s][:], acc[s][:], lg[:], ALU.mult).then_inc(scaled, 1)
                    pool.wait_ge(scaled, t + 1)
                    pool.tensor_tensor(yo[s][:], yo[s][:], lb[:], ALU.add).then_inc(ready, 1)
                pool.wait_ge(par_in, 32)
                pipeline(pool, TT, 2, [(0, gather), (1, affine)])

            @block.sync
            def _(sp):
                apart(sp, S)
                for dst, name in ((lg, "ln2_g"), (lb, "ln2_b")):
                    sp.dma_start(dst[:], A[name][0].partition_broadcast(P)).then_inc(par_in, 16)

                def load(q, s):
                    t = 2 * q + s
                    wait(sp, stats, t - 1)
                    apart(sp, S)
                    sp.dma_start(x1[s][:], S.x1_d[bass.ds(t * P, P), :]).then_inc(x1_in[s], 16)

                def store(q, s):
                    t = 2 * q + s
                    sp.wait_ge(ready, t + 1)
                    apart(sp, S)
                    sp.dma_start(out[bass.ds(t * P, P), :], yo[s][:]).then_inc(stored[s], 16)
                pipeline(sp, TT, 2, [(0, load), (2, store)])
                for s in range(2):
                    sp.wait_ge(stored[s], 8 * TT)

            @block.scalar
            def _(act):
                def first_root(q, s):
                    act.wait_ge(stats, 2 * q + s + 1)
                    act.activation(sd[s][:], mv[s][:, 1:2], ACT.Sqrt, bias=S.eps[:]).then_inc(root, 1)
                pipeline(act, TT, 2, [(0, first_root)])

            @block.vector
            def _(dve):
                chain = Chain(dve, link)

                def blend(q, s):
                    t = 2 * q + s
                    chain.item(t, STEPS)
                    dve.wait_ge(rows_in[s], 16 * TOPK * (q + 1))
                    wait(dve, ready, t - 1)
                    chain.step(dve.tensor_scalar(acc[s][:], rows[0][s][:], S.probs[:, bass.ds(t * TOPK, 1)], None, ALU.mult))
                    for k in range(1, TOPK):
                        chain.step(dve.scalar_tensor_tensor(out=acc[s][:], in0=rows[k][s][:], scalar=S.probs[:, bass.ds(t * TOPK + k, 1)],
                                                            in1=acc[s][:], op0=ALU.mult, op1=ALU.add))
                    chain.step(dve.tensor_tensor(acc[s][:], acc[s][:], S.g2[:], ALU.mult))
                    dve.wait_ge(x1_in[s], 16 * (q + 1))
                    chain.step(dve.scalar_tensor_tensor(out=acc[s][:], in0=x1[s][:], scalar=DN_ALPHA, in1=acc[s][:], op0=ALU.mult, op1=ALU.add))
                    dve.bn_stats(st[s][:, 0, :], acc[s][:, 0:BANK])
                    chain.step(dve.bn_stats(st[s][:, 1, :], acc[s][:, BANK:D]))
                    apart(dve, S)
                    dve.bn_aggr(mv[s][:], st[s][:]).then_inc(stats, 1)
                    dve.wait_ge(root, t + 1)
                    chain.step(dve.reciprocal(rs[s][:], sd[s][:]))
                    dve.tensor_scalar(acc[s][:], acc[s][:], mv[s][:, 0:1], rs[s][:], ALU.subtract, ALU.mult).then_inc(normed, 1)
                    chain.end()
                pipeline(dve, TT, 2, [(0, blend)])


def build(nc, A, out):
    with ExitStack() as top:
        in_use = []

        def sem(name):
            in_use.append(nc.alloc_semaphore(name=name))
            return in_use[-1]

        def release_semaphores():
            nc.clear_and_free_semaphores(in_use)
            in_use.clear()
            nc.all_engine_barrier()

        def sems(name, n):
            return [sem(f"{name}{i}") for i in range(n)]

        def dram(name, shape, dt=F32):
            return nc.dram_tensor(name, shape, dt).ap()

        S = Shared()
        S.passed = nc.alloc_semaphore(name="passed")
        S.rows_d = dram("rows_scratch", (N_ROWS * P, SEQ))
        S.acum_d = dram("acum_scratch", (HEADS, SEQ))
        S.y_d = dram("y_scratch", (INNER, SEQ))
        S.mixin_d = dram("mixin_scratch", (D, SEQ))
        S.x1_d = dram("x1_scratch", (SEQ, D))
        S.xn2_d = dram("xn2_scratch", (SEQ, D))
        S.slot_token_d = dram("slot_token_scratch", (SLOTS, 1), I32)
        S.slot_out_d = dram("slot_out_scratch", (MOE_TILES * P, D))

        sb, _ = stack(top, nc, "keep")
        S.ident = sb("ident", [P, P])
        S.tri = sb("tri", [P, P])
        S.ones = sb("ones", [P, P])
        S.eps = sb("eps", [P, 1])
        S.modT = sb("modT", [P, 6 * KD])
        S.g1 = sb("g1", [P, D])
        S.g2 = sb("g2", [P, D])
        S.logits = sb("logits", [P, TT * EXPERTS])
        S.probs = sb("probs", [P, TT * TOPK])
        S.pos = sb("pos", [P, TT * TOPK], I32)
        S.slot_token = sb("slot_token", [P, MOE_COLS], I32)
        S.gu_row = sb("gu_row", [P, MOE_COLS], I32)
        S.dn_row = sb("dn_row", [P, MOE_COLS], I32)
        S.rounds = sb("rounds", [P, 1], I32)
        S.expert_row = sb("expert_row", [P, MOE_COLS], I32)

        modulation(nc, A, S, sem, sems)
        with ExitStack() as ctx:
            sb, _ = stack(ctx, nc, "table")
            S.dt = sb("dt", [P, TT * HEADS])
            S.acum = sb("acum", [P, TT * HEADS])
            S.decay = sb("decay", [P, TT * HEADS])
            S.chunk_decay = sb("chunk_decay", [P, TT * HEADS])
            with ExitStack() as hctx:
                sb, _ = stack(hctx, nc, "h")
                h_hi = sb("hi", [P, KD, SEQ], F32R)
                h_lo = sb("lo", [P, KD, SEQ], F32R)
                norm_in(nc, A, S, sem, sems, h_hi, h_lo)
                decay(nc, A, S, sem, sems, h_hi, h_lo)
                project(nc, A, S, sem, sems, h_hi, h_lo)
            ssd(nc, A, S, sem, sems)
        release_semaphores()
        branches(nc, A, S, sem, sems)
        mix_out(nc, A, S, sem, sems)
        route(nc, A, S, sem, sems)
        experts(nc, A, S, sem, sems)
        combine(nc, A, S, sem, sems, out)
        in_use.append(S.passed)
        release_semaphores()


def layouts(i):
    import numpy as np
    z1 = INNER
    s1 = z1 + N_XBC * P
    s2 = s1 + HEADS
    w_in = i["w_in"][0]
    cols = [w_in[:, 0:s1]]
    short = w_in[:, s2:s2 + 3 * D].reshape(D, 3, N_SC, P)[:, [1, 2, 0]]
    cols.append(short.transpose(0, 2, 1, 3).reshape(D, 3 * D))
    cols.append(w_in[:, s2 + 3 * D:])
    w_main = np.concatenate(cols, axis=1)

    def col_tiles(w, width=P):
        rows, n = w.shape
        return w.reshape(rows // P, P, n // width, width).transpose(2, 1, 0, 3).reshape(n // width * P, rows // P * width)

    def expert_rows(w, rows):
        e, k, n = w.shape
        return w.reshape(e, rows // P, k // rows, P, n).transpose(0, 1, 3, 2, 4).reshape(e * rows, k // rows * n)

    def columns(v):
        return v.reshape(-1, P).T
    return {
        "x": i["x"][0],
        "cT": columns(i["c"][0]),
        "w_ada_t": col_tiles(i["w_ada"][0], BANK).reshape(6 * D // BANK, P, KD * BANK),
        "b_adaT": columns(i["b_ada"][0]),
        "b_ada": i["b_ada"],
        "w_in_t": col_tiles(w_main),
        "w_dt": col_tiles(w_in[:, s1:s2], HEADS),
        "conv_w": i["conv_ssd_w"][0].reshape(CONV, N_XBC, P).transpose(2, 1, 0).reshape(P, N_XBC * CONV),
        "conv_b": columns(i["conv_ssd_b"][0]),
        "short_w": i["conv_short_w"][0].reshape(SCONV, N_SC, P).transpose(2, 1, 0).reshape(P, N_SC * SCONV),
        "b_gateT": columns(i["b_gate"][0]),
        "dt_bias": i["dt_bias"],
        "a_log": i["a_log"],
        "d_skipT": columns(np.repeat(i["d_skip"][0], HD)),
        "ssd_norm_wT": columns(i["ssd_norm_w"][0]),
        "w_branch_t": col_tiles(np.concatenate([i["w_ssd_out"][0], i["w_short_out"][0]], axis=0)),
        "w_o": i["w_o"][0],
        "ln1_g": i["ln1_g"], "ln1_b": i["ln1_b"],
        "w_router_t": col_tiles(i["w_router"][0], EXPERTS),
        "b_router": i["b_router"],
        "w_gu_t": expert_rows(i["w_gu"][0], GU_ROWS),
        "b_gu": i["b_gu"][0],
        "w_down_t": expert_rows(i["w_down"][0], DN_ROWS),
        "b_down": i["b_down"][0],
        "ln2_g": i["ln2_g"], "ln2_b": i["ln2_b"],
    }


def kernel(**inputs):
    import numpy as np
    from concourse import bacc
    from concourse.bass_utils import run_bass_kernel_spmd

    nc = bacc.Bacc("TRN2", target_bir_lowering=False, num_devices=1)
    arrays, A = {}, {}
    for name, a in layouts({k: np.asarray(v) for k, v in inputs.items()}).items():
        a = np.ascontiguousarray(a)
        arrays[f"in_{name}"] = a
        A[name] = nc.dram_tensor(f"in_{name}", a.shape, mybir.dt.from_np(a.dtype), kind="ExternalInput").ap()
    out = nc.dram_tensor("out_x", (SEQ, D), F32, kind="ExternalOutput").ap()
    build(nc, A, out)
    r = run_bass_kernel_spmd(nc, [arrays], core_ids=[0])
    return r.results[0]["out_x"].reshape(1, SEQ, D)
```

```python
from contextlib import ExitStack

import concourse.bass as bass
from concourse import mybir

F32 = mybir.dt.float32
F32R = mybir.dt.float32r
I32 = mybir.dt.int32
U32 = mybir.dt.uint32
ALU = mybir.AluOpType
ACT = mybir.ActivationFunctionType
AX = mybir.AxisListType

P = 128
D = 1024
SEQ = 2048
KD = D // P
TT = SEQ // P
INNER = 2 * D
HEADS = 32
HD = 64
GROUPS = 4
HG = HEADS // GROUPS
NSTATE = 128
CONV = 4
SCONV = 3
EXPERTS = 32
TOPK = 4
FF = D
LIMIT = 7.0
SWIGLU_ALPHA = 1.702
DN_ALPHA = 2.0 ** 0.25
EPS = 1e-5
BANK = 512

N_Z = INNER // P
N_XBC = (INNER + 2 * GROUPS * NSTATE) // P
N_SC = D // P
N_GATE = 2 * D // P
N_PROJ = N_Z + N_XBC + 3 * N_SC + N_GATE
ROW_Z = 0
ROW_XBC = N_Z
ROW_Q = ROW_XBC + N_XBC
ROW_GATE = ROW_Q + N_SC
N_ROWS = ROW_GATE + N_GATE

MOE_TILES = SEQ * TOPK // P + EXPERTS
MOE_ROUNDS = (MOE_TILES + 4) // 2
MOE_COLS = 2 * MOE_ROUNDS
SLOTS = MOE_COLS * P
GU_ROWS = D * 2 * FF // 4096
DN_ROWS = FF * D // 4096
SH1, SC1 = 0, KD
ADA_G1, ADA_SH2, ADA_SC2, ADA_G2 = range(4)
ADA_FIRST = 2 * D // BANK


class Shared:
    pass


def wait(eng, sem, value):
    if isinstance(value, int) and value <= 0:
        return
    eng.wait_ge(sem, value)


def apart(eng, S):
    eng.sem_inc(S.passed, 1)


def pipeline(eng, n, unroll, stages):
    most = max(lag for lag, _ in stages)
    rounds = -(-(n + most) // unroll)
    lead = -(-most // unroll) + 1
    full = n // unroll

    def one(r):
        for s in range(unroll):
            for lag, fn in stages:
                q, slot = (s - lag) // unroll, (s - lag) % unroll
                if isinstance(r, int) and not 0 <= (r + q) * unroll + slot < n:
                    continue
                fn(r + q, slot)

    if full - lead < 2:
        for r in range(rounds):
            one(r)
        return
    for r in range(lead):
        one(r)
    with eng.Fori(lead, full) as r:
        one(r)
    for r in range(full, rounds):
        one(r)


class Chain:

    def __init__(self, eng, sem):
        self.eng, self.sem, self.n, self.k = eng, sem, 0, 0

    def item(self, i, per_item):
        self.n, self.k, self.per = i * per_item, 0, per_item

    def step(self, ins):
        self.k += 1
        ins.then_inc(self.sem, 1)
        self.eng.wait_ge(self.sem, self.n + self.k)

    def end(self):
        assert self.k == self.per, (self.k, self.per)



def stack(ctx, nc, phase):
    def sb(name, shape, dt=F32):
        return ctx.enter_context(nc.sbuf_tensor(f"{phase}_{name}", shape, dt))

    def ps(name, shape, dt=F32):
        return ctx.enter_context(nc.psum_tensor(f"{phase}_ps_{name}", shape, dt))
    return sb, ps


def product(pe, out, lhs, rhs, steps):
    parts = ((0, 0), (0, 1), (1, 0))
    for k in range(steps):
        for n, (a, b) in enumerate(parts):
            last = pe.matmul(out, lhs[a](k), rhs[b](k), start=(k == 0 and n == 0), stop=(k == steps - 1 and n == 2))
    return last


def modulation(nc, A, S, sem, sems):
    with ExitStack() as ctx:
        sb, ps = stack(ctx, nc, "mod")
        cT = sb("cT", [P, KD])
        rows = sb("rows", [1, ADA_FIRST * BANK])
        wa = [sb(f"w{b}", [P, KD, BANK]) for b in range(ADA_FIRST)]
        psR = [ps(f"row{b}", [P, BANK]) for b in range(ADA_FIRST)]
        psT = ps("cols", [P, BANK])
        small_in, consts, silu_done, row_done, row_added, turned, table = (
            sem(f"mod_{n}") for n in ("small_in", "consts", "silu", "row", "row_added", "turned", "table"))
        w_in = sems("mod_w", ADA_FIRST)

        with nc.Block() as block:
            @block.sync
            def _(sp):
                sp.dma_start(cT[:], A["cT"]).then_inc(small_in, 16)
                sp.dma_start(rows[:], A["b_ada"][0:1, 0:ADA_FIRST * BANK]).then_inc(small_in, 16)
                for b in range(ADA_FIRST):
                    sp.dma_start(wa[b][:], A["w_ada_t"][b].rearrange("p (k n) -> p k n", k=KD)).then_inc(w_in[b], 16)

            @block.gpsimd
            def _(pool):
                pool.memset(S.ones[:], 1.0).then_inc(consts, 1)
                pool.memset(S.eps[:], EPS).then_inc(consts, 1)
                pool.wait_ge(consts, 2)
                pool.affine_select(out=S.tri[:], in_=S.ones[:], pattern=[[1, P]], compare_op=ALU.is_ge, fill=0.0,
                                   base=0, channel_multiplier=-1).then_inc(consts, 1)
                pool.affine_select(out=S.ident[:], in_=S.ones[:], pattern=[[1, P]], compare_op=ALU.is_equal, fill=0.0,
                                   base=0, channel_multiplier=-1).then_inc(consts, 1)
                pool.wait_ge(consts, 4)

            @block.scalar
            def _(act):
                act.wait_ge(small_in, 32)
                act.activation(S.silu_c[:], cT[:], ACT.Silu).then_inc(silu_done, 1)

            @block.tensor
            def _(pe):
                pe.wait_ge(silu_done, 1)
                for b in range(ADA_FIRST):
                    pe.wait_ge(w_in[b], 16)
                    for k in range(KD):
                        last = pe.matmul(psR[b][0:1, :], S.silu_c[:, k:k + 1], wa[b][:, k, :], start=(k == 0), stop=(k == KD - 1))
                    last.then_inc(row_done, 1)
                pe.wait_ge(consts, 4)
                for b in range(ADA_FIRST):
                    pe.wait_ge(row_added, b + 1)
                    for j in range(b * BANK // P, (b + 1) * BANK // P):
                        last = pe.matmul(psT[:, j:j + 1], rows[:, j * P:(j + 1) * P], S.ones[0:1, 0:1], start=True, stop=True)
                last.then_inc(turned, 1)

            @block.vector
            def _(dve):
                dve.wait_ge(small_in, 32)
                for b in range(ADA_FIRST):
                    dve.wait_ge(row_done, b + 1)
                    part = rows[:, b * BANK:(b + 1) * BANK]
                    dve.tensor_tensor(part, psR[b][0:1, :], part, ALU.add).then_inc(row_added, 1)
                dve.wait_ge(turned, 1)
                dve.tensor_copy(S.modT[:, SH1:SH1 + KD], psT[:, SH1:SH1 + KD]).then_inc(table, 1)
                dve.tensor_scalar(S.modT[:, SC1:SC1 + KD], psT[:, SC1:SC1 + KD], 1.0, None, ALU.add).then_inc(table, 1)
                dve.wait_ge(table, 2)


def norm_in(nc, A, S, sem, sems, h_hi, h_lo):
    with ExitStack() as ctx:
        sb, ps = stack(ctx, nc, "nin")
        R = 4
        xt = [sb(f"x{i}", [P, D]) for i in range(R)]
        st = [sb(f"st{i}", [P, 2, 6]) for i in range(R)]
        mv = [sb(f"mv{i}", [P, 2]) for i in range(R)]
        sd = [sb(f"sd{i}", [P, 1]) for i in range(R)]
        rs = [sb(f"rs{i}", [P, 1]) for i in range(R)]
        ht = [sb(f"h{i}", [P, KD, P]) for i in range(2)]
        wa = [sb(f"w{i}", [P, KD, BANK]) for i in range(2)]
        row = [sb(f"row{i}", [1, BANK]) for i in range(2)]
        kept = [sb(f"kept{i}", [1, BANK]) for i in range(2)]
        psT = [ps(f"t{i}", [P, KD, P]) for i in range(2)]
        psR = [ps(f"row{i}", [P, BANK]) for i in range(2)]
        x_in, w_in, bias_in, row_out = sems("nin_x", R), sems("nin_w", 2), sems("nin_bias", 2), sems("nin_row_out", 2)
        halves, stats, sqrt_done, inverse, normed, transposed, modulated, rounded, split, row_done, row_kept, row_added = (
            sem(f"nin_{n}") for n in ("halves", "stats", "sqrt", "inverse", "normed", "transposed", "modulated",
                                      "rounded", "split", "row", "row_kept", "row_added"))
        plus_one = sem("nin_plus_one")
        BLOCKS = 6 * D // BANK - ADA_FIRST
        assert 2 * BLOCKS == TT

        with nc.Block() as block:
            @block.sync
            def _(sp):
                def load(q, s):
                    t = R * q + s
                    wait(sp, transposed, t - R + 1)
                    apart(sp, S)
                    sp.dma_start(xt[s][:], A["x"][bass.ds(t * P, P), :]).then_inc(x_in[s], 16)
                pipeline(sp, TT, R, [(0, load)])

            @block.gpsimd
            def _(pool):
                def load(i):
                    s, b = i % 2, ADA_FIRST + i
                    wait(pool, row_done, i - 1)
                    pool.dma_start(wa[s][:], A["w_ada_t"][b].rearrange("p (k n) -> p k n", k=KD)).then_inc(w_in[s], 16)
                    wait(pool, row_out[s], 16 * (i // 2))
                    pool.dma_start(row[s][:], A["b_ada"][0:1, b * BANK:(b + 1) * BANK]).then_inc(bias_in[s], 16)

                def add(i):
                    s = i % 2
                    pool.wait_ge(bias_in[s], 16 * (i // 2 + 1))
                    pool.wait_ge(row_kept, i + 1)
                    if i * BANK // D == ADA_SC2:
                        pool.tensor_tensor(row[s][:], row[s][:], S.ones[0:1, 0:1].to_broadcast([1, BANK]), ALU.add).then_inc(plus_one, 1)
                        pool.wait_ge(plus_one, i - ADA_SC2 * D // BANK + 1)
                    pool.tensor_tensor(row[s][:], kept[s][:], row[s][:], ALU.add).then_inc(row_added, 1)
                    pool.wait_ge(row_added, i + 1)
                    pool.dma_start(S.ada_d[0:1, i * BANK:(i + 1) * BANK], row[s][:]).then_inc(row_out[s], 16)

                load(0)
                for i in range(BLOCKS):
                    if i + 1 < BLOCKS:
                        load(i + 1)
                    add(i)
                for s in range(2):
                    pool.wait_ge(row_out[s], 16 * BLOCKS // 2)

            @block.vector
            def _(dve):
                def statistics(q, s):
                    t = R * q + s
                    dve.wait_ge(x_in[s], 16 * (q + 1))
                    for half in range(2):
                        dve.bn_stats(st[s][:, half, :], xt[s][:, half * BANK:(half + 1) * BANK]).then_inc(halves, 1)
                    dve.wait_ge(halves, 2 * (t + 1))
                    apart(dve, S)
                    dve.bn_aggr(mv[s][:], st[s][:]).then_inc(stats, 1)

                def norm(q, s):
                    t = R * q + s
                    dve.wait_ge(sqrt_done, t + 1)
                    dve.reciprocal(rs[s][:], sd[s][:]).then_inc(inverse, 1)
                    dve.wait_ge(inverse, t + 1)
                    dve.tensor_scalar(xt[s][:], xt[s][:], mv[s][:, 0:1], rs[s][:], ALU.subtract,
                                      ALU.mult).then_inc(normed, 1)

                def low(q, s):
                    t = R * q + s
                    dve.wait_ge(rounded, t + 1)
                    cols = bass.ds(t * P, P)
                    dve.tensor_tensor(h_lo[:, :, cols], ht[s % 2][:], h_hi[:, :, cols].bitcast(F32),
                                      ALU.subtract).then_inc(split, 1)
                pipeline(dve, TT, R, [(0, statistics), (1, norm), (3, low)])
                dve.wait_ge(split, TT)

            @block.tensor
            def _(pe):
                def turn(q, s):
                    t = R * q + s
                    pe.wait_ge(normed, t + 1)
                    wait(pe, modulated, t - 1)
                    for k in range(KD):
                        last = pe.transpose(psT[s % 2][:, k, :], xt[s][:, k * P:(k + 1) * P], S.ident[:])
                    last.then_inc(transposed, 1)

                def ada_row(q, s):
                    if s % 2:
                        r = s // 2
                        pe.wait_ge(w_in[r], 16 * (q + 1))
                        wait(pe, row_kept, 2 * q + r - 1)
                        for k in range(KD):
                            last = pe.matmul(psR[r][0:1, :], S.silu_c[:, k:k + 1], wa[r][:, k, :], start=(k == 0), stop=(k == KD - 1))
                        last.then_inc(row_done, 1)
                pipeline(pe, TT, R, [(0, turn), (0, ada_row)])

            @block.scalar
            def _(act):
                def root(q, s):
                    act.wait_ge(stats, R * q + s + 1)
                    act.activation(sd[s][:], mv[s][:, 1:2], ACT.Sqrt, bias=S.eps[:]).then_inc(sqrt_done, 1)

                def modulate(q, s):
                    t, half = R * q + s, s % 2
                    act.wait_ge(transposed, t + 1)
                    wait(act, split, t - 1)
                    for k in range(KD):
                        last = act.activation(ht[half][:, k, :], psT[half][:, k, :], ACT.Identity,
                                              bias=S.modT[:, SH1 + k:SH1 + k + 1], scale=S.modT[:, SC1 + k:SC1 + k + 1])
                    last.then_inc(modulated, 1)
                    act.wait_ge(modulated, t + 1)
                    act.copy(h_hi[:, :, bass.ds(t * P, P)], ht[half][:]).then_inc(rounded, 1)

                def keep_row(q, s):
                    if s % 2:
                        r = s // 2
                        act.wait_ge(row_done, 2 * q + r + 1)
                        wait(act, row_added, 2 * q + r - 1)
                        act.copy(kept[r][:], psR[r][0:1, :]).then_inc(row_kept, 1)
                pipeline(act, TT, R, [(0, root), (2, modulate), (2, keep_row)])


def decay(nc, A, S, sem, sems, h_hi, h_lo):
    with ExitStack() as ctx:
        sb, ps = stack(ctx, nc, "dec")
        W = TT * HEADS
        w = sb("w", [P, KD, HEADS])
        w_hi = sb("w_hi", [P, KD, HEADS], F32R)
        w_lo = sb("w_lo", [P, KD, HEADS], F32R)
        bias = sb("bias", [P, HEADS])
        alog = sb("alog", [P, HEADS])
        a = sb("a", [P, HEADS])
        v = sb("v", [P, W])
        av = sb("av", [P, W])
        e = sb("e", [P, W])
        u = sb("u", [P, W])
        um = sb("um", [P, W])
        zero = sb("zero", [P, W])
        ln = sb("ln", [P, W])
        la = sb("la", [P, W])
        acT = sb("acT", [HEADS, SEQ])
        psD = ps("dt", [P, W])
        psA = ps("acum", [P, W])
        psE = ps("total", [P, W])
        psAT = ps("acumT", [HEADS, SEQ])
        loads, w_rounded, w_split, dt_done, link, exp_a, exp_v, ln_u, la_ready, sums, turned, copied, stored, tail = (
            sem("dec_loads"), sem("dec_w_rounded"), sem("dec_w_split"), sem("dec_dt"), sem("dec_link"), sem("dec_exp_a"),
            sem("dec_exp_v"), sem("dec_ln"), sem("dec_la"), sem("dec_sums"), sem("dec_turned"), sem("dec_copied"),
            sem("dec_stored"), sem("dec_tail"))
        heads_done, heads_kept = sem("dec_heads_done"), sem("dec_heads_kept")

        def per_tile(t):
            return t[:].rearrange("p (t h) -> p t h", h=HEADS)

        with nc.Block() as block:
            @block.sync
            def _(sp):
                sp.dma_start(w[:], A["w_dt"].rearrange("p (k n) -> p k n", k=KD)).then_inc(loads, 16)
                sp.dma_start(bias[:], A["dt_bias"][0].partition_broadcast(P)).then_inc(loads, 16)
                sp.dma_start(alog[:], A["a_log"][0].partition_broadcast(P)).then_inc(loads, 16)
                sp.wait_ge(copied, 1)
                apart(sp, S)
                sp.dma_start(S.acum_d, acT[:]).then_inc(stored, 16)
                sp.wait_ge(stored, 16)

            @block.tensor
            def _(pe):
                pe.wait_ge(w_split, 1)
                for b in range(SEQ // BANK):
                    product(pe, psAT[:, b * BANK:(b + 1) * BANK], [lambda k, x=x: x[:, k, :] for x in (w_hi, w_lo)],
                            [lambda k, x=x: x[:, k, b * BANK:(b + 1) * BANK] for x in (h_hi, h_lo)], KD).then_inc(heads_done, 1)
                for t in range(TT):
                    pe.wait_ge(heads_kept, t * P // BANK + 1)
                    last = pe.transpose(psD[:, t * HEADS:(t + 1) * HEADS], acT[:, t * P:(t + 1) * P], S.ident[0:HEADS, 0:HEADS])
                last.then_inc(dt_done, 1)
                pe.wait_ge(la_ready, 1)
                pe.matmul(psA[:], S.tri[:], la[:], start=True, stop=True)
                pe.matmul(psE[:], S.ones[:], la[:], start=True, stop=True).then_inc(sums, 1)
                for t in range(TT):
                    last = pe.matmul(psAT[:, t * P:(t + 1) * P], la[:, t * HEADS:(t + 1) * HEADS], S.tri[:],
                                     start=True, stop=True)
                last.then_inc(turned, 1)

            @block.scalar
            def _(act):
                act.wait_ge(loads, 48)
                act.copy(w_hi[:], w[:]).then_inc(w_rounded, 1)
                act.activation(a[:], alog[:], ACT.Exp).then_inc(exp_a, 1)
                for b in range(SEQ // BANK):
                    act.wait_ge(heads_done, b + 1)
                    act.copy(acT[:, b * BANK:(b + 1) * BANK], psAT[:, b * BANK:(b + 1) * BANK]).then_inc(heads_kept, 1)
                act.wait_ge(link, 2)
                act.activation(e[:], av[:], ACT.Exp, scale=-1.0).then_inc(exp_v, 1)
                act.wait_ge(link, 3)
                act.activation(ln[:], u[:], ACT.Ln).then_inc(ln_u, 1)
                act.wait_ge(sums, 1)
                act.activation(S.chunk_decay[:], psE[:], ACT.Exp).then_inc(tail, 1)
                act.wait_ge(link, 12)
                act.activation(S.decay[:], v[:], ACT.Exp).then_inc(tail, 1)
                act.wait_ge(turned, 1)
                act.copy(acT[:], psAT[:]).then_inc(copied, 1)
                act.wait_ge(tail, 2)

            @block.vector
            def _(dve):
                dve.wait_ge(w_rounded, 1)
                dve.tensor_tensor(w_lo[:], w[:], w_hi[:].bitcast(F32), ALU.subtract).then_inc(w_split, 1)
                chain = Chain(dve, link)
                dve.wait_ge(loads, 48)
                dve.wait_ge(dt_done, 1)
                chain.step(dve.tensor_tensor(per_tile(v), per_tile(psD), bias[:].unsqueeze(1).to_broadcast([P, TT, HEADS]), ALU.add))
                chain.step(dve.scalar_tensor_tensor(out=av[:], in0=v[:], scalar=-1.0, in1=v[:], op0=ALU.mult, op1=ALU.max))
                dve.wait_ge(exp_v, 1)
                chain.step(dve.tensor_scalar(u[:], e[:], 1.0, None, ALU.add))
                chain.step(dve.tensor_scalar(um[:], u[:], -1.0, None, ALU.add))
                chain.step(dve.tensor_scalar(zero[:], um[:], 0.0, None, ALU.is_equal))
                chain.step(dve.tensor_tensor(um[:], um[:], zero[:], ALU.add))
                dve.wait_ge(ln_u, 1)
                chain.step(dve.tensor_tensor(ln[:], ln[:], zero[:], ALU.add))
                chain.step(dve.reciprocal(um[:], um[:]))
                chain.step(dve.tensor_tensor(ln[:], ln[:], um[:], ALU.mult))
                chain.step(dve.tensor_tensor(ln[:], ln[:], e[:], ALU.mult))
                chain.step(dve.scalar_tensor_tensor(out=S.dt[:], in0=v[:], scalar=0.0, in1=ln[:], op0=ALU.max, op1=ALU.add))
                dve.wait_ge(exp_a, 1)
                dve.scalar_tensor_tensor(out=per_tile(la), in0=per_tile(S.dt), scalar=-1.0,
                                         in1=a[:].unsqueeze(1).to_broadcast([P, TT, HEADS]), op0=ALU.mult,
                                         op1=ALU.mult).then_inc(la_ready, 1)
                dve.wait_ge(sums, 1)
                dve.tensor_copy(S.acum[:], psA[:]).then_inc(la_ready, 1)
                dve.wait_ge(la_ready, 2)
                dve.wait_ge(tail, 1)
                chain.step(dve.tensor_tensor(v[:], psE[:], S.acum[:], ALU.subtract))


def project(nc, A, S, sem, sems, h_hi, h_lo):
    with ExitStack() as ctx:
        sb, ps = stack(ctx, nc, "prj")
        TB = SEQ // BANK
        w = [sb(f"w{i}", [P, KD, P]) for i in range(2)]
        w_hi = [sb(f"w_hi{i}", [P, KD, P], F32R) for i in range(2)]
        w_lo = [sb(f"w_lo{i}", [P, KD, P], F32R) for i in range(2)]
        ob = [sb(f"out{i}", [P, SEQ]) for i in range(2)]
        c_sb = sb("c", [P, SEQ])
        cx = sb("cx", [P, SEQ])
        cw = sb("conv_w", [P, N_XBC * CONV])
        cb = sb("conv_b", [P, N_XBC])
        sw = sb("short_w", [P, N_SC * SCONV])
        gb = sb("gate_b", [P, N_GATE])
        psP = [ps(f"p{i}", [P, SEQ]) for i in range(2)]
        w_in = sems("prj_w", 2)
        stored = sems("prj_stored", 2)
        filled, params, w_rounded, w_split, done, act_out, act_part, drained, link = (
            sem("prj_filled"), sem("prj_params"), sem("prj_w_rounded"), sem("prj_w_split"), sem("prj_done"), sem("prj_act_out"),
            sem("prj_act_part"), sem("prj_drained"), sem("prj_link"))
        X0, C0, G0 = N_Z, N_Z + N_XBC, N_Z + N_XBC + 3 * N_SC

        def kinds(eng, z, xbc, short, gate):
            for s in range(2):
                z(s, s, s)
            with eng.Fori(1, N_Z // 2) as r:
                for s in range(2):
                    z(r * 2 + s, r * 2 + s, s)
            with eng.Fori(0, N_XBC // 2) as r:
                for s in range(2):
                    xbc(X0 + r * 2 + s, r * 2 + s, s)
            with eng.Fori(0, N_SC // 2) as r:
                for s in range(2):
                    for part in range(3):
                        short(C0 + r * 6 + s * 3 + part, r * 2 + s, s, part)
            with eng.Fori(0, N_GATE // 2 - 1) as r:
                for s in range(2):
                    gate(G0 + r * 2 + s, r * 2 + s, s)
            for s in range(2):
                gate(N_PROJ - 2 + s, N_GATE - 2 + s, s)

        with nc.Block() as block:
            @block.sync
            def _(sp):
                apart(sp, S)
                for dst, name in ((cw, "conv_w"), (cb, "conv_b"), (sw, "short_w"), (gb, "b_gateT")):
                    sp.dma_start(dst[:], A[name]).then_inc(params, 16)

                def load(q, s):
                    n = 2 * q + s
                    wait(sp, w_split, n - 1)
                    apart(sp, S)
                    sp.dma_start(w[s][:], A["w_in_t"][bass.ds(n * P, P), :].rearrange("p (k m) -> p k m", k=KD)).then_inc(w_in[s], 16)
                pipeline(sp, N_PROJ, 2, [(0, load)])

            @block.tensor
            def _(pe):
                def tile(q, s):
                    n = 2 * q + s
                    pe.wait_ge(w_split, n + 1)
                    wait(pe, drained, n - 1)
                    for b in range(TB):
                        last = product(pe, psP[s][:, b * BANK:(b + 1) * BANK],
                                       [lambda k, x=x: x[:, k, :] for x in (w_hi[s], w_lo[s])],
                                       [lambda k, x=x: x[:, k, b * BANK:(b + 1) * BANK] for x in (h_hi, h_lo)], KD)
                    last.then_inc(done, 1)
                pipeline(pe, N_PROJ, 2, [(0, tile)])

            @block.scalar
            def _(act):
                def round_w(n, s):
                    act.wait_ge(w_in[s], 8 * (n - s) + 16)
                    wait(act, done, n - 1)
                    act.copy(w_hi[s][:], w[s][:]).then_inc(w_rounded, 1)

                def ahead(n, s):
                    if not (isinstance(n, int) and n + 1 >= N_PROJ):
                        round_w(n + 1, 1 - s)
                    act.wait_ge(done, n + 1)

                def z(n, i, s):
                    ahead(n, s % 2)
                    wait(act, stored[s], 8 * (ROW_Z + i - s))
                    act.activation(ob[s][:], psP[s][:], ACT.Silu).then_inc(act_out, 1)

                def xbc(n, i, s):
                    ahead(n, s)
                    act.wait_ge(stored[s], 8 * (ROW_XBC + i - s))
                    act.activation(ob[s][:], psP[s][:], ACT.Identity, bias=cb[:, bass.ds(i, 1)],
                                   scale=cw[:, bass.ds(i * CONV + CONV - 1, 1)]).then_inc(act_part, 1)
                    act.wait_ge(drained, n + 1)
                    act.activation(ob[s][:], ob[s][:], ACT.Silu).then_inc(act_out, 1)

                def short(n, i, s, part):
                    slot = (3 * s + part) % 2
                    ahead(n, slot)
                    if part == 0:
                        act.wait_ge(drained, n - 1)
                        act.copy(c_sb[:], psP[slot][:]).then_inc(act_part, 1)

                def gate(n, i, s):
                    ahead(n, s)
                    act.wait_ge(stored[s], 8 * (ROW_GATE + i - s))
                    act.activation(ob[s][:], psP[s][:], ACT.Sigmoid, bias=gb[:, bass.ds(i, 1)]).then_inc(act_out, 1)

                act.wait_ge(params, 64)
                round_w(0, 0)
                kinds(act, z, xbc, short, gate)

            @block.vector
            def _(dve):
                chain = Chain(dve, link)

                def split_w(n, s):
                    dve.wait_ge(w_rounded, n + 1)
                    dve.tensor_tensor(w_lo[s][:], w[s][:], w_hi[s][:].bitcast(F32), ALU.subtract).then_inc(w_split, 1)

                def ahead(n, s):
                    if not (isinstance(n, int) and n + 1 >= N_PROJ):
                        split_w(n + 1, 1 - s)

                def z(n, i, s):
                    ahead(n, s)
                    dve.wait_ge(act_out, n + 1)
                    wait(dve, drained, n)
                    dve.sem_inc(drained, 1)

                def xbc(n, i, s):
                    ahead(n, s)
                    dve.wait_ge(act_part, i + 1)
                    chain.item(i, CONV - 2)
                    for shift in range(1, CONV):
                        ins = dve.scalar_tensor_tensor(out=ob[s][:, shift:], in0=psP[s][:, :SEQ - shift],
                                                       scalar=cw[:, bass.ds(i * CONV + CONV - 1 - shift, 1)],
                                                       in1=ob[s][:, shift:], op0=ALU.mult, op1=ALU.add)
                        if shift < CONV - 1:
                            chain.step(ins)
                        else:
                            ins.then_inc(drained, 1)
                    chain.end()

                def short(n, i, s, part):
                    slot = (3 * s + part) % 2
                    ahead(n, slot)
                    first = N_XBC * (CONV - 2)
                    if part == 0:
                        dve.wait_ge(act_part, N_XBC + i + 1)
                        dve.wait_ge(drained, n)
                        dve.sem_inc(drained, 1)
                    if part == 1:
                        dve.wait_ge(done, n + 1)
                        dve.tensor_tensor(cx[:], psP[slot][:], c_sb[:], ALU.mult).then_inc(drained, 1)
                        dve.wait_ge(drained, n + 1)
                        dve.wait_ge(stored[s], 8 * (ROW_Q + i - s))
                        chain.item(i, SCONV)
                        chain.n = chain.n + first
                        chain.step(dve.tensor_scalar(ob[s][:], cx[:], sw[:, bass.ds(i * SCONV + SCONV - 1, 1)], None, ALU.mult))
                        for shift in range(1, SCONV):
                            chain.step(dve.scalar_tensor_tensor(out=ob[s][:, shift:], in0=cx[:, :SEQ - shift],
                                                                scalar=sw[:, bass.ds(i * SCONV + SCONV - 1 - shift, 1)],
                                                                in1=ob[s][:, shift:], op0=ALU.mult, op1=ALU.add))
                        chain.end()
                    if part == 2:
                        dve.wait_ge(done, n + 1)
                        dve.tensor_tensor(ob[s][:], psP[slot][:], ob[s][:], ALU.mult).then_inc(drained, 1)

                def gate(n, i, s):
                    ahead(n, s)
                    dve.wait_ge(act_out, N_Z + N_XBC + i + 1)
                    dve.wait_ge(drained, n)
                    dve.sem_inc(drained, 1)

                dve.wait_ge(params, 64)
                split_w(0, 0)
                kinds(dve, z, xbc, short, gate)

            @block.gpsimd
            def _(pool):
                def store(m, s):
                    apart(pool, S)
                    pool.dma_start(S.rows_d[bass.ds(m * P, P), :], ob[s][:]).then_inc(stored[s], 16)

                def by_act(n, i, s, row, count):
                    pool.wait_ge(act_out, count)
                    store(row + i, s)

                def short(n, i, s, part):
                    if part == 2:
                        pool.wait_ge(drained, n + 1)
                        store(ROW_Q + i, s)

                with pool.Fori(SEQ * TOPK // P, MOE_TILES) as i:
                    pool.dma_start(S.slot_out_d[bass.ds(i * P, P), :], h_hi[:, 0, 0:D].bitcast(F32)).then_inc(filled, 16)
                kinds(pool, lambda n, i, s: by_act(n, i, s, ROW_Z, i + 1),
                      lambda n, i, s: by_act(n, i, s, ROW_XBC, i + N_Z + 1), short,
                      lambda n, i, s: by_act(n, i, s, ROW_GATE, i + N_Z + N_XBC + 1))
                for s in range(2):
                    pool.wait_ge(stored[s], 8 * N_ROWS)
                pool.wait_ge(filled, 16 * (MOE_TILES - SEQ * TOPK // P))


def ssd(nc, A, S, sem, sems):
    with ExitStack() as ctx:
        sb, ps = stack(ctx, nc, "ssd")
        GT = HG * HD // P
        LOADS = 5
        xT = [sb(f"xT{i}", [P, GT, P]) for i in range(4)]
        zT = [sb(f"zT{i}", [P, GT, P]) for i in range(4)]
        bT = [sb(f"bT{i}", [P, P]) for i in range(4)]
        cT = [sb(f"cT{i}", [P, P]) for i in range(4)]
        ab = [sb(f"acum{i}", [P, HG, P]) for i in range(4)]
        xd = [sb(f"xd{i}", [P, HG, HD]) for i in range(2)]
        xdd = [sb(f"xdd{i}", [P, HG, HD]) for i in range(2)]
        b_tok = [sb(f"b{i}", [P, P]) for i in range(2)]
        cbm = [sb(f"cbm{i}", [P, P]) for i in range(2)]
        seg = [sb(f"seg{i}", [P, HG, P]) for i in range(2)]
        ldec = [sb(f"ldec{i}", [P, HG, P]) for i in range(2)]
        m = [sb(f"m{i}", [P, HG, P]) for i in range(2)]
        ea = [sb(f"ea{i}", [P, HG, P]) for i in range(2)]
        cs = [sb(f"cs{i}", [P, HG, P]) for i in range(2)]
        xs = [sb(f"xs{i}", [P, GT, P]) for i in range(2)]
        yo = [sb(f"y{i}", [P, GT, P]) for i in range(4)]
        prev = [sb(f"state{i}", [P, HG, HD]) for i in range(4)]
        dsk = sb("d_skip", [P, INNER // P])
        psX = [ps(f"x{i}", [P, GT * P]) for i in range(2)]
        psB = [ps(f"b{i}", [P, BANK]) for i in range(2)]
        psY = [ps(f"y{i}", [P, GT * P]) for i in range(2)]
        psS = [ps(f"s{i}", [P, HG * HD]) for i in range(2)]
        loaded = sems("ssd_in", 4)
        stored = sems("ssd_stored", 4)
        d_in, zeroed, turned, x_ready, seg_ready, m_ready, ea_ready, b_ready, l_ready, xdd_ready, cs_ready, xs_ready, \
            y_done, skipped, decayed, state_ready, y_ready, masked = (sem(f"ssd_{n}") for n in (
                "d", "zeroed", "turned", "x", "seg", "m", "ea", "b", "l", "xdd", "cs", "xs", "y_done", "skipped",
                "decayed", "state", "y", "masked"))

        def heads(t, c, g):
            return t[:, bass.ds(c * HEADS + g * HG, HG)]

        with nc.Block() as block:
            @block.sync
            def _(sp):
                def store(c, g):
                    sp.wait_ge(y_ready, 4 * c + g + 1)
                    apart(sp, S)
                    sp.dma_start(S.y_d[g * GT * P:(g + 1) * GT * P, bass.ds(c * P, P)].rearrange("(a p) t -> p a t", p=P),
                                 yo[g][:]).then_inc(stored[g], 16)

                def load(c, g):
                    cols = bass.ds(c * P, P)
                    for dst, row, tiles in ((xT[g], ROW_XBC + g * GT, GT), (zT[g], ROW_Z + g * GT, GT)):
                        sp.dma_start(dst[:], S.rows_d[row * P:(row + tiles) * P, cols].rearrange(
                            "(a p) t -> p a t", p=P)).then_inc(loaded[g], 16)
                    for dst, row in ((bT[g], ROW_XBC + N_Z + g), (cT[g], ROW_XBC + N_Z + GROUPS + g)):
                        sp.dma_start(dst[:], S.rows_d[row * P:(row + 1) * P, cols]).then_inc(loaded[g], 16)
                    sp.dma_start(ab[g][:], S.acum_d[g * HG:(g + 1) * HG, cols].partition_broadcast(P)).then_inc(loaded[g], 16)

                sp.dma_start(dsk[:], A["d_skipT"]).then_inc(d_in, 16)
                pipeline(sp, 4 * TT, 4, [(4, store), (0, load)])
                for g in range(4):
                    sp.wait_ge(stored[g], 16 * TT)

            @block.tensor
            def _(pe):
                def front(c, g):
                    u, s = 4 * c + g, g % 2
                    pe.wait_ge(loaded[g], 16 * LOADS * (c + 1))
                    wait(pe, x_ready, u - 1)
                    wait(pe, b_ready, u - 1)
                    wait(pe, masked, u - 1)
                    for a in range(GT):
                        pe.transpose(psX[s][:, a * P:(a + 1) * P], xT[g][:, a, :], S.ident[:])
                    pe.transpose(psB[s][:, 0:P], bT[g][:], S.ident[:])
                    pe.matmul(psB[s][:, P:2 * P], bT[g][:], cT[g][:], start=True, stop=True).then_inc(turned, 1)

                def back(c, g):
                    u, s = 4 * c + g, g % 2
                    pe.wait_ge(x_ready, u + 1)
                    pe.wait_ge(m_ready, u + 1)
                    pe.wait_ge(cs_ready, u + 1)
                    pe.wait_ge(zeroed, 4)
                    wait(pe, state_ready, u - 3)
                    wait(pe, skipped, u - 1)
                    for h in range(HG):
                        rows, cols = slice(h % 2 * HD, (h % 2 + 1) * HD), slice(h // 2 * P, (h // 2 + 1) * P)
                        pe.matmul(psY[s][rows, cols], xd[s][:, h, :], m[s][:, h, :], start=True, stop=False)
                        last = pe.matmul(psY[s][rows, cols], prev[g][:, h, :], cs[s][:, h, :], start=False, stop=True)
                    pe.wait_ge(b_ready, u + 1)
                    pe.wait_ge(xdd_ready, u + 1)
                    wait(pe, state_ready, u - 1)
                    pe.matmul(psS[s][:], b_tok[s][:], xdd[s][:].rearrange("p h d -> p (h d)"),
                              start=True, stop=True).then_inc(y_done, 1)
                pipeline(pe, 4 * TT, 4, [(0, front), (1, back)])

            @block.scalar
            def _(act):
                def front(c, g):
                    u, s = 4 * c + g, g % 2
                    act.wait_ge(loaded[g], 16 * LOADS * (c + 1))
                    wait(act, cs_ready, u - 1)
                    act.activation(ea[s][:], ab[g][:], ACT.Exp).then_inc(ea_ready, 1)
                    for h in range(HG):
                        last = act.activation(seg[s][:, h, :], ab[g][:, h, :], ACT.Relu, scale=-1.0,
                                              bias=S.acum[:, bass.ds(c * HEADS + g * HG + h, 1)])
                    last.then_inc(seg_ready, 1)
                    act.wait_ge(turned, u + 1)
                    wait(act, y_done, u - 1)
                    act.copy(b_tok[s][:], psB[s][:, 0:P]).then_inc(b_ready, 1)
                    act.wait_ge(seg_ready, u + 1)
                    wait(act, m_ready, u - 1)
                    act.activation(ldec[s][:], seg[s][:], ACT.Exp, scale=-1.0).then_inc(l_ready, 1)
                pipeline(act, 4 * TT, 4, [(0, front)])

            @block.vector
            def _(dve):
                def front(c, g):
                    u, s = 4 * c + g, g % 2
                    dve.wait_ge(turned, u + 1)
                    wait(dve, y_done, u - 1)
                    wait(dve, xdd_ready, u - 1)
                    dve.tensor_tensor(xd[s][:], psX[s][:].rearrange("p (h d) -> p h d", h=HG),
                                      heads(S.dt, c, g).unsqueeze(2).to_broadcast([P, HG, HD]), ALU.mult).then_inc(x_ready, 1)
                    dve.wait_ge(b_ready, u + 1)
                    dve.tensor_tensor(cbm[s][:], psB[s][:, P:2 * P], S.tri[:], ALU.mult).then_inc(masked, 1)

                def back(c, g):
                    u, s = 4 * c + g, g % 2
                    dve.wait_ge(y_done, u + 1)
                    dve.tensor_tensor(prev[g][:], prev[g][:], heads(S.chunk_decay, c, g).unsqueeze(2).to_broadcast([P, HG, HD]),
                                      ALU.mult).then_inc(decayed, 1)
                    dve.wait_ge(xs_ready, u + 1)
                    wait(dve, stored[g], 16 * c)
                    dve.tensor_tensor(yo[g][:], psY[s][:].rearrange("p (a t) -> p a t", a=GT), xs[s][:], ALU.add).then_inc(skipped, 1)
                    dve.wait_ge(decayed, u + 1)
                    dve.tensor_tensor(prev[g][:], psS[s][:].rearrange("p (h d) -> p h d", h=HG), prev[g][:],
                                      ALU.add).then_inc(state_ready, 1)
                    dve.wait_ge(skipped, u + 1)
                    dve.tensor_tensor(yo[g][:], yo[g][:], zT[g][:], ALU.mult).then_inc(y_ready, 1)

                def decayed_scores(c, g):
                    u, s = 4 * c + g, g % 2
                    dve.wait_ge(l_ready, u + 1)
                    dve.wait_ge(masked, u + 1)
                    dve.tensor_tensor(m[s][:], ldec[s][:], cbm[s][:].unsqueeze(1).to_broadcast([P, HG, P]),
                                      ALU.mult).then_inc(m_ready, 1)

                for g in range(4):
                    dve.memset(prev[g][:], 0.0).then_inc(zeroed, 1)
                dve.wait_ge(zeroed, 4)
                pipeline(dve, 4 * TT, 4, [(0, front), (0, decayed_scores), (1, back)])

            @block.gpsimd
            def _(pool):
                def unit(c, g):
                    u, s = 4 * c + g, g % 2
                    pool.wait_ge(ea_ready, u + 1)
                    wait(pool, y_done, u - 1)
                    pool.tensor_tensor(cs[s][:], ea[s][:], cT[g][:].unsqueeze(1).to_broadcast([P, HG, P]), ALU.mult).then_inc(cs_ready, 1)
                    pool.wait_ge(x_ready, u + 1)
                    pool.tensor_tensor(xdd[s][:], xd[s][:], heads(S.decay, c, g).unsqueeze(2).to_broadcast([P, HG, HD]),
                                       ALU.mult).then_inc(xdd_ready, 1)
                    wait(pool, skipped, u - 1)
                    pool.tensor_tensor(xs[s][:], xT[g][:], dsk[:, g * GT:(g + 1) * GT].unsqueeze(2).to_broadcast([P, GT, P]),
                                       ALU.mult).then_inc(xs_ready, 1)
                pool.wait_ge(d_in, 16)
                pipeline(pool, 4 * TT, 4, [(0, unit)])


def branches(nc, A, S, sem, sems):
    with ExitStack() as ctx:
        sb, ps = stack(ctx, nc, "brn")
        KY, KQ = INNER // P, KD
        ITEMS = KY + KQ
        NU = D // P
        TB = SEQ // BANK
        NRAW, NSQ = 8, 4
        SECOND = 16
        raw = [sb(f"raw{i}", [P, BANK]) for i in range(NRAW)]
        hi = sb("hi", [P, ITEMS, BANK], F32R)
        lo = sb("lo", [P, ITEMS, BANK], F32R)
        sq = [sb(f"sq{i}", [P, BANK]) for i in range(NSQ)]
        sqs = sb("sq_sum", [P, BANK])
        rstd = sb("rstd", [P, BANK])
        HALF = ITEMS // 2
        w = [sb(f"w{c}", [P, HALF, P]) for c in range(2)]
        w_hi = [sb(f"w_hi{i}", [P, ITEMS, P], F32R) for i in range(2)]
        w_lo = [sb(f"w_lo{i}", [P, ITEMS, P], F32R) for i in range(2)]
        ga = [sb(f"ga{i}", [P, BANK]) for i in range(2)]
        gb = [sb(f"gb{i}", [P, BANK]) for i in range(2)]
        ta = [sb(f"ta{i}", [P, BANK]) for i in range(2)]
        tb_ = [sb(f"tb{i}", [P, BANK]) for i in range(2)]
        nw = sb("norm_w", [P, KY])
        psA = [ps(f"a{i}", [P, BANK]) for i in range(2)]
        psB = [ps(f"b{i}", [P, BANK]) for i in range(2)]
        psQ = ps("squares", [P, BANK])
        raw_in, w_in, gates_in = sems("brn_raw", NRAW), sems("brn_w", 2), sems("brn_gates", 2)
        stored, squared = sems("brn_stored", 2), sems("brn_squared", 2)
        nw_in, rounded, low, summed, w_rounded, w_split, item_used, unit_done, ss_done, root_done, rstd_ready, part_a, \
            part_b, scaled, combined = (sem(f"brn_{n}") for n in (
                "nw", "rounded", "low", "summed", "w_rounded", "w_split", "item_used", "unit", "ss", "root", "rstd",
                "part_a", "part_b", "scaled", "combined"))

        def middle(eng, tb, fn):
            with eng.Fori(1, NU // 2 - 1) as r:
                for s in range(2):
                    fn(r * 2 + (tb * NU + s), r * 2 + s, s)

        def ends(tb, fn):
            for s in range(2):
                fn(tb * NU + NU - 2 + s, NU - 2 + s, s)

        with nc.Block() as block:
            @block.sync
            def _(sp):
                sp.dma_start(nw[:], A["ssd_norm_wT"]).then_inc(nw_in, 16)

                def load_w(u, n, s, tb):
                    for c in range(2):
                        wait(sp, w_split, 2 * u - 1 + c)
                        apart(sp, S)
                        sp.dma_start(w[c][:], A["w_branch_t"][bass.ds(n * P, P), c * HALF * P:(c + 1) * HALF * P]
                                     .rearrange("p (k m) -> p k m", k=HALF)).then_inc(w_in[c], 16)

                def load_gates(u, n, s, tb):
                    wait(sp, combined, u - 1)
                    apart(sp, S)
                    for dst, row in ((ga, ROW_GATE), (gb, ROW_GATE + NU)):
                        sp.dma_start(dst[s][:], S.rows_d[bass.ds((n + row) * P, P), tb * BANK:(tb + 1) * BANK]).then_inc(gates_in[s], 16)

                def load(u, n, s, tb):
                    load_w(u, n, s, tb)
                    load_gates(u, n, s, tb)

                def load_items(tb, items):
                    for j in items:
                        i = tb * ITEMS + j
                        src = S.y_d[j * P:(j + 1) * P] if j < KY else S.rows_d[(ROW_Q + j - KY) * P:(ROW_Q + j - KY + 1) * P]
                        if i >= NRAW:
                            sp.wait_ge(low, i - NRAW + 1)
                            if (i - NRAW) % ITEMS < KY:
                                squares = (i - NRAW) // ITEMS * KY + (i - NRAW) % ITEMS + 1
                                sp.wait_ge(squared[j % 2], (squares + 1) // 2)
                        sp.dma_start(raw[j % NRAW][:], src[:, tb * BANK:(tb + 1) * BANK]).then_inc(raw_in[j % NRAW], 16)

                load_items(0, range(NRAW))
                for tb in range(TB):
                    load(tb * NU, 0, 0, tb)
                    load_items(tb, range(NRAW, SECOND))
                    load_w(tb * NU + 1, 1, 1, tb)
                    load_items(tb, range(SECOND, ITEMS))
                    load_gates(tb * NU + 1, 1, 1, tb)
                    middle(sp, tb, lambda u, n, s: load(u, n, s, tb))
                    load(tb * NU + NU - 2, NU - 2, 0, tb)
                    if tb + 1 < TB:
                        load_items(tb + 1, range(NRAW))
                    load(tb * NU + NU - 1, NU - 1, 1, tb)

            @block.gpsimd
            def _(pool):
                def store(u, n, s, tb):
                    pool.wait_ge(combined, u + 1)
                    apart(pool, S)
                    pool.dma_start(S.mixin_d[bass.ds(n * P, P), tb * BANK:(tb + 1) * BANK], ta[s][:]).then_inc(stored[s], 16)

                def add_squares(tb):
                    for j in range(KY):
                        i = tb * KY + j
                        pool.wait_ge(squared[j % 2], i // 2 + 1)
                        if j == 0:
                            wait(pool, ss_done, tb)
                            pool.tensor_copy(sqs[:], sq[0][:]).then_inc(summed, 1)
                        else:
                            pool.wait_ge(summed, i)
                            pool.tensor_tensor(sqs[:], sqs[:], sq[j % NSQ][:], ALU.add).then_inc(summed, 1)

                add_squares(0)
                for tb in range(TB):
                    for s in range(2):
                        store(tb * NU + s, s, s, tb)
                    middle(pool, tb, lambda u, n, s: store(u, n, s, tb))
                    store(tb * NU + NU - 2, NU - 2, 0, tb)
                    if tb + 1 < TB:
                        add_squares(tb + 1)
                    store(tb * NU + NU - 1, NU - 1, 1, tb)
                for s in range(2):
                    pool.wait_ge(stored[s], 16 * TB * NU // 2)

            @block.scalar
            def _(act):
                def round_w(u, n, s):
                    wait(act, unit_done, u - 1)
                    for c in range(2):
                        act.wait_ge(w_in[c], 16 * u + 16)
                        act.copy(w_hi[s][:, c * HALF:(c + 1) * HALF, :], w[c][:]).then_inc(w_rounded, 1)

                act.wait_ge(nw_in, 16)
                for tb in range(TB):
                    round_w(tb * NU, 0, 0)
                    for j in range(ITEMS):
                        i = tb * ITEMS + j
                        act.wait_ge(raw_in[j % NRAW], 16 * (i // NRAW + 1))
                        wait(act, item_used, (tb - 1) * ITEMS + j + 1 if tb else 0)
                        if j == ITEMS - 4:
                            round_w(tb * NU + 1, 1, 1)
                        if j < KY:
                            act.activation(hi[:, j, :], raw[j % NRAW][:], ACT.Identity, scale=nw[:, j:j + 1]).then_inc(rounded, 1)
                            if j % 2:
                                wait(act, summed, tb * KY + j - NSQ + 1)
                                act.activation(sq[j % NSQ][:], raw[j % NRAW][:], ACT.Square).then_inc(squared[1], 1)
                        else:
                            act.copy(hi[:, j, :], raw[j % NRAW][:]).then_inc(rounded, 1)
                    act.wait_ge(ss_done, tb + 1)
                    wait(act, combined, tb * NU)
                    act.activation(rstd[:], psQ[:], ACT.Sqrt, bias=S.eps[:], scale=1.0 / INNER).then_inc(root_done, 1)
                    middle(act, tb, round_w)
                    ends(tb, round_w)

            @block.vector
            def _(dve):
                def split_w(u, n, s):
                    for c in range(2):
                        part = slice(c * HALF, (c + 1) * HALF)
                        dve.wait_ge(w_rounded, 2 * u + c + 1)
                        dve.tensor_tensor(w_lo[s][:, part, :], w[c][:], w_hi[s][:, part, :].bitcast(F32), ALU.subtract).then_inc(w_split, 1)

                def combine(u, n, s):
                    dve.wait_ge(unit_done, u + 1)
                    dve.wait_ge(gates_in[s], 16 * (u - s) + 32)
                    wait(dve, stored[s], 8 * (u - s))
                    dve.tensor_tensor(ta[s][:], psA[s][:], rstd[:], ALU.mult).then_inc(part_a, 1)
                    dve.tensor_tensor(tb_[s][:], psB[s][:], gb[s][:], ALU.mult).then_inc(part_b, 1)
                    dve.wait_ge(part_a, u + 1)
                    dve.tensor_tensor(ta[s][:], ta[s][:], ga[s][:], ALU.mult).then_inc(scaled, 1)
                    dve.wait_ge(part_b, u + 1)
                    dve.wait_ge(scaled, u + 1)
                    dve.tensor_tensor(ta[s][:], ta[s][:], tb_[s][:], ALU.add).then_inc(combined, 1)

                def items(tb, js):
                    for j in js:
                        dve.wait_ge(rounded, tb * ITEMS + j + 1)
                        if j < KY:
                            dve.scalar_tensor_tensor(out=lo[:, j, :], in0=raw[j % NRAW][:], scalar=nw[:, j:j + 1],
                                                     in1=hi[:, j, :].bitcast(F32), op0=ALU.mult, op1=ALU.subtract).then_inc(low, 1)
                            if j % 2 == 0:
                                wait(dve, summed, tb * KY + j - NSQ + 1)
                                dve.tensor_tensor(sq[j % NSQ][:], raw[j % NRAW][:], raw[j % NRAW][:], ALU.mult).then_inc(squared[0], 1)
                        else:
                            dve.tensor_tensor(lo[:, j, :], raw[j % NRAW][:], hi[:, j, :].bitcast(F32), ALU.subtract).then_inc(low, 1)

                dve.wait_ge(nw_in, 16)
                for tb in range(TB):
                    split_w(tb * NU, 0, 0)
                    items(tb, range(SECOND))
                    if tb:
                        combine(tb * NU - 1, NU - 1, 1)
                    items(tb, range(SECOND, ITEMS))
                    split_w(tb * NU + 1, 1, 1)
                    dve.wait_ge(root_done, tb + 1)
                    dve.reciprocal(rstd[:], rstd[:]).then_inc(rstd_ready, 1)
                    dve.wait_ge(rstd_ready, tb + 1)
                    with dve.Fori(0, NU // 2 - 1) as r:
                        for s in range(2):
                            combine(r * 2 + (tb * NU + s), r * 2 + s, s)
                            split_w(r * 2 + (tb * NU + s + 2), r * 2 + s + 2, s)
                    combine(tb * NU + NU - 2, NU - 2, 0)
                combine(TB * NU - 1, NU - 1, 1)

            @block.tensor
            def _(pe):
                def unit(u, n, s, first=None, last=False):
                    wait(pe, combined, u - 1)
                    for k in range(ITEMS):
                        if k % HALF == 0:
                            pe.wait_ge(w_split, 2 * u + k // HALF + 1)
                        if first is not None:
                            pe.wait_ge(low, first + k + 1)
                        out = psA if k < KY else psB
                        for m, (a, b) in enumerate(((w_hi, hi), (w_hi, lo), (w_lo, hi))):
                            ins = pe.matmul(out[s][:], a[s][:, k, :], b[:, k, :], start=(k in (0, KY) and m == 0),
                                            stop=(k in (KY - 1, ITEMS - 1) and m == 2))
                        if last:
                            ins.then_inc(item_used, 1)
                    if last:
                        pe.wait_ge(item_used, (u // NU + 1) * ITEMS)
                        pe.sem_inc(unit_done, 1)
                    else:
                        ins.then_inc(unit_done, 1)

                for tb in range(TB):
                    unit(tb * NU, 0, 0, first=tb * ITEMS)
                    pe.wait_ge(summed, (tb + 1) * KY)
                    wait(pe, root_done, tb)
                    pe.matmul(psQ[:], S.ones[:], sqs[:], start=True, stop=True).then_inc(ss_done, 1)
                    unit(tb * NU + 1, 1, 1)
                    middle(pe, tb, unit)
                    unit(tb * NU + NU - 2, NU - 2, 0)
                    unit(tb * NU + NU - 1, NU - 1, 1, last=True)


def mix_out(nc, A, S, sem, sems):
    with ExitStack() as ctx:
        sb, ps = stack(ctx, nc, "mix")
        wo_hi = sb("wo_hi", [P, KD, D], F32R)
        wo_lo = sb("wo_lo", [P, KD, D], F32R)
        wr = sb("w_router", [P, KD, EXPERTS])
        br = sb("b_router", [P, EXPERTS])
        lg = sb("ln_g", [P, D])
        lb = sb("ln_b", [P, D])
        g1, sh2, sc2 = sb("g1", [P, D]), sb("sh2", [P, D]), sb("sc2", [P, D])
        NWO = 4
        wo = [sb(f"wo{i}", [P, D]) for i in range(NWO)]

        def pair(name, shape, dt=F32):
            return [sb(f"{name}{i}", shape, dt) for i in range(2)]
        mt, mt_hi, mt_lo = pair("m", [P, KD, P]), pair("m_hi", [P, KD, P], F32R), pair("m_lo", [P, KD, P], F32R)
        xt, r, x1, xn = pair("x", [P, D]), pair("r", [P, D]), pair("x1", [P, D]), pair("xn", [P, D])
        st, mv, sd, rs = pair("st", [P, 2, 6]), pair("mv", [P, 2]), pair("sd", [P, 1]), pair("rs", [P, 1])
        st2, mv2, sd2, rs2 = pair("st2", [P, 2, 6]), pair("mv2", [P, 2]), pair("sd2", [P, 1]), pair("rs2", [P, 1])
        hT = pair("hT", [P, KD, P])
        psM = [ps(f"m{i}", [P, D]) for i in range(2)]
        psT = ps("t", [P, KD, P])
        psL = ps("logits", [P, BANK])
        par_in, wo_rounded, wo_split = (sem(f"mix_{n}") for n in ("params", "wo_rounded", "wo_split"))
        wo_in, t_in, x1_out, h_out = sems("mix_wo", NWO), sems("mix_in", 2), sems("mix_x1_out", 2), sems("mix_h_out", 2)
        m_rounded, m_split, mixed, gated, summed, halves, stats, root1, inv1, normed, scaled, x1_ready, halves2, stats2, \
            root2, inv2, xn_ready, xn_scaled, h_ready, turned, h_kept, routed, logits = (sem(f"mix_{n}") for n in (
                "m_rounded", "m_split", "mixed", "gated", "summed", "halves", "stats", "root1", "inv1", "normed", "scaled",
                "x1", "halves2", "stats2", "root2", "inv2", "xn", "xn_scaled", "h", "turned", "h_kept", "routed", "logits"))

        with nc.Block() as block:
            @block.sync
            def _(sp):
                for k in range(KD):
                    wait(sp, wo_split, k - NWO + 1)
                    apart(sp, S)
                    sp.dma_start(wo[k % NWO][:], A["w_o"][k * P:(k + 1) * P, :]).then_inc(wo_in[k % NWO], 16)

                def params():
                    sp.dma_start(wr[:], A["w_router_t"].rearrange("p (k n) -> p k n", k=KD)).then_inc(par_in, 16)
                    for dst, name in ((br, "b_router"), (lg, "ln1_g"), (lb, "ln1_b")):
                        sp.dma_start(dst[:], A[name][0].partition_broadcast(P)).then_inc(par_in, 16)
                    for dst, i in ((g1, ADA_G1), (sh2, ADA_SH2), (sc2, ADA_SC2)):
                        sp.dma_start(dst[:], S.ada_d[0, i * D:(i + 1) * D].partition_broadcast(P)).then_inc(par_in, 16)

                def load(q, s):
                    t = 2 * q + s
                    wait(sp, summed, t - 1)
                    apart(sp, S)
                    sp.dma_start(mt[s][:], S.mixin_d[:, bass.ds(t * P, P)].rearrange("(k p) t -> p k t", p=P)).then_inc(t_in[s], 16)
                    sp.dma_start(xt[s][:], A["x"][bass.ds(t * P, P), :]).then_inc(t_in[s], 16)
                    if isinstance(q, int) and t == 0:
                        params()
                pipeline(sp, TT, 2, [(0, load)])

            @block.gpsimd
            def _(pool):
                def affine(q, s):
                    t = 2 * q + s
                    pool.wait_ge(normed, t + 1)
                    wait(pool, x1_out[s], 16 * q)
                    wait(pool, stats2, t - 1)
                    wait(pool, xn_ready, t - 1)
                    pool.tensor_tensor(x1[s][:], r[s][:], lg[:], ALU.mult).then_inc(scaled, 1)
                    pool.wait_ge(scaled, t + 1)
                    pool.tensor_tensor(x1[s][:], x1[s][:], lb[:], ALU.add).then_inc(x1_ready, 1)

                def shift(q, s):
                    t = 2 * q + s
                    pool.wait_ge(xn_scaled, t + 1)
                    pool.tensor_tensor(xn[s][:], xn[s][:], sh2[:], ALU.add).then_inc(h_ready, 1)

                def store(q, s):
                    t = 2 * q + s
                    pool.wait_ge(x1_ready, t + 1)
                    apart(pool, S)
                    pool.dma_start(S.x1_d[bass.ds(t * P, P), :], x1[s][:]).then_inc(x1_out[s], 16)
                    pool.wait_ge(h_ready, t + 1)
                    apart(pool, S)
                    pool.dma_start(S.h2_d[bass.ds(t * P, P), :], xn[s][:]).then_inc(h_out[s], 16)
                pool.wait_ge(par_in, 112)
                pipeline(pool, TT, 2, [(0, affine), (1, shift), (1, store)])
                for s in range(2):
                    pool.wait_ge(x1_out[s], 8 * TT)
                    pool.wait_ge(h_out[s], 8 * TT)

            @block.scalar
            def _(act):
                for k in range(KD):
                    act.wait_ge(wo_in[k % NWO], 16 * (k // NWO + 1))
                    act.copy(wo_hi[:, k, :], wo[k % NWO][:]).then_inc(wo_rounded, 1)

                def round_m(q, s):
                    t = 2 * q + s
                    act.wait_ge(t_in[s], 32 * (q + 1))
                    wait(act, mixed, t - 1)
                    act.copy(mt_hi[s][:], mt[s][:]).then_inc(m_rounded, 1)

                def first_root(q, s):
                    act.wait_ge(stats, 2 * q + s + 1)
                    act.activation(sd[s][:], mv[s][:, 1:2], ACT.Sqrt, bias=S.eps[:]).then_inc(root1, 1)

                def second_root(q, s):
                    act.wait_ge(stats2, 2 * q + s + 1)
                    act.activation(sd2[s][:], mv2[s][:, 1:2], ACT.Sqrt, bias=S.eps[:]).then_inc(root2, 1)

                def keep_h(q, s):
                    t = 2 * q + s
                    act.wait_ge(turned, t + 1)
                    wait(act, routed, t - 1)
                    act.copy(hT[s][:], psT[:]).then_inc(h_kept, 1)
                pipeline(act, TT, 2, [(0, round_m), (1, first_root), (2, second_root), (3, keep_h)])

            @block.tensor
            def _(pe):
                def mix(q, s):
                    t = 2 * q + s
                    pe.wait_ge(m_split, t + 1)
                    wait(pe, gated, t - 1)
                    for half in range(2):
                        cols = slice(half * BANK, (half + 1) * BANK)
                        last = product(pe, psM[s][:, cols], [lambda k, x=x: x[:, k, :] for x in (mt_hi[s], mt_lo[s])],
                                       [lambda k, x=x: x[:, k, cols] for x in (wo_hi, wo_lo)], KD)
                    last.then_inc(mixed, 1)

                def turn(q, s):
                    t = 2 * q + s
                    pe.wait_ge(h_ready, t + 1)
                    wait(pe, h_kept, t)
                    for k in range(KD):
                        last = pe.transpose(psT[:, k, :], xn[s][:, k * P:(k + 1) * P], S.ident[:])
                    last.then_inc(turned, 1)

                def route(q, s):
                    t = 2 * q + s
                    if isinstance(q, int) and t == 0:
                        pe.wait_ge(par_in, 112)
                    pe.wait_ge(h_kept, t + 1)
                    wait(pe, logits, t)
                    for k in range(KD):
                        last = pe.matmul(psL[:, 0:EXPERTS], hT[s][:, k, :], wr[:, k, :], start=(k == 0), stop=(k == KD - 1))
                    last.then_inc(routed, 1)
                pe.wait_ge(wo_split, KD)
                pipeline(pe, TT, 2, [(3, turn), (0, mix), (3, route)])

            @block.vector
            def _(dve):
                for k in range(KD):
                    dve.wait_ge(wo_rounded, k + 1)
                    dve.tensor_tensor(wo_lo[:, k, :], wo[k % NWO][:], wo_hi[:, k, :].bitcast(F32), ALU.subtract).then_inc(wo_split, 1)

                def split_m(q, s):
                    dve.wait_ge(m_rounded, 2 * q + s + 1)
                    dve.tensor_tensor(mt_lo[s][:], mt[s][:], mt_hi[s][:].bitcast(F32), ALU.subtract).then_inc(m_split, 1)

                def residual(q, s):
                    t = 2 * q + s
                    if isinstance(q, int) and t == 0:
                        dve.wait_ge(par_in, 112)
                    dve.wait_ge(mixed, t + 1)
                    wait(dve, x1_ready, t - 1)
                    dve.tensor_tensor(r[s][:], psM[s][:], g1[:], ALU.mult).then_inc(gated, 1)
                    dve.wait_ge(gated, t + 1)
                    dve.scalar_tensor_tensor(out=r[s][:], in0=xt[s][:], scalar=DN_ALPHA, in1=r[s][:], op0=ALU.mult,
                                             op1=ALU.add).then_inc(summed, 1)
                    dve.wait_ge(summed, t + 1)
                    for half in range(2):
                        dve.bn_stats(st[s][:, half, :], r[s][:, half * BANK:(half + 1) * BANK]).then_inc(halves, 1)
                    dve.wait_ge(halves, 2 * (t + 1))
                    apart(dve, S)
                    dve.bn_aggr(mv[s][:], st[s][:]).then_inc(stats, 1)

                def normalise(q, s):
                    t = 2 * q + s
                    dve.wait_ge(root1, t + 1)
                    dve.reciprocal(rs[s][:], sd[s][:]).then_inc(inv1, 1)
                    dve.wait_ge(inv1, t + 1)
                    dve.tensor_scalar(r[s][:], r[s][:], mv[s][:, 0:1], rs[s][:], ALU.subtract, ALU.mult).then_inc(normed, 1)

                def second_stats(q, s):
                    t = 2 * q + s
                    dve.wait_ge(x1_ready, t + 1)
                    for half in range(2):
                        dve.bn_stats(st2[s][:, half, :], x1[s][:, half * BANK:(half + 1) * BANK]).then_inc(halves2, 1)
                    dve.wait_ge(halves2, 2 * (t + 1))
                    apart(dve, S)
                    dve.bn_aggr(mv2[s][:], st2[s][:]).then_inc(stats2, 1)

                def second_norm(q, s):
                    t = 2 * q + s
                    dve.wait_ge(root2, t + 1)
                    dve.reciprocal(rs2[s][:], sd2[s][:]).then_inc(inv2, 1)
                    dve.wait_ge(inv2, t + 1)
                    wait(dve, h_out[s], 16 * q)
                    wait(dve, turned, t - 1)
                    dve.tensor_scalar(xn[s][:], x1[s][:], mv2[s][:, 0:1], rs2[s][:], ALU.subtract, ALU.mult).then_inc(xn_ready, 1)
                    dve.wait_ge(xn_ready, t + 1)
                    dve.tensor_tensor(xn[s][:], xn[s][:], sc2[:], ALU.mult).then_inc(xn_scaled, 1)

                def keep_logits(q, s):
                    t = 2 * q + s
                    dve.wait_ge(routed, t + 1)
                    dve.tensor_tensor(S.logits[:, bass.ds(t * EXPERTS, EXPERTS)], psL[:, 0:EXPERTS], br[:], ALU.add).then_inc(logits, 1)
                pipeline(dve, TT, 2, [(0, split_m), (1, residual), (1, normalise), (2, second_stats), (2, second_norm), (4, keep_logits)])
                dve.wait_ge(logits, TT)


def route(nc, A, S, sem, sems):
    with ExitStack() as ctx:
        sb, ps = stack(ctx, nc, "rt")
        E = EXPERTS
        top = sb("top", [P, TT, 8])
        idx = sb("idx", [P, TT, 8], U32)
        idxf = sb("idxf", [P, TT, TOPK])
        iota_e = sb("iota_e", [P, E])
        iota_t = sb("iota_t", [P, MOE_COLS])
        token = sb("token", [P, TT], I32)
        zero_i = sb("zero_i", [P, MOE_COLS], I32)
        hot = sb("hot", [P, TT, TOPK, E])
        chosen = sb("chosen", [P, TT, E])
        strict = sb("strict", [P, P])
        rank = sb("rank", [P, TT, E])
        count = sb("count", [P, TT, E])
        base = sb("base", [P, TT + 1, E])
        cnt_i = sb("cnt_i", [P, E], I32)
        tiles = sb("tiles", [P, E])
        cum = [sb(f"cum{i}", [P, E]) for i in range(2)]
        place = sb("place", [P, TT, E])
        posf = sb("posf", [P, TT, TOPK])
        cmp = sb("cmp", [P, MOE_COLS, E])
        te = sb("te", [P, MOE_COLS])
        fresh = sb("fresh", [P, MOE_COLS])
        last = sb("last", [P, 1])
        sums = sb("sums", [P, TT])
        inv = sb("inv", [P, TT])
        psR = ps("rank", [P, TT * E])
        psC = ps("count", [P, TT * E])
        iotas, zeroed, tops, link, chosen_ready, ranked, diffs, exped, placed, cleared, scattered, listed = (
            sem(f"rt_{n}") for n in ("iotas", "zeroed", "tops", "link", "chosen", "ranked", "diffs", "exp", "placed",
                                     "cleared", "scattered", "listed"))

        with nc.Block() as block:
            @block.gpsimd
            def _(pool):
                pool.iota(iota_e[:], [[1, E]], base=0, channel_multiplier=0, allow_small_or_imprecise_dtypes=True).then_inc(iotas, 1)
                pool.iota(iota_t[:], [[1, MOE_COLS]], base=0, channel_multiplier=0, allow_small_or_imprecise_dtypes=True).then_inc(iotas, 1)
                pool.iota(token[:], [[P, TT]], base=0, channel_multiplier=1).then_inc(iotas, 1)
                pool.affine_select(out=strict[:], in_=S.ones[:], pattern=[[1, P]], compare_op=ALU.is_gt, fill=0.0,
                                   base=0, channel_multiplier=-1).then_inc(iotas, 1)
                pool.memset(zero_i[:], 0).then_inc(zeroed, 1)
                pool.wait_ge(iotas, 4)
                pool.wait_ge(placed, 1)
                pool.wait_ge(cleared, 16)
                for t in range(TT):
                    for k in range(TOPK):
                        apart(pool, S)
                        pool.indirect_dma_start(S.slot_token_d, bass.IndirectOffsetOnAxis(ap=S.pos[:, t * TOPK + k:t * TOPK + k + 1], axis=0),
                                                token[:, t:t + 1], None).then_inc(scattered, 16)
                pool.wait_ge(scattered, 16 * TT * TOPK)

            @block.sync
            def _(sp):
                sp.wait_ge(zeroed, 1)
                apart(sp, S)
                sp.dma_start(S.slot_token_d.rearrange("(p t) o -> p (t o)", p=P), zero_i[:]).then_inc(cleared, 16)
                sp.wait_ge(scattered, 16 * TT * TOPK)
                with nc.allow_non_contiguous_dma(reason="a table of 48 KB"):
                    apart(sp, S)
                    sp.dma_start(S.slot_token[:], S.slot_token_d.rearrange("(t p) o -> p (t o)", p=P)).then_inc(listed, 16)
                sp.wait_ge(listed, 16)

            @block.tensor
            def _(pe):
                pe.wait_ge(iotas, 4)
                pe.wait_ge(chosen_ready, 1)
                rhs = chosen[:].rearrange("p t e -> p (t e)")
                pe.matmul(psR[:], strict[:], rhs, start=True, stop=True)
                pe.matmul(psC[:], S.ones[:], rhs, start=True, stop=True).then_inc(ranked, 1)

            @block.scalar
            def _(act):
                act.wait_ge(diffs, 1)
                act.activation(S.probs[:], S.probs[:], ACT.Exp).then_inc(exped, 1)

            @block.vector
            def _(dve):
                for t in range(TT):
                    dve.max(top[:, t, :], S.logits[:, t * E:(t + 1) * E]).then_inc(tops, 1)
                dve.wait_ge(tops, TT)
                for t in range(TT):
                    dve.max_index(idx[:, t, :], top[:, t, :], S.logits[:, t * E:(t + 1) * E]).then_inc(tops, 1)
                chain = Chain(dve, link)
                probs = S.probs[:].rearrange("p (t k) -> p t k", k=TOPK)
                dve.tensor_tensor(probs, top[:, :, 0:TOPK], top[:, :, 0:1].to_broadcast([P, TT, TOPK]), ALU.subtract).then_inc(diffs, 1)
                dve.wait_ge(tops, 2 * TT)
                dve.wait_ge(iotas, 4)
                chain.step(dve.tensor_copy(idxf[:], idx[:, :, 0:TOPK]))
                hot3 = hot[:].rearrange("p t k e -> p (t k) e")
                chain.step(dve.tensor_tensor(hot3, idxf[:].rearrange("p t k -> p (t k)").unsqueeze(2).to_broadcast([P, TT * TOPK, E]),
                                             iota_e[:].unsqueeze(1).to_broadcast([P, TT * TOPK, E]), ALU.is_equal))
                dve.tensor_reduce(chosen[:], hot[:].rearrange("p t k e -> p t e k"), AX.X, ALU.add).then_inc(chosen_ready, 1)
                dve.wait_ge(exped, 1)
                chain.step(dve.tensor_reduce(sums[:], probs, AX.X, ALU.add))
                chain.step(dve.reciprocal(inv[:], sums[:]))
                chain.step(dve.tensor_tensor(probs, probs, inv[:].unsqueeze(2).to_broadcast([P, TT, TOPK]), ALU.mult))
                dve.wait_ge(ranked, 1)
                chain.step(dve.tensor_copy(rank[:].rearrange("p t e -> p (t e)"), psR[:]))
                chain.step(dve.tensor_copy(count[:].rearrange("p t e -> p (t e)"), psC[:]))
                chain.step(dve.memset(base[:, 0, :], 0.0))
                for t in range(TT):
                    chain.step(dve.tensor_tensor(base[:, t + 1, :], base[:, t, :], count[:, t, :], ALU.add))
                chain.step(dve.tensor_scalar(cum[0][:], base[:, TT, :], float(P - 1), None, ALU.add))
                chain.step(dve.tensor_copy(cnt_i[:], cum[0][:]))
                chain.step(dve.tensor_scalar(cnt_i[:], cnt_i[:], 7, None, ALU.arith_shift_right))
                chain.step(dve.tensor_copy(tiles[:], cnt_i[:]))
                chain.step(dve.tensor_copy(cum[0][:], tiles[:]))
                a = 0
                for shift in (1, 2, 4, 8, 16):
                    chain.step(dve.tensor_copy(cum[1 - a][:, 0:shift], cum[a][:, 0:shift]))
                    chain.step(dve.tensor_tensor(cum[1 - a][:, shift:], cum[a][:, shift:], cum[a][:, :E - shift], ALU.add))
                    a = 1 - a
                chain.step(dve.tensor_tensor(tiles[:], cum[a][:], tiles[:], ALU.subtract))
                chain.step(dve.tensor_scalar(tiles[:], tiles[:], float(P), None, ALU.mult))
                chain.step(dve.tensor_tensor(place[:], rank[:], base[:, 0:TT, :], ALU.add))
                chain.step(dve.tensor_tensor(place[:], place[:], tiles[:].unsqueeze(1).to_broadcast([P, TT, E]), ALU.add))
                for k in range(TOPK):
                    chain.step(dve.tensor_tensor(hot[:, :, k, :], hot[:, :, k, :], place[:], ALU.mult))
                chain.step(dve.tensor_reduce(posf[:], hot[:], AX.X, ALU.add))
                dve.tensor_copy(S.pos[:], posf[:].rearrange("p t k -> p (t k)")).then_inc(placed, 1)
                chain.step(dve.tensor_tensor(cmp[:], iota_t[:].unsqueeze(2).to_broadcast([P, MOE_COLS, E]),
                                             cum[a][:].unsqueeze(1).to_broadcast([P, MOE_COLS, E]), ALU.is_ge))
                chain.step(dve.tensor_reduce(te[:], cmp[:], AX.X, ALU.add))
                chain.step(dve.tensor_scalar(te[:], te[:], float(E - 1), None, ALU.min))
                chain.step(dve.tensor_copy(S.expert[:], te[:]))
                chain.step(dve.memset(fresh[:, 0:1], 1.0))
                chain.step(dve.tensor_tensor(fresh[:, 1:], te[:, 1:], te[:, :MOE_COLS - 1], ALU.not_equal))
                chain.step(dve.tensor_copy(S.fresh[:], fresh[:]))
                chain.step(dve.tensor_scalar(last[:], cum[a][:, E - 1:E], 1.0, None, ALU.add))
                chain.step(dve.tensor_copy(cnt_i[:, 0:1], last[:]))
                chain.step(dve.tensor_scalar(cnt_i[:, 0:1], cnt_i[:, 0:1], 1, None, ALU.arith_shift_right))
                chain.step(dve.tensor_copy(S.rounds[:], cnt_i[:, 0:1]))
                dve.wait_ge(placed, 1)


def experts(nc, A, S, sem, sems):
    with ExitStack() as ctx:
        sb, ps = stack(ctx, nc, "moe")
        F2 = 2 * FF
        KF = FF // P
        NBUF = 6
        PART = 4
        GU, DN = 2 * KD, KF
        GL, DL = GU // PART, DN // PART
        W = 1024

        def pair(name, shape, dt=F32):
            return [sb(f"{name}{i}", shape, dt) for i in range(2)]
        w_gu = [sb(f"w_gu{k}", [P, PART * W]) for k in range(GL)]
        w_dn = [sb(f"w_dn{k}", [P, PART * W]) for k in range(DL)]
        b_gu = sb("b_gu", [P, F2])
        b_dn = sb("b_dn", [P, D])
        w_hi, w_lo = ([sb(f"{n}{i}", [P, W], F32R) for i in range(NBUF)] for n in ("w_hi", "w_lo"))
        xs = sb("xs", [P, D])
        hT_hi, hT_lo = sb("hT_hi", [P, KD, P], F32R), sb("hT_lo", [P, KD, P], F32R)
        aT_hi, aT_lo = sb("aT_hi", [P, KF, P], F32R), sb("aT_lo", [P, KF, P], F32R)
        gate, up, sig = sb("gate", [P, FF]), sb("up", [P, FF]), sb("sig", [P, FF])
        rows = sb("rows", [P, D])
        tok_i = pair("tok_i", [P, 1], I32)
        psG = ps("gu", [P, F2])
        psD = ps("down", [P, D])
        psT = ps("t", [P, KD, P])
        x_in, stored = sem("moe_x"), sem("moe_stored")
        gu_in, dn_in = sems("moe_gu_in", GL), sems("moe_dn_in", DL)
        bgu_in, bdn_in, picked, gu_hi, gu_lo, dn_hi, dn_lo, gu_used, dn_used, h_turned, \
            h_hi, h_lo, g_added, u_added, g_cut, u_cut, gated, sig_done, act_ready, a_turned, a_hi, a_lo, rows_kept, out_ready = (
                sem(f"moe_{n}") for n in (
                    "bgu_in", "bdn_in", "picked", "gu_hi", "gu_lo", "dn_hi", "dn_lo", "gu_used",
                    "dn_used", "h_turned", "h_hi", "h_lo", "g_added", "u_added", "g_cut", "u_cut", "gated",
                    "sig", "act", "a_turned", "a_hi", "a_lo", "rows_kept", "out"))
        LEAD = 3

        def tiles(eng, step):
            rounds_less_2 = eng.value_load(S.rounds[0:1, 0:1], min_val=SEQ * TOPK // P // 2, max_val=MOE_ROUNDS - 2)

            def at(r, s, lag, fn, *more):
                q, slot = (s - lag) // 2, (s - lag) % 2
                if isinstance(r, int) and (r + q) * 2 + slot < 0:
                    return
                fn(2 * (r + q) + slot, r + q, slot, *more)

            for r in range(LEAD):
                for s in range(2):
                    step(lambda lag, fn, *more: at(r, s, lag, fn, *more))
            with eng.Fori(LEAD, MOE_ROUNDS) as r:
                with eng.If(r < rounds_less_2 + 2):
                    for s in range(2):
                        step(lambda lag, fn, *more: at(r, s, lag, fn, *more))
            return rounds_less_2

        def raw(parts, n):
            return parts[n // PART][:, n % PART * W:(n % PART + 1) * W]

        with nc.Block() as block:
            @block.gpsimd
            def _(pool):
                def fetch_tokens(i, q, s):
                    wait(pool, h_turned, i)
                    apart(pool, S)
                    pool.tensor_copy(tok_i[s][:], S.slot_token[:, bass.ds(i, 1)]).then_inc(picked, 1)
                    pool.wait_ge(picked, i + 1)
                    apart(pool, S)
                    pool.indirect_dma_start(xs[:], None, S.h2_d, bass.IndirectOffsetOnAxis(ap=tok_i[s][:], axis=0)).then_inc(x_in, 16)

                def clip_up(i, q, s):
                    pool.wait_ge(u_added, i + 1)
                    apart(pool, S)
                    pool.tensor_scalar(up[:], up[:], LIMIT, -LIMIT, ALU.min, ALU.max).then_inc(u_cut, 1)

                def activate(i, q, s):
                    pool.wait_ge(gated, i + 1)
                    pool.wait_ge(sig_done, i + 1)
                    pool.tensor_tensor(up[:], up[:], sig[:], ALU.mult).then_inc(act_ready, 1)

                def add_bias_dn(i, q, s):
                    pool.wait_ge(rows_kept, i + 1)
                    pool.wait_ge(bdn_in, 16 * (i + 1))
                    pool.tensor_tensor(rows[:], rows[:], b_dn[:], ALU.add).then_inc(out_ready, 1)

                def store(i, q, s):
                    pool.wait_ge(out_ready, i + 1)
                    apart(pool, S)
                    pool.dma_start(S.slot_out_d[bass.ds(i * P, P), :], rows[:]).then_inc(stored, 16)

                def step(at):
                    at(4, add_bias_dn)
                    at(3, activate)
                    at(4, store)
                    at(2, clip_up)
                    at(0, fetch_tokens)
                less_2 = tiles(pool, step)
                pool.wait_ge(x_in, 32 * less_2 + 64)
                apart(pool, S)
                pool.wait_ge(stored, 32 * less_2)
                apart(pool, S)

            @block.tensor
            def _(pe):
                def item(out, high, low, b, k, col):
                    for m, (x, w) in enumerate(((high, w_hi), (high, w_lo), (low, w_hi))):
                        for c in range(W // BANK):
                            ins = pe.matmul(out[:, col + c * BANK:col + (c + 1) * BANK], x[:, k, :],
                                            w[b][:, c * BANK:(c + 1) * BANK],
                                            start=(k == 0 and m == 0), stop=(k == KD - 1 and m == 2))
                    return ins

                def gate_up(i, q, s, items):
                    for n in items:
                        if n == 0:
                            pe.wait_ge(h_lo, i + 1)
                            wait(pe, u_added, i)
                        pe.wait_ge(gu_lo, GU * i + n + 1)
                        item(psG, hT_hi, hT_lo, n % NBUF, n // 2, n % 2 * W).then_inc(gu_used, 1)

                def turn_act(i, q, s):
                    pe.wait_ge(act_ready, i + 1)
                    pe.wait_ge(h_lo, i + 2)
                    for k in range(KF):
                        last = pe.transpose(psT[:, k, :], up[:, k * P:(k + 1) * P], S.ident[:])
                    last.then_inc(a_turned, 1)

                def turn_h(i, q, s):
                    pe.wait_ge(x_in, 16 * (i + 1))
                    wait(pe, a_lo, i - 1)
                    for k in range(KD):
                        last = pe.transpose(psT[:, k, :], xs[:, k * P:(k + 1) * P], S.ident[:])
                    last.then_inc(h_turned, 1)

                def down(i, q, s):
                    wait(pe, rows_kept, i)
                    pe.wait_ge(a_lo, i + 1)
                    for n in range(DN):
                        pe.wait_ge(dn_lo, DN * i + n + 1)
                        item(psD, aT_hi, aT_lo, (GU + n) % NBUF, n, 0).then_inc(dn_used, 1)

                def step(at):
                    at(2, gate_up, range(0, 8))
                    at(3, turn_act)
                    at(2, gate_up, range(8, 16))
                    at(1, turn_h)
                    at(3, down)
                tiles(pe, step)

            @block.scalar
            def _(act):
                def gu(i, q, s, items):
                    for n in items:
                        if n % PART == 0:
                            act.wait_ge(gu_in[n // PART], 16 * (i + 1))
                        if n >= NBUF:
                            act.wait_ge(gu_used, GU * i + n - NBUF + 1)
                        else:
                            wait(act, dn_used, DN * (i - 2) + DN - NBUF + n + 1)
                        act.copy(w_hi[n % NBUF][:], raw(w_gu, n)).then_inc(gu_hi, 1)

                def dn(i, q, s, items):
                    for n in items:
                        if n % PART == 0:
                            act.wait_ge(dn_in[n // PART], 16 * (i + 1))
                        if n >= NBUF:
                            act.wait_ge(dn_used, DN * i + n - NBUF + 1)
                        else:
                            act.wait_ge(gu_used, GU * (i + 1) + GU - NBUF + n + 1)
                        act.copy(w_hi[(GU + n) % NBUF][:], raw(w_dn, n)).then_inc(dn_hi, 1)

                def keep_act(i, q, s):
                    act.wait_ge(a_turned, i + 1)
                    wait(act, dn_used, DN * i)
                    act.copy(aT_hi[:], psT[:]).then_inc(a_hi, 1)

                def keep_h(i, q, s):
                    act.wait_ge(h_turned, i + 1)
                    wait(act, gu_used, GU * i)
                    act.copy(hT_hi[:], psT[:]).then_inc(h_hi, 1)

                def keep_rows(i, q, s):
                    act.wait_ge(dn_used, DN * (i + 1))
                    wait(act, stored, 16 * i)
                    act.copy(rows[:], psD[:]).then_inc(rows_kept, 1)

                def sigmoid(i, q, s):
                    act.wait_ge(g_cut, i + 1)
                    wait(act, act_ready, i)
                    act.activation(sig[:], gate[:], ACT.Sigmoid, scale=SWIGLU_ALPHA).then_inc(sig_done, 1)

                def step(at):
                    at(2, gu, range(0, 2))
                    at(3, sigmoid)
                    at(2, gu, range(2, 6))
                    at(4, keep_rows)
                    at(2, gu, range(6, 13))
                    at(3, keep_act)
                    at(2, gu, range(13, 16))
                    at(3, dn, range(0, 6))
                    at(1, keep_h)
                    at(3, dn, range(6, 8))
                tiles(act, step)

            @block.vector
            def _(dve):
                def gu(i, q, s, items):
                    for n in items:
                        dve.wait_ge(gu_hi, GU * i + n + 1)
                        dve.tensor_tensor(w_lo[n % NBUF][:], raw(w_gu, n), w_hi[n % NBUF][:].bitcast(F32), ALU.subtract).then_inc(gu_lo, 1)

                def dn(i, q, s, items):
                    for n in items:
                        b = (GU + n) % NBUF
                        dve.wait_ge(dn_hi, DN * i + n + 1)
                        dve.tensor_tensor(w_lo[b][:], raw(w_dn, n), w_hi[b][:].bitcast(F32), ALU.subtract).then_inc(dn_lo, 1)

                def add_bias(i, q, s):
                    dve.wait_ge(gu_used, GU * (i + 1))
                    dve.wait_ge(bgu_in, 16 * (i + 1))
                    wait(dve, a_turned, i)
                    dve.tensor_tensor(gate[:], psG[:, 0:FF], b_gu[:, 0:FF], ALU.add).then_inc(g_added, 1)
                    dve.tensor_tensor(up[:], psG[:, FF:F2], b_gu[:, FF:F2], ALU.add).then_inc(u_added, 1)
                    dve.wait_ge(g_added, i + 1)
                    dve.tensor_scalar(gate[:], gate[:], LIMIT, None, ALU.min).then_inc(g_cut, 1)

                def gate_up(i, q, s):
                    dve.wait_ge(g_cut, i + 1)
                    dve.wait_ge(u_cut, i + 1)
                    dve.scalar_tensor_tensor(out=up[:], in0=up[:], scalar=1.0, in1=gate[:], op0=ALU.add, op1=ALU.mult).then_inc(gated, 1)

                def low_h(i, q, s):
                    dve.wait_ge(h_hi, i + 1)
                    dve.tensor_tensor(hT_lo[:], psT[:], hT_hi[:].bitcast(F32), ALU.subtract).then_inc(h_lo, 1)

                def low_act(i, q, s):
                    dve.wait_ge(a_hi, i + 1)
                    dve.tensor_tensor(aT_lo[:], psT[:], aT_hi[:].bitcast(F32), ALU.subtract).then_inc(a_lo, 1)

                def step(at):
                    at(2, gu, range(0, 4))
                    at(3, gate_up)
                    at(2, gu, range(4, 13))
                    at(3, low_act)
                    at(2, gu, range(13, 16))
                    at(3, dn, range(0, 6))
                    at(2, add_bias)
                    at(3, dn, range(6, 7))
                    at(1, low_h)
                    at(3, dn, range(7, 8))
                tiles(dve, step)

            @block.sync
            def _(sp):
                def fetch(i, loads):
                    for _, _, landed, _, _ in loads:
                        wait(sp, landed, 16 * i)
                        apart(sp, S)
                    fresh = sp.value_load(S.fresh[0:1, bass.ds(i, 1)], min_val=0, max_val=1)
                    with sp.If(fresh > 0):
                        expert = sp.value_load(S.expert[0:1, bass.ds(i, 1)], min_val=0, max_val=EXPERTS - 1)
                        for dst, source, landed, used, count in loads:
                            wait(sp, used, count)
                            apart(sp, S)
                            sp.dma_start(dst[:], source(expert)).then_inc(landed, 16)
                    with sp.Else():
                        for _, _, landed, _, _ in loads:
                            sp.sem_inc(landed, 16)

                def fetch_gu(i, q, s):
                    fetch(i, [(w_gu[c], lambda e, c=c: A["w_gu_t"][bass.ds(e * GU_ROWS + c * P, P), :], gu_in[c],
                               gu_lo, GU * (i - 1) + PART * (c + 1)) for c in range(GL)])

                def fetch_dn(i, q, s):
                    fetch(i, [(w_dn[c], lambda e, c=c: A["w_down_t"][bass.ds(e * DN_ROWS + c * P, P), :], dn_in[c],
                               dn_lo, DN * (i - 1) + PART * (c + 1)) for c in range(DL)])

                def fetch_bias_gu(i, q, s):
                    fetch(i, [(b_gu, lambda e: A["b_gu"][bass.ds(e, 1), :].to_broadcast([P, F2]), bgu_in, u_added, i)])

                def fetch_bias_dn(i, q, s):
                    fetch(i, [(b_dn, lambda e: A["b_down"][bass.ds(e, 1), :].to_broadcast([P, D]), bdn_in, out_ready, i)])

                def step(at):
                    at(1, fetch_gu)
                    at(2, fetch_dn)
                    at(1, fetch_bias_gu)
                    at(3, fetch_bias_dn)
                less_2 = tiles(sp, step)
                for landed, past in ((gu_in, 48), (dn_in, 32), ([bgu_in], 48), ([bdn_in], 16)):
                    for part in landed:
                        sp.wait_ge(part, 32 * less_2 + past)
                        apart(sp, S)


def combine(nc, A, S, sem, sems, out):
    with ExitStack() as ctx:
        sb, _ = stack(ctx, nc, "fin")

        SLOT = 4

        def ring(name, shape, dt=F32):
            return [sb(f"{name}{i}", shape, dt) for i in range(SLOT)]
        rows = [ring(f"rows{k}_", [P, D]) for k in range(TOPK)]
        idx = ring("idx", [P, TOPK], I32)
        x1, acc, yo = ring("x1", [P, D]), ring("acc", [P, D]), ring("y", [P, D])
        st, mv, sd, rs = ring("st", [P, 2, 6]), ring("mv", [P, 2]), ring("sd", [P, 1]), ring("rs", [P, 1])
        lg, lb, g2 = sb("ln_g", [P, D]), sb("ln_b", [P, D]), sb("g2", [P, D])
        par_in, picked, first, link, stats, root, inverse, normed, scaled, ready = (sem(f"fin_{n}") for n in (
            "params", "picked", "first", "link", "stats", "root", "inverse", "normed", "scaled", "ready"))
        rows_in, x1_in, stored = sems("fin_rows", SLOT), sems("fin_x1", SLOT), sems("fin_stored", SLOT)
        STEPS = TOPK + 2

        with nc.Block() as block:
            @block.gpsimd
            def _(pool):
                def gather(q, s):
                    t = SLOT * q + s
                    wait(pool, stats, t - SLOT + 1)
                    apart(pool, S)
                    pool.tensor_copy(idx[s][:], S.pos[:, bass.ds(t * TOPK, TOPK)]).then_inc(picked, 1)
                    pool.wait_ge(picked, t + 1)
                    for k in range(TOPK):
                        apart(pool, S)
                        pool.indirect_dma_start(rows[k][s][:], None, S.slot_out_d,
                                                bass.IndirectOffsetOnAxis(ap=idx[s][:, k:k + 1], axis=0)).then_inc(rows_in[s], 16)

                def affine(q, s):
                    t = SLOT * q + s
                    if isinstance(q, int) and t == 0:
                        pool.wait_ge(par_in, 48)
                    pool.wait_ge(normed, t + 1)
                    wait(pool, stored[s], 16 * q)
                    pool.tensor_tensor(yo[s][:], acc[s][:], lg[:], ALU.mult).then_inc(scaled, 1)
                    pool.wait_ge(scaled, t + 1)
                    pool.tensor_tensor(yo[s][:], yo[s][:], lb[:], ALU.add).then_inc(ready, 1)
                pipeline(pool, TT, SLOT, [(0, gather), (3, affine)])

            @block.sync
            def _(sp):
                def load(q, s):
                    t = SLOT * q + s
                    wait(sp, stats, t - SLOT + 1)
                    apart(sp, S)
                    sp.dma_start(x1[s][:], S.x1_d[bass.ds(t * P, P), :]).then_inc(x1_in[s], 16)

                def store(q, s):
                    t = SLOT * q + s
                    sp.wait_ge(ready, t + 1)
                    apart(sp, S)
                    sp.dma_start(out[bass.ds(t * P, P), :], yo[s][:]).then_inc(stored[s], 16)
                sp.dma_start(g2[:], S.ada_d[0, ADA_G2 * D:(ADA_G2 + 1) * D].partition_broadcast(P)).then_inc(par_in, 16)
                for dst, name in ((lg, "ln2_g"), (lb, "ln2_b")):
                    sp.dma_start(dst[:], A[name][0].partition_broadcast(P)).then_inc(par_in, 16)
                pipeline(sp, TT, SLOT, [(0, load), (3, store)])
                for s in range(SLOT):
                    sp.wait_ge(stored[s], 16 * TT // SLOT)

            @block.scalar
            def _(act):
                def first_row(q, s):
                    t = SLOT * q + s
                    act.wait_ge(rows_in[s], 16 * TOPK * (q + 1))
                    wait(act, scaled, t - SLOT + 1)
                    act.activation(acc[s][:], rows[0][s][:], ACT.Copy, scale=S.probs[:, bass.ds(t * TOPK, 1)]).then_inc(first, 1)

                def take_root(q, s):
                    act.wait_ge(stats, SLOT * q + s + 1)
                    act.activation(sd[s][:], mv[s][:, 1:2], ACT.Sqrt, bias=S.eps[:]).then_inc(root, 1)
                pipeline(act, TT, SLOT, [(0, first_row), (1, take_root)])

            @block.vector
            def _(dve):
                chain = Chain(dve, link)
                dve.wait_ge(par_in, 48)

                def blend(q, s):
                    t = SLOT * q + s
                    chain.item(t, STEPS)
                    dve.wait_ge(first, t + 1)
                    for k in range(1, TOPK):
                        chain.step(dve.scalar_tensor_tensor(out=acc[s][:], in0=rows[k][s][:], scalar=S.probs[:, bass.ds(t * TOPK + k, 1)],
                                                            in1=acc[s][:], op0=ALU.mult, op1=ALU.add))
                    chain.step(dve.tensor_tensor(acc[s][:], acc[s][:], g2[:], ALU.mult))
                    dve.wait_ge(x1_in[s], 16 * (q + 1))
                    chain.step(dve.scalar_tensor_tensor(out=acc[s][:], in0=x1[s][:], scalar=DN_ALPHA, in1=acc[s][:], op0=ALU.mult, op1=ALU.add))
                    dve.bn_stats(st[s][:, 0, :], acc[s][:, 0:BANK])
                    chain.step(dve.bn_stats(st[s][:, 1, :], acc[s][:, BANK:D]))
                    apart(dve, S)
                    dve.bn_aggr(mv[s][:], st[s][:]).then_inc(stats, 1)
                    chain.end()

                def normalise(q, s):
                    t = SLOT * q + s
                    dve.wait_ge(root, t + 1)
                    dve.reciprocal(rs[s][:], sd[s][:]).then_inc(inverse, 1)
                    dve.wait_ge(inverse, t + 1)
                    dve.tensor_scalar(acc[s][:], acc[s][:], mv[s][:, 0:1], rs[s][:], ALU.subtract, ALU.mult).then_inc(normed, 1)
                pipeline(dve, TT, SLOT, [(0, blend), (1, normalise)])


def build(nc, A, out):
    with ExitStack() as top:
        in_use = []

        def sem(name):
            in_use.append(nc.alloc_semaphore(name=name))
            return in_use[-1]

        def release_semaphores():
            nc.clear_and_free_semaphores(in_use)
            in_use.clear()
            nc.all_engine_barrier()

        def sems(name, n):
            return [sem(f"{name}{i}") for i in range(n)]

        def dram(name, shape, dt=F32):
            return nc.dram_tensor(name, shape, dt).ap()

        S = Shared()
        S.passed = nc.alloc_semaphore(name="passed")
        S.ada_d = dram("ada_scratch", (1, 4 * D))
        S.rows_d = dram("rows_scratch", (N_ROWS * P, SEQ))
        S.acum_d = dram("acum_scratch", (HEADS, SEQ))
        S.y_d = dram("y_scratch", (INNER, SEQ))
        S.mixin_d = dram("mixin_scratch", (D, SEQ))
        S.x1_d = dram("x1_scratch", (SEQ, D))
        S.h2_d = dram("h2_scratch", (SEQ, D))
        S.slot_token_d = dram("slot_token_scratch", (SLOTS, 1), I32)
        S.slot_out_d = dram("slot_out_scratch", (MOE_TILES * P, D))

        sb, _ = stack(top, nc, "keep")
        S.ident = sb("ident", [P, P])
        S.tri = sb("tri", [P, P])
        S.ones = sb("ones", [P, P])
        S.eps = sb("eps", [P, 1])
        S.probs = sb("probs", [P, TT * TOPK])
        S.pos = sb("pos", [P, TT * TOPK], I32)
        S.slot_token = sb("slot_token", [P, MOE_COLS], I32)
        S.expert = sb("expert", [P, MOE_COLS], I32)
        S.fresh = sb("fresh", [P, MOE_COLS], I32)
        S.rounds = sb("rounds", [P, 1], I32)

        mid = top.enter_context(ExitStack())
        sb, _ = stack(mid, nc, "keep_mid")
        S.modT = sb("modT", [P, 2 * KD])
        S.silu_c = sb("silu_c", [P, KD])
        S.logits = sb("logits", [P, TT * EXPERTS])

        modulation(nc, A, S, sem, sems)
        with ExitStack() as ctx:
            sb, _ = stack(ctx, nc, "table")
            S.dt = sb("dt", [P, TT * HEADS])
            S.acum = sb("acum", [P, TT * HEADS])
            S.decay = sb("decay", [P, TT * HEADS])
            S.chunk_decay = sb("chunk_decay", [P, TT * HEADS])
            with ExitStack() as hctx:
                sb, _ = stack(hctx, nc, "h")
                h_hi = sb("hi", [P, KD, SEQ], F32R)
                h_lo = sb("lo", [P, KD, SEQ], F32R)
                norm_in(nc, A, S, sem, sems, h_hi, h_lo)
                decay(nc, A, S, sem, sems, h_hi, h_lo)
                project(nc, A, S, sem, sems, h_hi, h_lo)
            ssd(nc, A, S, sem, sems)
        release_semaphores()
        branches(nc, A, S, sem, sems)
        mix_out(nc, A, S, sem, sems)
        route(nc, A, S, sem, sems)
        mid.close()
        experts(nc, A, S, sem, sems)
        combine(nc, A, S, sem, sems, out)
        in_use.append(S.passed)
        release_semaphores()


def layouts(i):
    import numpy as np
    z1 = INNER
    s1 = z1 + N_XBC * P
    s2 = s1 + HEADS
    w_in = i["w_in"][0]
    cols = [w_in[:, 0:s1]]
    short = w_in[:, s2:s2 + 3 * D].reshape(D, 3, N_SC, P)[:, [1, 2, 0]]
    cols.append(short.transpose(0, 2, 1, 3).reshape(D, 3 * D))
    cols.append(w_in[:, s2 + 3 * D:])
    w_main = np.concatenate(cols, axis=1)

    def col_tiles(w, width=P):
        rows, n = w.shape
        return w.reshape(rows // P, P, n // width, width).transpose(2, 1, 0, 3).reshape(n // width * P, rows // P * width)

    def expert_rows(w, rows):
        e, k, n = w.shape
        return w.reshape(e, rows // P, k // rows, P, n).transpose(0, 1, 3, 2, 4).reshape(e * rows, k // rows * n)

    def columns(v):
        return v.reshape(-1, P).T
    return {
        "x": i["x"][0],
        "cT": columns(i["c"][0]),
        "w_ada_t": col_tiles(i["w_ada"][0], BANK).reshape(6 * D // BANK, P, KD * BANK),
        "b_ada": i["b_ada"],
        "w_in_t": col_tiles(w_main),
        "w_dt": col_tiles(w_in[:, s1:s2], HEADS),
        "conv_w": i["conv_ssd_w"][0].reshape(CONV, N_XBC, P).transpose(2, 1, 0).reshape(P, N_XBC * CONV),
        "conv_b": columns(i["conv_ssd_b"][0]),
        "short_w": i["conv_short_w"][0].reshape(SCONV, N_SC, P).transpose(2, 1, 0).reshape(P, N_SC * SCONV),
        "b_gateT": columns(i["b_gate"][0]),
        "dt_bias": i["dt_bias"],
        "a_log": i["a_log"],
        "d_skipT": columns(np.repeat(i["d_skip"][0], HD)),
        "ssd_norm_wT": columns(i["ssd_norm_w"][0]),
        "w_branch_t": col_tiles(np.concatenate([i["w_ssd_out"][0], i["w_short_out"][0]], axis=0)),
        "w_o": i["w_o"][0],
        "ln1_g": i["ln1_g"], "ln1_b": i["ln1_b"],
        "w_router_t": col_tiles(i["w_router"][0], EXPERTS),
        "b_router": i["b_router"],
        "w_gu_t": expert_rows(i["w_gu"][0], GU_ROWS),
        "b_gu": i["b_gu"][0],
        "w_down_t": expert_rows(i["w_down"][0], DN_ROWS),
        "b_down": i["b_down"][0],
        "ln2_g": i["ln2_g"], "ln2_b": i["ln2_b"],
    }


def kernel(**inputs):
    import numpy as np
    from concourse import bacc
    from concourse.bass_utils import run_bass_kernel_spmd

    nc = bacc.Bacc("TRN2", target_bir_lowering=False, num_devices=1)
    arrays, A = {}, {}
    for name, a in layouts({k: np.asarray(v) for k, v in inputs.items()}).items():
        a = np.ascontiguousarray(a)
        arrays[f"in_{name}"] = a
        A[name] = nc.dram_tensor(f"in_{name}", a.shape, mybir.dt.from_np(a.dtype), kind="ExternalInput").ap()
    out = nc.dram_tensor("out_x", (SEQ, D), F32, kind="ExternalOutput").ap()
    build(nc, A, out)
    r = run_bass_kernel_spmd(nc, [arrays], core_ids=[0])
    return r.results[0]["out_x"].reshape(1, SEQ, D)
```
